# Optimizing a Trainium2 kernel written in Bass

```python
import math
import jax, jax.numpy as jnp
from jax import lax
import numpy as np

D_MODEL = 1024
BATCH = 1
SEQ = 128
DEPTH = 1
DEC_BATCH = 1
DEC_SEQ = 512
PAST_LEN = 256

GRID_W = 64
RET_HEADS = 4
RET_KD = D_MODEL // 8
RET_VD = D_MODEL // 4
RET_CHUNK = 128
DIFF_HEADS = 8
DIFF_HD = D_MODEL // 16
Q_BLOCK = 128
ROPE_BASE = 10000.0
N_GROUPS = 4
EXPERTS_PER_GROUP = 8
N_EXPERTS = N_GROUPS * EXPERTS_PER_GROUP
EXPERT_TOP_K = 2
EXPERT_FF = D_MODEL // 4
NORM_EPS = 1e-6

RET_QK_W = RET_HEADS * RET_KD
RET_V_W = RET_HEADS * RET_VD
DIFF_QK_W = DIFF_HEADS * 2 * DIFF_HD
DIFF_V_W = DIFF_HEADS * 2 * DIFF_HD
IN_WIDTHS = (RET_QK_W, RET_QK_W, RET_V_W, RET_V_W, DIFF_QK_W, DIFF_QK_W, DIFF_V_W, D_MODEL, D_MODEL)
IN_SPLITS = tuple(sum(IN_WIDTHS[:i + 1]) for i in range(len(IN_WIDTHS) - 1))
IN_W = sum(IN_WIDTHS)

kernel_name = 'hybrid_retention_diffattn_hmoe_diffusion_step'

F32 = jnp.float32

def rmsnorm(x, g):
    xf = x.astype(F32)
    y = xf * lax.rsqrt(jnp.mean(xf * xf, axis=-1, keepdims=True) + NORM_EPS)
    return (y * g.astype(F32)).astype(x.dtype)

def head_groupnorm(o, g):
    B, T = o.shape[0], o.shape[1]
    mu = jnp.mean(o, axis=-1, keepdims=True)
    d = o - mu
    y = d * lax.rsqrt(jnp.mean(d * d, axis=-1, keepdims=True) + NORM_EPS)
    return y.reshape(B, T, -1) * g.astype(F32)

def axial_rope(x):
    T, dh = x.shape[1], x.shape[-1]
    n_rows = T // GRID_W
    row = jnp.repeat(jnp.arange(n_rows), GRID_W).astype(F32)
    col = jnp.tile(jnp.arange(GRID_W), n_rows).astype(F32)
    axis_dim = dh // 2
    n_freq = axis_dim // 2
    inv = ROPE_BASE ** (-jnp.arange(n_freq, dtype=F32) / n_freq)

    def rot(part, pos):
        ang = pos[:, None] * inv[None, :]
        cos = jnp.cos(ang)[None, :, None, None, :]
        sin = jnp.sin(ang)[None, :, None, None, :]
        p1, p2 = part[..., :n_freq], part[..., n_freq:]
        return jnp.concatenate([p1 * cos - p2 * sin, p1 * sin + p2 * cos], axis=-1)

    xf = x.astype(F32)
    out = jnp.concatenate([rot(xf[..., :axis_dim], row), rot(xf[..., axis_dim:], col)], axis=-1)
    return out.astype(x.dtype)

def retention_chunkwise(q, k, v, log_gamma, s0):
    B, T, H, _ = q.shape
    dv = v.shape[-1]
    n = T // RET_CHUNK
    lg = log_gamma.astype(F32)
    pos = jnp.arange(RET_CHUNK, dtype=F32)
    rel = pos[:, None] - pos[None, :]
    intra = jnp.where(rel >= 0, jnp.exp(lg[:, None, None] * jnp.maximum(rel, 0.0)), 0.0)
    q_dec = jnp.exp(lg[:, None] * (pos + 1.0))[None]
    k_dec = jnp.exp(lg[:, None] * (RET_CHUNK - 1.0 - pos))[None]
    c_dec = jnp.exp(lg * RET_CHUNK)[None, :, None, None]

    def to_chunks(a):
        return a.astype(F32).reshape(B, n, RET_CHUNK, H, a.shape[-1]).swapaxes(0, 1)

    def step(s, qkv):
        qc, kc, vc = qkv
        scores = jnp.einsum('bihd,bjhd->bhij', qc, kc) * intra
        o = (jnp.einsum('bhij,bjhe->bihe', scores, vc)
             + jnp.einsum('bihd,bhi,bhde->bihe', qc, jnp.broadcast_to(q_dec, (B, H, RET_CHUNK)), s))
        s = c_dec * s + jnp.einsum('bjhd,bhj,bjhe->bhde', kc, jnp.broadcast_to(k_dec, (B, H, RET_CHUNK)), vc)
        return s, o

    s_final, o = lax.scan(step, s0.astype(F32), (to_chunks(q), to_chunks(k), to_chunks(v)))
    return o.swapaxes(0, 1).reshape(B, T, H, dv), s_final

def diff_attention(q, k, v, lam):
    B, Tq, H, _, dh = q.shape
    nb = Tq // Q_BLOCK
    qb = q.reshape(B, nb, Q_BLOCK, H, 2, dh).swapaxes(0, 1)
    vf = v.astype(F32)
    scale = dh ** -0.5

    def block(qblk):
        s = jnp.einsum('bqhcd,bkhcd->bchqk', qblk, k).astype(F32) * scale
        p = jax.nn.softmax(s, axis=-1)
        a = p[:, 0] - lam * p[:, 1]
        return jnp.einsum('bhqk,bkhe->bqhe', a, vf)

    o = lax.map(block, qb)
    return o.swapaxes(0, 1).reshape(B, Tq, H, v.shape[-1])

def mixer(h, ctx, lam, lam_init, w_in, lg_f, lg_b, ret_norm_g, subln_g, w_ret_o, w_diff_o, w_o):
    B, T, _ = h.shape
    rq, rk, rv, rg, dq, dk, dv, gr, gd = jnp.split(h @ w_in, IN_SPLITS, axis=-1)
    rq = rq.reshape(B, T, RET_HEADS, RET_KD)
    rk = rk.reshape(B, T, RET_HEADS, RET_KD) * (RET_KD ** -0.5)
    rv = rv.reshape(B, T, RET_HEADS, RET_VD)
    dq = dq.reshape(B, T, DIFF_HEADS, 2, DIFF_HD)
    dk = dk.reshape(B, T, DIFF_HEADS, 2, DIFF_HD)
    dv = dv.reshape(B, T, DIFF_HEADS, 2 * DIFF_HD)
    if ctx is None:
        s0_f = jnp.zeros((B, RET_HEADS, RET_KD, RET_VD), F32)
        s0_b = s0_f
        q_att, k_att, v_att = dq, dk, dv
    else:
        ctx_k, ctx_v, s0_f, s0_b = ctx
        q_att = axial_rope(dq)
        k_att = jnp.concatenate([axial_rope(dk), ctx_k.astype(dk.dtype)], axis=1)
        v_att = jnp.concatenate([dv, ctx_v.astype(dv.dtype)], axis=1)
    o_f, s_f = retention_chunkwise(rq, rk, rv, lg_f, s0_f)
    o_b, s_b = retention_chunkwise(rq[:, ::-1], rk[:, ::-1], rv[:, ::-1], lg_b, s0_b)
    o_r = head_groupnorm(o_f + o_b[:, ::-1], ret_norm_g)
    ret_out = (jax.nn.silu(rg.astype(F32)) * o_r).astype(h.dtype) @ w_ret_o
    o_d = diff_attention(q_att, k_att, v_att, lam)
    o_d = (o_d * lax.rsqrt(jnp.mean(o_d * o_d, axis=-1, keepdims=True) + NORM_EPS)
           * subln_g.astype(F32) * (1.0 - lam_init))
    diff_out = o_d.reshape(B, T, DIFF_V_W).astype(h.dtype) @ w_diff_o
    merged = jax.nn.sigmoid(gr) * ret_out + jax.nn.sigmoid(gd) * diff_out
    return merged @ w_o, dk, dv, s_f, s_b

def hier_moe(h, rgw, rgb, rew, reb, wg, wu, wd):
    B, T, D = h.shape
    hf = h.reshape(B * T, D)
    p_grp = jax.nn.softmax((hf @ rgw + rgb).astype(F32), axis=-1)
    p_top, g_idx = lax.top_k(p_grp, 1)
    e_logits = (hf @ rew + reb).astype(F32).reshape(-1, N_GROUPS, EXPERTS_PER_GROUP)
    e_logits = jnp.take_along_axis(e_logits, g_idx[:, :, None], axis=1)[:, 0]
    e_top, e_idx = lax.top_k(jax.nn.softmax(e_logits, axis=-1), EXPERT_TOP_K)
    w = p_top * e_top / jnp.sum(e_top, axis=-1, keepdims=True)
    gidx = g_idx * EXPERTS_PER_GROUP + e_idx
    combine = jnp.einsum('nk,nke->ne', w, jax.nn.one_hot(gidx, N_EXPERTS, dtype=F32))
    a = jax.nn.silu(jnp.einsum('nd,edf->nef', hf, wg)) * jnp.einsum('nd,edf->nef', hf, wu)
    y = jnp.einsum('nef,efd->nd', a * combine[:, :, None].astype(a.dtype), wd)
    return y.reshape(B, T, D)

def trunk_layer(x, mod, ctx, lam, lam_init, n1, n2, w_in, lg_f, lg_b, ret_norm_g, subln_g,
                w_ret_o, w_diff_o, w_o, rgw, rgb, rew, reb, wg, wu, wd):
    sh1, sc1, g1, sh2, sc2, g2 = jnp.split(mod, 6, axis=-1)
    h = rmsnorm(x, n1) * (1.0 + sc1) + sh1
    mix, k_c, v_c, s_f, s_b = mixer(h, ctx, lam, lam_init, w_in, lg_f, lg_b, ret_norm_g, subln_g,
                                    w_ret_o, w_diff_o, w_o)
    x = x + g1 * mix
    h2 = rmsnorm(x, n2) * (1.0 + sc2) + sh2
    x = x + g2 * hier_moe(h2, rgw, rgb, rew, reb, wg, wu, wd)
    return x, k_c, v_c, s_f, s_b

def setup_inputs(seed: int = 0) -> dict:
    key = jax.random.key(seed)
    ks = jax.random.split(key, 32)

    def nrm(k, shape, s):
        return jax.random.normal(k, shape, F32) * s

    base_logit = jnp.log(2.0 ** (5.0 + jnp.arange(RET_HEADS, dtype=F32)) - 1.0)
    return {
        'x_prompt': nrm(ks[0], (BATCH, SEQ, D_MODEL), 1.0),
        'x_sample': nrm(ks[1], (DEC_BATCH, DEC_SEQ, D_MODEL), 1.0),
        'cache_diff_k': nrm(ks[2], (DEC_BATCH, DEPTH, PAST_LEN, DIFF_HEADS, 2, DIFF_HD), 1.0),
        'cache_diff_v': nrm(ks[3], (DEC_BATCH, DEPTH, PAST_LEN, DIFF_HEADS, 2 * DIFF_HD), 1.0),
        'state_ret_fwd': nrm(ks[4], (DEC_BATCH, DEPTH, RET_HEADS, RET_KD, RET_VD), 0.5),
        'state_ret_bwd': nrm(ks[5], (DEC_BATCH, DEPTH, RET_HEADS, RET_KD, RET_VD), 0.5),
        'c': nrm(ks[6], (DEC_BATCH, D_MODEL), 1.0),
        'c_ctx': nrm(ks[7], (D_MODEL,), 1.0),
        'w_ada': nrm(ks[8], (DEPTH, D_MODEL, 6 * D_MODEL), 0.5 * D_MODEL ** -0.5),
        'b_ada': nrm(ks[9], (DEPTH, 6 * D_MODEL), 0.01),
        'norm1_g': 1.0 + nrm(ks[10], (DEPTH, D_MODEL), 0.01),
        'norm2_g': 1.0 + nrm(ks[11], (DEPTH, D_MODEL), 0.01),
        'w_in': nrm(ks[12], (DEPTH, D_MODEL, IN_W), D_MODEL ** -0.5),
        'ret_decay_fwd': base_logit[None] + nrm(ks[13], (DEPTH, RET_HEADS), 0.1),
        'ret_decay_bwd': base_logit[None] + nrm(ks[14], (DEPTH, RET_HEADS), 0.1),
        'ret_norm_g': 1.0 + nrm(ks[15], (DEPTH, RET_V_W), 0.01),
        'diff_lambda_q1': nrm(ks[16], (DEPTH, DIFF_HD), 0.1),
        'diff_lambda_k1': nrm(ks[17], (DEPTH, DIFF_HD), 0.1),
        'diff_lambda_q2': nrm(ks[18], (DEPTH, DIFF_HD), 0.1),
        'diff_lambda_k2': nrm(ks[19], (DEPTH, DIFF_HD), 0.1),
        'diff_subln_g': 1.0 + nrm(ks[20], (DEPTH, 2 * DIFF_HD), 0.01),
        'w_ret_o': nrm(ks[21], (DEPTH, RET_V_W, D_MODEL), RET_V_W ** -0.5),
        'w_diff_o': nrm(ks[22], (DEPTH, DIFF_V_W, D_MODEL), DIFF_V_W ** -0.5),
        'w_o': nrm(ks[23], (DEPTH, D_MODEL, D_MODEL), D_MODEL ** -0.5),
        'router_group_w': nrm(ks[24], (DEPTH, D_MODEL, N_GROUPS), D_MODEL ** -0.5),
        'router_group_b': nrm(ks[25], (DEPTH, N_GROUPS), 0.01),
        'router_expert_w': nrm(ks[26], (DEPTH, D_MODEL, N_EXPERTS), D_MODEL ** -0.5),
        'router_expert_b': nrm(ks[27], (DEPTH, N_EXPERTS), 0.01),
        'moe_w_gate': nrm(ks[28], (DEPTH, N_EXPERTS, D_MODEL, EXPERT_FF), D_MODEL ** -0.5),
        'moe_w_up': nrm(ks[29], (DEPTH, N_EXPERTS, D_MODEL, EXPERT_FF), D_MODEL ** -0.5),
        'moe_w_down': nrm(ks[30], (DEPTH, N_EXPERTS, EXPERT_FF, D_MODEL), EXPERT_FF ** -0.5),
        'final_norm_g': 1.0 + nrm(ks[31], (D_MODEL,), 0.01),
    }

def reference(x_prompt, x_sample, cache_diff_k, cache_diff_v, state_ret_fwd, state_ret_bwd, c, c_ctx,
              w_ada, b_ada, norm1_g, norm2_g, w_in, ret_decay_fwd, ret_decay_bwd, ret_norm_g,
              diff_lambda_q1, diff_lambda_k1, diff_lambda_q2, diff_lambda_k2, diff_subln_g,
              w_ret_o, w_diff_o, w_o, router_group_w, router_group_b, router_expert_w, router_expert_b,
              moe_w_gate, moe_w_up, moe_w_down, final_norm_g):
    xp, xs = x_prompt, x_sample
    silu_ctx = jax.nn.silu(c_ctx)
    silu_c = jax.nn.silu(c)
    ks_l, vs_l, sf_l, sb_l = [], [], [], []
    for l in range(DEPTH):
        lam_init = 0.8 - 0.6 * math.exp(-0.3 * l)
        lam = (jnp.exp(jnp.sum(diff_lambda_q1[l].astype(F32) * diff_lambda_k1[l].astype(F32)))
               - jnp.exp(jnp.sum(diff_lambda_q2[l].astype(F32) * diff_lambda_k2[l].astype(F32))) + lam_init)
        lg_f = jax.nn.log_sigmoid(ret_decay_fwd[l].astype(F32))
        lg_b = jax.nn.log_sigmoid(ret_decay_bwd[l].astype(F32))
        shared = (lam, lam_init, norm1_g[l], norm2_g[l], w_in[l], lg_f, lg_b, ret_norm_g[l], diff_subln_g[l],
                  w_ret_o[l], w_diff_o[l], w_o[l], router_group_w[l], router_group_b[l],
                  router_expert_w[l], router_expert_b[l], moe_w_gate[l], moe_w_up[l], moe_w_down[l])
        mod_p = silu_ctx @ w_ada[l] + b_ada[l]
        mod_s = (silu_c @ w_ada[l] + b_ada[l])[:, None, :]
        xp, k_c, v_c, s_f, s_b = trunk_layer(xp, mod_p, None, *shared)
        ks_l.append(k_c)
        vs_l.append(v_c)
        sf_l.append(s_f.astype(xp.dtype))
        sb_l.append(s_b.astype(xp.dtype))
        ctx = (cache_diff_k[:, l], cache_diff_v[:, l], state_ret_fwd[:, l], state_ret_bwd[:, l])
        xs, _, _, _, _ = trunk_layer(xs, mod_s, ctx, *shared)
    y_prompt = rmsnorm(xp, final_norm_g)
    y_sample = rmsnorm(xs, final_norm_g)
    new_diff_k = jnp.stack(ks_l, axis=1)
    new_diff_v = jnp.stack(vs_l, axis=1)
    new_ret_fwd = jnp.stack(sf_l, axis=1)
    new_ret_bwd = jnp.stack(sb_l, axis=1)
    return (y_prompt, y_sample, new_diff_k, new_diff_v, new_ret_fwd, new_ret_bwd)


_drawn_inputs = setup_inputs


def setup_inputs(seed=0):
    import zlib

    import numpy as np

    out = dict(_drawn_inputs(seed))
    spreads = {}
    factors = {'state_ret_fwd': 3.983,
     'state_ret_bwd': 4.076,
     'norm1_g': 4.864,
     'norm2_g': 6.699,
     'ret_norm_g': 8.0,
     'diff_lambda_q1': 3.787,
     'diff_lambda_q2': 4.562,
     'diff_lambda_k2': 3.753,
     'diff_subln_g': 8.0,
     'router_group_b': 8.0,
     'router_expert_b': 8.0,
     'final_norm_g': 5.79}
    for name, (base, spread) in spreads.items():
        noise = np.random.default_rng([zlib.crc32(name.encode()), seed]).standard_normal(out[name].shape)
        drawn = base * np.exp(spread * noise) if base else spread * noise
        out[name] = __import__('jax').numpy.asarray(drawn.astype(out[name].dtype))
    for name, factor in factors.items():
        out[name] = (out[name] * factor).astype(out[name].dtype)
    return out
```

```python
from contextlib import ExitStack

import numpy as np

import concourse.bass as bass
from concourse import mybir

F32 = mybir.dt.float32
F32R = mybir.dt.float32r
I32 = mybir.dt.int32
U32 = mybir.dt.uint32
ALU = mybir.AluOpType
ACT = mybir.ActivationFunctionType
AXX = mybir.AxisListType.X

P = 128
D = 1024
KC = D // P
NT = 5
PT = NT - 1
N512 = 512
N256 = 256
RH, RK, RV = 4, 128, 256
AH, DH = 8, 64
CTX = 256
KEYS = 512 + CTX
GRP, EPG, NE, FF = 4, 8, 32, 256
BLK = 64
PAIRS = NE // 2
OVER = 20
SLOTS = (NE + OVER) * BLK
NPAIR = (NE + OVER) // 2
EPS = 1e-6
BIG = 1e30


def host_constants():
    i = np.arange(P, dtype=np.float32)
    rel = i[None, :] - i[:, None]
    s = np.float32(RK ** -0.5)
    parts = {}
    parts["ident"] = np.eye(P, dtype=np.float32)
    parts["rel_f"] = np.maximum(rel, 0)
    parts["rel_b"] = np.maximum(-rel, 0)
    parts["on_f"] = (rel >= 0) * s
    parts["on_b"] = (rel <= 0) * s
    parts["pos_f"] = np.broadcast_to(i + 1, (P, P))
    parts["pos_b"] = np.broadcast_to(P - i, (P, P))
    parts["kpos"] = np.stack([P - 1 - i, i], 1)
    tok = np.arange(512)
    inv = (np.float32(10000.0) ** (-np.arange(16, dtype=np.float32) / np.float32(16))).astype(np.float32)
    ang = np.stack([(tok // 64).astype(np.float32)[:, None] * inv, (tok % 64).astype(np.float32)[:, None] * inv], 1)
    ang = ang.reshape(4, P, 32).transpose(1, 0, 2).reshape(P, 128).astype(np.float32)
    parts["cos"] = np.cos(ang)
    parts["sin"] = np.sin(ang)
    parts = {k: parts[k] for k in ("rel_f", "rel_b", "on_f", "on_b", "pos_f", "pos_b", "ident", "kpos", "cos", "sin")}
    main = np.concatenate([np.asarray(v, np.float32) for v in parts.values()], 1)
    at, off = 0, {}
    for k, v in parts.items():
        off[k] = (at, at + v.shape[1])
        at += v.shape[1]
    r = {}
    r["before"] = (i[:, None] < i[None, :]) * 1.0
    r["ones"] = np.ones((P, P))
    r["ramp128"] = np.broadcast_to(i, (P, P))
    r["ramp32"] = np.broadcast_to(np.arange(32), (P, 32))
    r["ramp26"] = np.broadcast_to(np.arange(NPAIR), (P, NPAIR))
    r["x64"] = np.broadcast_to(64 * np.arange(1, 10), (P, 9))
    r["x128"] = np.broadcast_to(128 * np.arange(1, NPAIR), (P, NPAIR - 1))
    e = np.arange(32)
    r["lower"] = np.broadcast_to((e[None, :] < e[:, None]).reshape(1, -1), (P, 1024))
    r["ramp20"] = np.broadcast_to(np.arange(OVER), (P, OVER))
    r["token"] = np.arange(NT)[None, :] * P + i[:, None]
    route = np.concatenate([np.asarray(v, np.float32) for v in r.values()], 1)
    at, roff = 0, {}
    for k, v in r.items():
        roff[k] = (at, at + v.shape[1])
        at += v.shape[1]
    return np.ascontiguousarray(main, np.float32), off, np.ascontiguousarray(route, np.float32), roff


def build(nc, a, o, coff, roff, nconst, nroute):
    ctx = ExitStack()
    with ctx:
        sem_names = {}

        def sem(name):
            s = ctx.enter_context(nc.semaphore(name))
            sem_names[name] = s
            return s

        def sb(name, shape, dt=F32):
            return ctx.enter_context(nc.sbuf_tensor(name, shape, dt))

        KB = 256
        arena_base = -(-nc.sbuf_base // 32) * 32
        arena = sb("arena", [P, 198 * KB])

        def at(kb, n, kb_end=None):
            v = arena[:, int(kb * KB):int(kb * KB) + n]
            return v

        def split_at(name, kb, k, n, dt=F32R):
            return nc.alloc_sbuf_tensor_at(name, [P, k, n], dt, offset=arena_base + kb * 1024)

        def tiles(kb, t, n):
            return at(kb, t * n).rearrange("p (t n) -> p t n", t=t)

        setup_n = coff["ident"][0]
        const, const0 = sb("const", [P, nconst - setup_n]), at(20, setup_n)

        def C(k):
            lo, hi = coff[k]
            return const0[:, lo:hi] if lo < setup_n else const[:, lo - setup_n:hi - setup_n]

        dq, dk, dv = tiles(0, NT, N512), tiles(10, NT, N512), tiles(20, NT, N512)
        rq, rk = tiles(30, NT, N512), tiles(40, NT, N512)
        ctx_k, ctx_v = tiles(30, 2, N512), tiles(34, 2, N512)
        gate_t, gate_p = tiles(38, 4, N256), tiles(42, 2, N256)
        rope_t = tiles(82, 4, 256)
        w_ring = [at(86 + 16 * i, KC * N512).rearrange("p (k n) -> p k n", k=KC) for i in range(2)]
        w_raw = [split_at(f"w_loaded{i}", 86 + 16 * i, KC, N256, F32)[:] for i in range(2)]
        w_lo = [split_at(f"w_low{i}", 86 + 16 * i, KC, N256) for i in range(2)]
        w_hi = [split_at(f"w_high{i}", 94 + 16 * i, KC, N256) for i in range(2)]
        hT = at(118, KC * NT * P).rearrange("p (k t) -> p k t", k=KC)
        h_full = split_at("h_whole", 158, KC, NT * P, F32)
        h_hi, h_lo = split_at("h_high", 118, KC, NT * P), split_at("h_low", 158, KC, NT * P)
        rv, oT, gd_t = tiles(138, NT, D), at(138, KC * NT * P).rearrange("p (k t) -> p k t", k=KC), tiles(138, NT, D)
        xn = tiles(0, NT, D)
        merge = tiles(158, NT, D)
        od = tiles(178, NT, D)
        states_b = tiles(178, 4, D)
        ret = tiles(178, NT, D)
        state_f, state_out = at(50, D), tiles(54, 2, D)
        rqT, rkT = at(62, N512), at(64, N512)
        qf, qb = at(66, N512), at(68, N512)
        sm, ks = at(70, N512), tiles(72, 2, N512)
        square_t = at(76, D)
        qz = [tiles(50 + 4 * i, 2, N512) for i in range(2)]
        kT = [at(58 + 3.5 * i, KEYS + P) for i in range(2)]
        qzp = [at(65 + i, 2 * P).rearrange("p (c n) -> p c n", c=2) for i in range(2)]
        probs = at(67, 2 * KEYS).rearrange("p (c n) -> p c n", c=2)
        mixed = at(73, KEYS)
        mixedT = [at(76 + 3 * i, KEYS) for i in range(2)]
        ada_ring = [at(178 + 8 * i, 4 * N512) for i in range(2)]
        bias_rows, mod_rows = tiles(50, 3, N512), tiles(56, 3, N512)
        rows = at(62, P)
        rows_t = at(62.5, P)
        ccol = at(63, KC * 32).rearrange("p (k m) -> p k m", k=KC)
        lam_in = at(64, 4 * DH).rearrange("p (v n) -> p v n", v=4)
        decay_e = at(65, 8 * P).rearrange("p (h n) -> p h n", h=8)
        odT = hT
        gr_t = tiles(118, NT, D)
        x1 = tiles(0, NT, D)
        g1_rows = tiles(20, 2, D)
        mT = at(178, KC * NT * P).rearrange("p (k t) -> p k t", k=KC)
        merge_t = tiles(76, 2, N512)
        h2T = at(142, KC * NT * P).rearrange("p (k t) -> p k t", k=KC)
        scale2, shift2 = tiles(162, 2, D), tiles(170, 2, D)
        h2, square2 = tiles(130, 2, D), at(138, D)
        route = at(118, nroute)
        R = lambda k: route[:, roff[k][0]:roff[k][1]]
        rw = at(124, KC * 36).rearrange("p (k n) -> p k n", k=KC)
        rb = at(125.5, 36)
        n2_row = at(126, D)
        w_gu = [at(k, KC * 2 * FF).rearrange("p (k g f) -> p k g f", k=KC, g=2) for k in (28, 52, 86, 162, 126, 142)]
        w_dn = [at(k, 2 * D).rearrange("p (k n) -> p k n", k=2) for k in (44, 68, 102, 20, 110, 76)]
        xg, xgT = tiles(178, 2, D), [at(186 + 4 * i, D).rearrange("p (k n) -> p k n", k=KC) for i in range(2)]
        y_out = tiles(118, 2, D)
        act_t, act_s = tiles(158, 2, FF), tiles(160, 2, FF)
        act_a, act_aT = tiles(194, 2, FF), [at(196 + i, 2 * P).rearrange("p (k n) -> p k n", k=2) for i in range(2)]
        g2_rows, fin_row = tiles(126, 2, D), at(134, D)
        fin_t = tiles(142, 2, D)
        y1, y2 = tiles(28, NT, D), tiles(48, NT, D)

        scr_at = [178]

        def scratch(n):
            v = at(scr_at[0], n)
            scr_at[0] += -(-n // 8) / 32
            return v

        logits = scratch(NT * 36).rearrange("p (t n) -> p t n", t=NT)
        g_max, g_idx, g_sum, p_top = [scratch(NT) for _ in range(4)]
        g_eq, g_hot, g_diff = [scratch(NT * GRP).rearrange("p (t n) -> p t n", t=NT) for _ in range(3)]
        e_m, e_eq = [scratch(NT * NE).rearrange("p (t n) -> p t n", t=NT) for _ in range(2)]
        hot = scratch(2 * NT * NE).rearrange("p (k t n) -> p k t n", k=2, t=NT)
        e_max, e_idx = scratch(2 * NT).rearrange("p (k t) -> p k t", k=2), scratch(2 * NT).rearrange("p (k t) -> p k t", k=2)
        e_x, e_den = scratch(NT), scratch(NT)
        e_any = scratch(NT * NE).rearrange("p (t n) -> p t n", t=NT)
        rank_m = scratch(NT * NE).rearrange("p (t n) -> p t n", t=NT)
        prod = scratch(2 * NT * NE).rearrange("p (k t n) -> p k t n", k=2, t=NT)
        cnt_a, cnt_b, over, over_at, over_end = [scratch(NE) for _ in range(5)]
        cmp9 = scratch(NE * 9).rearrange("p (e m) -> p e m", m=9)
        cmp_r = scratch(2 * NT * 9).rearrange("p (x m) -> p x m", m=9)
        rk_s, ob_s, qq, slot, pair_i, pos_i, has = [scratch(2 * NT) for _ in range(7)]
        cmp_p = scratch(2 * NT * (NPAIR - 1)).rearrange("p (x m) -> p x m", m=NPAIR - 1)
        hot_all = scratch(2 * NT * P)
        hot_pos = hot_all.rearrange("p (x n) -> p x n", n=P)
        low_p = hot_all[:, 0:NE * NE].rearrange("p (e f) -> p e f", e=NE)
        val_pair = scratch(2 * NT * NPAIR).rearrange("p (x n) -> p x n", n=NPAIR)
        ov_cmp = scratch(OVER * NE).rearrange("p (j e) -> p j e", j=OVER)
        ov_f, n_ov_f = scratch(OVER), scratch(1)
        assert scr_at[0] <= 198, scr_at[0]
        row_idx = sb("row_idx", [P, NPAIR], U32)
        idx_now = sb("idx_now", [P, 1], U32)
        y_idx = sb("y_idx", [P, 2 * NT], U32)
        w_tok = sb("w_tok", [P, 2, NT])
        ov_exp, n_ov = sb("ov_exp", [P, OVER], I32), sb("n_ov", [P, 1], I32)

        ssq, msq, rstd = sb("ssq", [P, NT]), sb("msq", [P, NT]), sb("rstd", [P, NT])
        neg_half = sb("neg_half", [P, 48])
        cols = sb("cols", [P, 25])
        modc = sb("modc", [P, 48, 2])
        mul1 = sb("mul1", [P, KC, 2])
        dec, dec_e, dec_n = sb("dec", [P, 8]), sb("dec_e", [P, 8]), sb("dec_n", [P, 8])
        lg = sb("lg", [P, 8])
        kd, cd = sb("kd", [P, 8]), sb("cd", [P, 8])
        lam_s, neg_lam = sb("lam_s", [P, 2]), sb("neg_lam", [P, 1])
        ret_mask = sb("ret_mask", [P, RH, P])
        q_dec = sb("q_dec", [P, 8, P])
        bn_s, bn_a = sb("bn_s", [P, RH, 6]), sb("bn_a", [P, RH, 2])
        var_e, ret_rstd = sb("var_e", [P, RH]), sb("ret_rstd", [P, RH])
        mx, neg_mx = sb("mx", [P, 2]), sb("neg_mx", [P, 2, 2])
        den, rden, coef = sb("den", [P, 2, 2]), sb("rden", [P, 2, 2]), sb("coef", [P, 2])
        od_ss, od_rstd = sb("od_ss", [P, NT, AH]), sb("od_rstd", [P, NT, AH])

        bank = [ctx.enter_context(nc.psum_tensor(f"bank{i}", [P, N512], F32)) for i in range(8)] if False else None
        ps = ctx.enter_context(nc.psum_tensor("ps", [P, 8, N512], F32))
        B = lambda i: ps[:, i, :]
        psf = ps[:].rearrange("p b n -> p (b n)")
        score = [psf[:, 2 * N512:2 * N512 + KEYS], psf[:, 2 * N512 + KEYS:2 * N512 + 2 * KEYS]]

        h2_dram = nc.dram_tensor("h2_rows", [NT * P, D], F32).ap()
        gates_dram = nc.dram_tensor("gates", [2, P, NT, D], F32).ap()
        y_dram = nc.dram_tensor("y_rows", [SLOTS, D], F32).ap()
        mod_dram = nc.dram_tensor("mod_rows_dram", [2, 6 * D], F32).ap()

        w_in = a["w_in"][0]
        off = dict(rq=0, rk=512, rv0=1024, rv1=1536, rg0=2048, rg1=2560, dq0=3072, dq1=3584, dk0=4096,
                   dk1=4608, dv0=5120, dv1=5632, gr0=6144, gr1=6656, gd0=7168, gd1=7680)
        SPLIT = ["rq", "rk", "rv0", "rv1", "dq0", "dk0", "dv0", "rg0", "rg1", "gr0", "gr1", "gd0", "gd1", "dq1", "dk1", "dv1"]
        WHOLE = ["wr0", "wr1", "wd0", "wd1", "wo0", "wo1"]
        UNITS = [(s, hh) for s in SPLIT for hh in range(2)] + [(s, None) for s in WHOLE]
        unit_at = {u: i for i, u in enumerate(UNITS)}
        N_SPLIT = 2 * len(SPLIT)

        def section_source(s, hh):
            if s in off:
                c = off[s] + N256 * hh
                return w_in[:, c:c + N256].rearrange("(k p) n -> p k n", p=P)
            else:
                m = {"wr": a["w_ret_o"], "wd": a["w_diff_o"], "wo": a["w_o"]}[s[:2]][0]
                c = 512 * int(s[2])
            return m[:, c:c + 512].rearrange("(k p) n -> p k n", p=P)

        plan = []
        dense = []

        def put_dense(*item):
            plan.append(("dense", len(dense)))
            dense.append(item)

        def emit(item):
            if item[0] == "cv":
                plan.append(item)
            else:
                put_dense(*item)

        def unit(s, hh):
            out = []
            i = unit_at[(s, hh)]
            for t in range(NT):
                out.append(("mm", s, t, hh))
                if t == 2 and i + 1 < N_SPLIT:
                    out.append(("cv", i + 1))
            return out

        def section(s):
            return unit(s, 0) + unit(s, 1) if s in off else unit(s, None)

        plan.append(("cv", 0))
        for t in range(2):
            for half in range(2):
                put_dense("T4", "h", t, half)
        ada_k = [(r, k) for r in (1, 2) for k in range(KC)]
        n = 0
        for item in [x for s in ("rq", "rk", "rv0", "rv1") for x in section(s)]:
            emit(item)
            if item[0] == "cv":
                continue
            if item[1] == "rq" and item[3] == 0 and item[2] + 2 < NT:
                for half in range(2):
                    put_dense("T4", "h", item[2] + 2, half)
            n += 1
            if n % 2 == 0 and ada_k:
                plan.append(("ada",) + ada_k.pop(0))
        UPDATES = [("b", 3), ("b", 2), ("b", 1), ("f", PT), ("b", PT), ("f", 0), ("f", 1), ("f", 2)]
        gaps = {0: [("U", 0, 0, 7), ("U", 0, 1, 4)],
                1: [("U", 1, 0, 7), ("U", 1, 1, 4), ("RT", PT)],
                2: [("U", 2, 0, 7), ("U", 2, 1, 4)],
                3: [("SC", PT), ("U", 3, 0, 7)],
                4: [("O", PT), ("RT", 0), ("U", 3, 1, 7), ("U", 4, 0, 4)],
                5: [("SC", 0), ("U", 4, 1, 7)],
                6: [("O", 0), ("RT", 1), ("U", 5, 0, 7), ("U", 5, 1, 4)],
                7: [("SC", 1)],
                8: [("O", 1), ("RT", 2), ("U", 6, 0, 7), ("U", 6, 1, 4)],
                9: [("SC", 2)],
                10: [("O", 2), ("RT", 3), ("U", 7, 0, 7), ("U", 7, 1, 4)],
                11: [("SC", 3)],
                12: [("O", 3)]}
        n = 0
        for item in [x for s in ("dq0", "dk0", "dv0") for x in section(s)]:
            emit(item)
            if item[0] != "cv":
                if n % 2:
                    plan.extend(gaps.get(n // 2, []))
                n += 1
        plan.append(("ret_end",))
        for s, hh, half in (("rg0", 0, None), ("rg0", 1, None), ("rg1", 0, 0), ("rg1", 1, 1)):
            for item in unit(s, hh):
                emit(item)
                if half is not None and item[0] == "mm" and item[2]:
                    put_dense("T4", "o", item[2] - 1, half)
            if half is not None:
                put_dense("T4", "o", PT, half)

        def prep(h, i):
            put_dense("T4", "prep", h, i)

        steps = [(h, t) for h in range(AH) for t in range(NT)]

        def attention(half, work):
            for i in range(3):
                prep(4 * half, i)
            mine = [s for s in range(len(steps)) if steps[s][0] // 4 == half]
            extra = {4 * half + h: [(4 * half + h + 1, i) for i in range(3)] for h in range(3)}
            share = [work[len(work) * j // len(mine):len(work) * (j + 1) // len(mine)] for j in range(len(mine))]
            for j, s in enumerate(mine):
                h, t = steps[s]
                plan.append(("S", s))
                if j:
                    plan.append(("AT", s - 1))
                for item in share[j]:
                    emit(item)
                if t in (1, 2, 3) and h in extra:
                    prep(*extra[h][t - 1])
                if j:
                    plan.append(("PV", s - 1))
            plan.append(("AT", mine[-1]))
            plan.append(("PV", mine[-1]))

        attention(0, [x for s in ("gr0", "gr1", "gd0", "gd1") for x in section(s)])
        for s in ["dq1", "dk1", "dv1"]:
            for item in section(s):
                emit(item)
        attention(1, [x for s in ("wr0", "wr1") for x in section(s)])
        plan.append(("att_end",))
        for s in ("wd0", "wd1"):
            for t in range(NT):
                if s == "wd0":
                    put_dense("T4", "od", t, 0)
                    put_dense("T4", "od", t, 1)
                put_dense("mm", s, t, None)
        for t in range(NT):
            put_dense("T4", "m", t, 0)
            put_dense("T4", "m", t, 1)
        put_dense("mm", "wo0", 0, None)
        for t in range(NT):
            if t + 1 < NT:
                put_dense("mm", "wo0", t + 1, None)
            if t:
                plan.append(("R", t - 1))
            put_dense("mm", "wo1", t, None)
            if t:
                plan.append(("L", t - 1))
            plan.append(("N", t))
        plan.append(("R", NT - 1))
        plan.append(("L", NT - 1))
        where = {(item[:3] if item[0] == "mm" else item): n for n, item in enumerate(dense)}

        def final_engine(n):
            kind, what = dense[n][0], dense[n][1]
            if kind == "T4":
                return "A" if what == "prep" or n % 2 == 0 else "D"
            return "D" if what[:2] in ("rg", "wr", "wd", "wo") else "A"

        count = {"A": 0, "D": 0}
        freed = []
        for n in range(len(dense)):
            e = final_engine(n)
            count[e] += 1
            freed.append((e, count[e]))
        rope_at = {}
        for item in dense:
            if item[0] == "mm" and item[1][:2] in ("dq", "dk") and item[2] < PT and item[3] == 1:
                rope_at[item[1:3]] = len(rope_at) + 1
        gate_at = {}
        for item in dense:
            if item[0] == "mm" and item[1][:2] == "rg":
                gate_at[item[1:]] = len(gate_at) + 1
        spill_at = {}
        for item in dense:
            if item[0] == "mm" and item[1][:2] in ("gr", "gd"):
                spill_at[item[1:]] = len(spill_at)
        last_of = {s: where[("mm", s, PT)] for s in SPLIT + WHOLE}
        unit_end = {n: unit_at[(item[1], item[3])] for n, item in enumerate(dense) if item[0] == "mm" and item[2] == PT}
        end_of = {i: n for n, i in unit_end.items()}
        n_u = {}
        u_before = 0
        sc_before = 0
        order = {}
        in_bank = {}
        for e in plan:
            if e[0] == "U":
                order[e] = (in_bank.get(e[3], 0), sc_before)
                u_before += 1
                in_bank[e[3]] = u_before
            if e[0] == "SC":
                order[e] = (u_before, sc_before)
                sc_before += 1
        RET = [PT, 0, 1, 2, 3]

        ld_const, ld_small, ld_x = sem("ld_const"), sem("ld_small"), sem("ld_x")
        ld_w = [sem("ld_w0"), sem("ld_w1")]
        ld_ada = [sem("ld_ada0"), sem("ld_ada1")]
        ld_state, ld_ctx = sem("ld_state"), [sem("ld_ctx0"), sem("ld_ctx1")]
        act_set, dve_set, pool_set, pe_set = sem("act_set"), sem("dve_set"), sem("pool_set"), sem("pe_set")
        dve_chain, act_chain, pool_chain = sem("dve_chain"), sem("act_chain"), sem("pool_chain")
        ssq_ready, rstd_ready, xn_ready = sem("ssq_ready"), sem("rstd_ready"), sem("xn_ready")
        pe_ada, ada_rows, pe_modT, mod_cols = sem("pe_ada"), sem("ada_rows"), sem("pe_modT"), sem("mod_cols")
        pe_dense, freed_a, freed_d = sem("pe_dense"), sem("freed_a"), sem("freed_d")
        rope_done, gate_done, merged = sem("rope_done"), sem("gate_done"), sem("merged")
        pe_u, u_read, u_keys = sem("pe_u"), sem("u_read"), sem("u_keys")
        pe_rt, rt_read, q_scaled = sem("pe_rt"), sem("rt_read"), sem("q_scaled")
        pe_sc, sc_masked, pe_o, o_read = sem("pe_sc"), sem("sc_masked"), sem("pe_o"), sem("o_read")
        o_stats, o_rstd, o_normed = sem("o_stats"), sem("o_rstd"), sem("o_normed")
        pe_scores, max_ready, exp_done, mixed_ready = sem("pe_scores"), sem("max_ready"), sem("exp_done"), sem("mixed_ready")
        tanh_done = sem("tanh_done")
        w_rounded, w_split, h_rounded, h_split = sem("w_rounded"), sem("w_split"), sem("h_rounded"), sem("h_split")
        st_gate, ld_gr, ld_gd = [sem(f"st_gate{i}") for i in range(4)], sem("ld_gr"), sem("ld_gd")
        pe_at, at_read, pe_pv, pv_read = sem("pe_at"), sem("at_read"), sem("pe_pv"), sem("pv_read")
        od_scaled, x1_ready = sem("od_scaled"), sem("x1_ready")
        st_mod, st_ret, st_kv = sem("st_mod"), sem("st_ret"), [sem("st_kv0"), sem("st_kv1")]
        st_fill = sem("st_fill")
        st_h2 = [sem("st_h2_0"), sem("st_h2_1")]
        ld_x1, ld_g1, ld_route, ld_row2 = sem("ld_x1"), sem("ld_g1"), sem("ld_route"), sem("ld_row2")
        st_sq2, pool2, h2_ready, pe_h2, h2_read, pe_logits = (sem(x) for x in
            ("st_sq2", "pool2", "h2_ready", "pe_h2", "h2_read", "pe_logits"))
        route_d, route_a, pe_rank, pe_table, idx_ready = (sem(x) for x in
            ("route_d", "route_a", "pe_rank", "pe_table", "idx_ready"))
        ld_gu, ld_dn = [sem(f"ld_gu{i}") for i in range(6)], [sem(f"ld_dn{i}") for i in range(6)]
        ld_xg = [sem("ld_xg0"), sem("ld_xg1")]
        ov_take = sem("ov_take")
        pe_xt, xt_read, pe_gu, gu_tanh, gu_act, pe_aT, aT_read, pe_dn, y_a, y_d = (sem(x) for x in
            ("pe_xt", "xt_read", "pe_gu", "gu_tanh", "gu_act", "pe_aT", "aT_read", "pe_dn", "y_a", "y_d"))
        gu_half = sem("gu_half")
        st_y = [sem("st_y0"), sem("st_y1")]
        (ov_free, ov_idx, ov_x, ov_w, ov_xt, ov_xr, ov_gu, ov_tanh, ov_half, ov_act, ov_aT, ov_ar, ov_dn, ov_ya,
         ov_yd, ov_st, ov_over) = (sem("ov_" + x) for x in ("free", "idx", "x", "w", "xt", "xr", "gu", "tanh", "half",
                                   "act", "aT", "ar", "dn", "ya", "yd", "st", "over"))
        ld_y = [sem(f"ld_y{t}") for t in range(NT)]
        y_used, fin_sq, fin_rstd, fin_ready, ld_fin = (sem(x) for x in ("y_used", "fin_sq", "fin_rstd", "fin_ready", "ld_fin"))
        y_scaled = sem("y_scaled")
        st_fin = [sem("st_fin0"), sem("st_fin1")]
        n_freed = {"A": count["A"], "D": count["D"]}

        block = ctx.enter_context(nc.Block())

        def wait_freed(eng, n):
            e, v = freed[n]
            eng.wait_ge(freed_a if e == "A" else freed_d, v)

        def free(ins, n):
            ins.then_inc(freed_a if freed[n][0] == "A" else freed_d, 1)

        @block.sync
        def _(sp):
            sp.dma_start(const[:], a["const"][:, setup_n:]).then_inc(ld_const, 16)
            sp.dma_start(const0, a["const"][:, 0:setup_n]).then_inc(ld_const, 16)
            small = 0
            vec = lambda v: v.rearrange("(k p) -> k p", p=P)
            for r0, v in ((0, a["c"][0]), (8, a["c_ctx"]), (16, a["norm1_g"][0]), (24, a["norm2_g"][0]),
                          (32, a["ret_norm_g"][0])):
                sp.dma_start(rows[r0:r0 + 8, :], vec(v)).then_inc(ld_small, 16)
            sp.dma_start(rows[40:41, :], vec(a["diff_subln_g"][0])).then_inc(ld_small, 16)
            sp.dma_start(dec[:, 0:4], a["ret_decay_fwd"][0].partition_broadcast(P)).then_inc(ld_small, 16)
            sp.dma_start(dec[:, 4:8], a["ret_decay_bwd"][0].partition_broadcast(P)).then_inc(ld_small, 16)
            for i, v in enumerate(("diff_lambda_q1", "diff_lambda_k1", "diff_lambda_q2", "diff_lambda_k2")):
                sp.dma_start(lam_in[:, i, :], a[v][0].partition_broadcast(P)).then_inc(ld_small, 16)
            for j in range(4):
                src = a["b_ada"][0].rearrange("(r j n) -> j r n", r=3, j=4)[j]
                sp.dma_start(bias_rows[32 * j:32 * j + 32, :, :], src.partition_broadcast(32)).then_inc(ld_small, 16)

            def load_ada(i):
                if i >= 2:
                    sp.wait_ge(pe_ada, i - 1)
                r, k = divmod(i, KC)
                sp.dma_start(ada_ring[i % 2], a["w_ada"][0][k * P:(k + 1) * P, 2048 * r:2048 * r + 2048]).then_inc(ld_ada[i % 2], 16)

            def load_w(i):
                if i >= 2:
                    sp.wait_ge(pe_dense, end_of[i - 2] + 1)
                dst = w_raw if i < N_SPLIT else w_ring
                sp.dma_start(dst[i % 2], section_source(*UNITS[i])).then_inc(ld_w[i % 2], 16)

            for i in range(2):
                load_ada(i)
            for t in range(NT):
                src = a["x_prompt"][0] if t == PT else a["x_sample"][0][t * P:(t + 1) * P, :]
                sp.dma_start(xn[:, t, :], src).then_inc(ld_x, 16)
            for i in range(2, KC):
                load_ada(i)
            load_w(0)
            load_w(1)
            load_ada(KC)
            load_ada(KC + 1)

            def mod_out():
                for r in (1, 2):
                    sp.wait_ge(ada_rows, r + 1)
                    for j in range(4):
                        c0 = (4 * r + j) * N512
                        sp.dma_start(mod_dram[:, c0:c0 + N512], mod_rows[32 * j:32 * j + 2, r, :]).then_inc(st_mod, 16)
                sp.wait_ge(pe_ada, 3 * KC)
                sp.dma_start(states_b[:, 3, :].rearrange("p (h e) -> p h e", h=RH),
                             a["state_ret_bwd"][0, 0].rearrange("h d e -> d h e")).then_inc(ld_state, 16)
                sp.wait_ge(st_mod, 16 * 8)
                sp.wait_ge(ada_rows, 3)
                sp.dma_start(state_f.rearrange("p (h e) -> p h e", h=RH),
                             a["state_ret_fwd"][0, 0].rearrange("h d e -> d h e")).then_inc(ld_state, 16)

            def fill_out():
                for i in range(OVER * BLK // (NT * P)):
                    r0 = NE * BLK + i * NT * P
                    sp.dma_start(y_dram[r0:r0 + NT * P, :].rearrange("(p k) n -> p (k n)", k=NT),
                                 h_hi[:].bitcast(F32).rearrange("p k t -> p (k t)")).then_inc(st_fill, 16)

            def state_out_dma(i):
                sp.wait_ge(u_read, 2 * (3 + i) + 2)
                sp.dma_start(o[("out_ret_f", "out_ret_b")[i]][0, 0].rearrange("h d e -> d h e"),
                             state_out[:, i, :].rearrange("p (h e) -> p h e", h=RH)).then_inc(st_ret, 16)

            def keys_out(half):
                c0 = N512 * half
                wait_freed(sp, where[("mm", f"dk{half}", PT)])
                sp.dma_start(o["out_k"][0, 0].rearrange("t h c d -> t (h c d)")[:, c0:c0 + N512], dk[:, PT, :]).then_inc(st_kv[half], 16)

            def values_out(half):
                c0 = N512 * half
                wait_freed(sp, where[("mm", f"dv{half}", PT)])
                sp.dma_start(o["out_v"][0, 0].rearrange("t h d -> t (h d)")[:, c0:c0 + N512], dv[:, PT, :]).then_inc(st_kv[half], 16)

            def gate_out(n):
                _, s, t, hh = dense[n]
                v = spill_at[dense[n][1:]]
                c0 = N512 * int(s[2]) + N256 * hh
                wait_freed(sp, n)
                sp.dma_start(gates_dram[0 if s[:2] == "gr" else 1, :, t, c0:c0 + N256], gate_t[:, v % 4, :]).then_inc(st_gate[v % 4], 16)

            def load_gates(i, dst, done):
                for x in st_gate:
                    sp.wait_ge(x, 16 * len(spill_at) // 4)
                sp.dma_start(dst, gates_dram[i]).then_inc(done, 16)

            def load_ctx(half):
                c0 = N512 * half
                sp.dma_start(ctx_k, a["cache_diff_k"][0, 0].rearrange("(t p) h c d -> p t (h c d)", p=P)[:, :, c0:c0 + N512]).then_inc(ld_ctx[half], 16)
                sp.dma_start(ctx_v, a["cache_diff_v"][0, 0].rearrange("(t p) h d -> p t (h d)", p=P)[:, :, c0:c0 + N512]).then_inc(ld_ctx[half], 16)

            def residual():
                sp.wait_ge(pe_pv, 40)
                sp.wait_ge(st_ret, 16 * 2)
                sp.wait_ge(st_kv[0], 16 * 2)
                sp.wait_ge(st_kv[1], 16 * 2)
                for t in range(NT):
                    src = a["x_prompt"][0] if t == PT else a["x_sample"][0][t * P:(t + 1) * P, :]
                    sp.dma_start(x1[:, t, :], src).then_inc(ld_x1, 16)
                for s in range(2):
                    sp.dma_start(g1_rows[:, s, :], mod_dram[s, 2 * D:3 * D].partition_broadcast(P)).then_inc(ld_g1, 16)

            def load_gate_up(e, slot):
                for g, w in enumerate((a["moe_w_gate"], a["moe_w_up"])):
                    sp.dma_start(w_gu[slot][:, :, g, :], w[0, e].rearrange("(k p) f -> p k f", p=P)).then_inc(ld_gu[slot], 16)

            def load_down(e, slot):
                sp.dma_start(w_dn[slot], a["moe_w_down"][0, e].rearrange("(k p) n -> p k n", p=P)).then_inc(ld_dn[slot], 16)

            def load_expert(e, slot):
                load_gate_up(e, slot)
                load_down(e, slot)

            for e in plan:
                if e[0] == "ada":
                    i = e[1] * KC + e[2]
                    if i + 2 < 3 * KC:
                        load_ada(i + 2)
                    if i == 3 * KC - 1:
                        mod_out()
                elif e[0] == "U" and e[1] in (3, 4) and e[2] == 1:
                    state_out_dma(e[1] - 3)
                elif e[0] == "ret_end":
                    sp.wait_ge(pe_rt, NT)
                    sp.wait_ge(u_keys, len(UPDATES))
                    load_ctx(0)
                    fill_out()
                elif e[0] == "N":
                    t = e[1]
                    sp.wait_ge(h2_ready, t + 1)
                    sp.dma_start(h2_dram[t * P:(t + 1) * P, :], h2[:, t % 2, :]).then_inc(st_h2[t % 2], 16)
                elif e == ("PV", 19):
                    sp.wait_ge(pe_pv, 20)
                    load_ctx(1)
                elif e[0] == "att_end":
                    residual()
                    load_expert(0, 0)
                    load_expert(1, 1)
                elif e[0] == "dense":
                    n = e[1]
                    item = dense[n]
                    if item[1][:2] in ("gr", "gd"):
                        gate_out(n)
                    if n in unit_end:
                        i = unit_end[n]
                        if i + 2 < len(UNITS):
                            load_w(i + 2)
                        if item[1][:2] == "dk" and item[3] == 1:
                            keys_out(int(item[1][2]))
                        elif item[1][:2] == "dv" and item[3] == 1:
                            values_out(int(item[1][2]))
                    if n == last_of["dv1"]:
                        sp.wait_ge(pe_dense, n + 1)
                        sp.wait_ge(st_fill, 16 * 2)
                        load_gates(0, gr_t, ld_gr)
                    elif n == last_of["wr1"]:
                        sp.wait_ge(pe_dense, n + 1)
                        load_gates(1, gd_t, ld_gd)
                    elif n == last_of["wo1"]:
                        sp.wait_ge(pe_dense, n + 1)
                        load_expert(2, 2)
                    elif n == last_of["wd1"]:
                        sp.wait_ge(pe_dense, n + 1)
                        sp.dma_start(route, a["route"]).then_inc(ld_route, 16)
                        sp.dma_start(rw[:, :, 0:GRP], a["router_group_w"][0].rearrange("(k p) n -> p k n", p=P)).then_inc(ld_route, 16)
                        sp.dma_start(rw[:, :, GRP:36], a["router_expert_w"][0].rearrange("(k p) n -> p k n", p=P)).then_inc(ld_route, 16)
                        sp.dma_start(rb[:, 0:GRP], a["router_group_b"][0].partition_broadcast(P)).then_inc(ld_route, 16)
                        sp.dma_start(rb[:, GRP:36], a["router_expert_b"][0].partition_broadcast(P)).then_inc(ld_route, 16)
                        sp.dma_start(n2_row, a["norm2_g"][0].partition_broadcast(P)).then_inc(ld_route, 16)
                    elif item == ("T4", "m", PT, 1):
                        sp.wait_ge(pe_dense, n + 1)
                        for i in range(2):
                            sp.dma_start(scale2[:, i, :], mod_dram[i, 4 * D:5 * D].partition_broadcast(P)).then_inc(ld_row2, 16)
                            sp.dma_start(shift2[:, i, :], mod_dram[i, 3 * D:4 * D].partition_broadcast(P)).then_inc(ld_row2, 16)
            sp.wait_ge(h2_ready, NT)
            load_gate_up(3, 3)
            sp.wait_ge(x1_ready, 2 * NT)
            load_down(3, 3)
            sp.wait_ge(st_sq2, NT)
            sp.wait_ge(pe_h2, NT)
            sp.wait_ge(st_h2[0], 16 * 3)
            sp.wait_ge(st_h2[1], 16 * 2)
            load_expert(4, 4)
            sp.wait_ge(pe_logits, NT)
            load_expert(5, 5)

            def pair_io(p, par, into=None):
                if into:
                    sp.wait_ge(pe_gu, p + 1)
                    for i in range(2):
                        load_gate_up(into[0] + i, into[1] + i)
                    sp.wait_ge(pe_dn, p + 1)
                    for i in range(2):
                        load_down(into[0] + i, into[1] + i)
                sp.wait_ge(y_a, p + 1)
                sp.wait_ge(y_d, p + 1)
                sp.dma_start(y_dram[bass.ds(p * P, P), :], y_out[:, par, :]).then_inc(st_y[par], 16)

            pair_io(0, 0, (6, 0))
            pair_io(1, 1, (8, 2))
            pair_io(2, 0)
            for i in range(2):
                sp.dma_start(g2_rows[:, i, :], mod_dram[i, 5 * D:6 * D].partition_broadcast(P)).then_inc(ld_fin, 16)
            sp.dma_start(fin_row, a["final_norm_g"].partition_broadcast(P)).then_inc(ld_fin, 16)
            with sp.Fori(0, (PAIRS - 6) // 2) as i:
                pair_io(2 * i + 3, 1, (4 * i + 10, 0))
                pair_io(2 * i + 4, 0, (4 * i + 12, 2))
            pair_io(PAIRS - 3, 1, (NE - 2, 0))
            pair_io(PAIRS - 2, 0)
            pair_io(PAIRS - 1, 1)
            for par in range(2):
                sp.wait_ge(st_y[par], 16 * PAIRS // 2)
            n_over = sp.value_load(n_ov[0:1, 0:1], min_val=0, max_val=OVER)
            with sp.If(n_over > 0):
                with sp.Fori(0, OVER // 2) as j:
                    with sp.If(n_over > 2 * j):
                        sp.wait_ge(ov_free, j + 1)
                        for i in range(2):
                            e = sp.value_load(ov_exp[0:1, bass.ds(2 * j + i, 1)], min_val=0, max_val=NE - 1)
                            for g, w in enumerate((a["moe_w_gate"], a["moe_w_up"])):
                                sp.dma_start(w_gu[i][:, :, g, :], w[0, bass.ds(e, 1)].rearrange("o (k p) f -> p (o k) f", p=P)).then_inc(ov_w, 16)
                            sp.dma_start(w_dn[i], a["moe_w_down"][0, bass.ds(e, 1)].rearrange("o (k p) n -> p (o k) n", p=P)).then_inc(ov_w, 16)
                        sp.wait_ge(ov_ya, j + 1)
                        sp.wait_ge(ov_yd, j + 1)
                        sp.dma_start(y_dram[bass.ds((j + PAIRS) * P, P), :], y_out[:, 0, :]).then_inc(ov_st, 16)
                        sp.wait_ge(ov_st, 16 * j + 16)
                        sp.sem_inc(ov_free, 1)
                    with sp.Else():
                        sp.nop()
            with sp.Else():
                sp.nop()
            sp.sem_inc(ov_over, 1)
            for t in range(NT):
                sp.wait_ge(fin_ready, t + 1)
                dst = o["out_p"][0] if t == PT else o["out_s"][0][t * P:(t + 1) * P, :]
                sp.dma_start(dst, fin_t[:, t % 2, :]).then_inc(st_fin[t % 2], 16)
            sp.wait_ge(st_fin[0], 16 * 3)
            sp.wait_ge(st_fin[1], 16 * 2)
            sp.wait_ge(st_ret, 16 * 2)
            sp.wait_ge(st_kv[0], 16 * 2)
            sp.wait_ge(st_kv[1], 16 * 2)

        @block.tensor
        def _(pe):
            ident = C("ident")
            pe.wait_ge(ld_const, 32)
            pe.wait_ge(dve_set, 1)
            pe.transpose(B(7)[:, 0:41], rows[0:41, :], ident[0:41, 0:41]).then_inc(pe_set, 1)

            def ada(r, k):
                i = r * KC + k
                pe.wait_ge(ld_ada[i % 2], 16 * (i // 2 + 1))
                if k == 0:
                    pe.wait_ge(dve_set, 2)
                    if r:
                        pe.wait_ge(ada_rows, r)
                for j in range(4):
                    mm = pe.matmul(B(7)[32 * j:32 * j + 32, :], ccol[:, k, :], ada_ring[i % 2][:, j * N512:(j + 1) * N512],
                                   start=(k == 0), stop=(k == KC - 1))
                mm.then_inc(pe_ada, 1)

            def mod_columns(r):
                pe.wait_ge(ada_rows, r + 1)
                if r:
                    pe.wait_ge(mod_cols, r)
                for m in range(4):
                    mm = pe.transpose(B(2)[:, m * P:(m + 1) * P], mod_rows[:, r, m * P:(m + 1) * P], ident)
                mm.then_inc(pe_modT, 1)

            for k in range(KC):
                ada(0, k)
            mod_columns(0)

            def dense_item(n):
                item = dense[n]
                if n >= 2:
                    wait_freed(pe, n - 2)
                out = B(n % 2)
                if item[0] == "mm":
                    _, s, t, hh = item
                    i = unit_at[(s, hh)]
                    if i < N_SPLIT:
                        if t == 0:
                            pe.wait_ge(w_split, i + 1)
                        if i == 0:
                            pe.wait_ge(h_split, 2 * t + 2)
                        for k in range(KC):
                            for j, (x, w) in enumerate(((h_hi, w_hi), (h_hi, w_lo), (h_lo, w_hi))):
                                mm = pe.matmul(out[:, 0:N256], x[:, k, t * P:(t + 1) * P], w[i % 2][:, k, :],
                                               start=(k == 0 and j == 0), stop=(k == KC - 1 and j == 2))
                    else:
                        if t == 0:
                            pe.wait_ge(ld_w[i % 2], 16 * (i // 2 + 1))
                        src = {"wr": oT, "wd": odT, "wo": mT}[s[:2]]
                        what = {"wr": "o", "wd": "od", "wo": "m"}[s[:2]]
                        wait_freed(pe, where[("T4", what, t, 0)])
                        wait_freed(pe, where[("T4", what, t, 1)])
                        for k in range(KC):
                            mm = pe.matmul(out, src[:, k, t * P:(t + 1) * P], w_ring[i % 2][:, k, :],
                                           start=(k == 0), stop=(k == KC - 1))
                else:
                    _, what, t, half = item
                    if what == "prep":
                        h, i = t, half
                        c0 = P * (h % 4)
                        hf = h // 4
                        if i == 0:
                            pe.wait_ge(rope_done, rope_at[(f"dq{hf}", PT - 1)])
                            src = [dq[:, q, c0:c0 + P] for q in range(4)]
                        elif i == 1:
                            pe.wait_ge(rope_done, rope_at[(f"dk{hf}", PT - 1)])
                            src = [dk[:, q, c0:c0 + P] for q in range(4)]
                        else:
                            pe.wait_ge(ld_ctx[hf], 32)
                            wait_freed(pe, where[("mm", f"dk{hf}", PT)])
                            src = [ctx_k[:, 0, c0:c0 + P], ctx_k[:, 1, c0:c0 + P], dk[:, PT, c0:c0 + P], dq[:, PT, c0:c0 + P]]
                    else:
                        if what == "h":
                            pe.wait_ge(xn_ready, t + 1)
                            buf = xn
                        elif what == "o":
                            pe.wait_ge(gate_done, gate_at[(f"rg{half}", t, 1)])
                            buf = ret
                        elif what == "od":
                            pe.wait_ge(od_scaled, t + 1)
                            buf = od
                        else:
                            pe.wait_ge(merged, NT + t + 1)
                            buf = merge
                        src = [buf[:, t, (4 * half + k) * P:(4 * half + k + 1) * P] for k in range(4)]
                    for k in range(4):
                        mm = pe.transpose(out[:, k * P:(k + 1) * P], src[k], ident)
                mm.then_inc(pe_dense, 1)

            def update(e):
                _, u, half, b = e
                dirn, t = UPDATES[u]
                ub, sc = order[e]
                pe.wait_ge(u_keys, u + 1)
                if ub:
                    pe.wait_ge(u_read, ub)
                if b == 4 and sc:
                    pe.wait_ge(sc_masked, sc)
                for i in range(2):
                    h = 2 * half + i
                    mm = pe.matmul(B(b)[:, i * RV:(i + 1) * RV], ks[:, u % 2, h * P:(h + 1) * P],
                                   rv[:, t, h * RV:(h + 1) * RV], start=(i == 0), stop=(i == 1), skip_group_check=True)
                mm.then_inc(pe_u, 1)

            def router_transposes(t):
                pe.wait_ge(h2_ready, t + 1)
                if t:
                    pe.wait_ge(h2_read, t)
                else:
                    pe.wait_ge(at_read, len(steps))
                for k in range(KC):
                    mm = pe.transpose(B(5 + k // 4)[:, (k % 4) * P:(k % 4 + 1) * P], h2[:, t % 2, k * P:(k + 1) * P], ident)
                mm.then_inc(pe_h2, 1)

            def logits_of(t):
                if t == 0:
                    pe.wait_ge(ld_route, 16 * 6)
                    pe.wait_ge(mixed_ready, len(steps))
                pe.wait_ge(h2_read, t + 1)
                for k in range(KC):
                    mm = pe.matmul(B(2)[:, t * 36:(t + 1) * 36], h2T[:, k, t * P:(t + 1) * P], rw[:, k, :],
                                   start=(k == 0), stop=(k == KC - 1), skip_group_check=True)
                mm.then_inc(pe_logits, 1)

            n_rt = n_sc = n_o = 0
            for e in plan:
                if e[0] == "dense":
                    dense_item(e[1])
                elif e[0] == "R":
                    router_transposes(e[1])
                elif e[0] == "L":
                    logits_of(e[1])
                elif e[0] == "ada":
                    ada(e[1], e[2])
                    if e[2] == KC - 1:
                        mod_columns(e[1])
                elif e[0] == "U":
                    update(e)
                elif e[0] == "RT":
                    t = e[1]
                    if n_rt:
                        pe.wait_ge(rt_read, n_rt)
                    if n_rt == 0:
                        pe.wait_ge(mod_cols, 3)
                    for h in range(RH):
                        pe.transpose(B(2)[:, h * P:(h + 1) * P], rq[:, t, h * P:(h + 1) * P], ident)
                    for h in range(RH):
                        mm = pe.transpose(B(3)[:, h * P:(h + 1) * P], rk[:, t, h * P:(h + 1) * P], ident)
                    mm.then_inc(pe_rt, 1)
                    n_rt += 1
                elif e[0] == "SC":
                    n_sc += 1
                    pe.wait_ge(rt_read, n_sc)
                    pe.wait_ge(u_read, order[e][0])
                    if n_sc > 1:
                        pe.wait_ge(sc_masked, n_sc - 1)
                    for h in range(RH):
                        mm = pe.matmul(B(4)[:, h * P:(h + 1) * P], rkT[:, h * P:(h + 1) * P], rqT[:, h * P:(h + 1) * P],
                                       start=(h == 0), stop=(h == RH - 1), skip_group_check=True)
                    mm.then_inc(pe_sc, 1)
                elif e[0] == "O":
                    t = e[1]
                    n_o += 1
                    pe.wait_ge(sc_masked, n_o)
                    if n_o > 1:
                        pe.wait_ge(o_read, n_o - 1)
                    if t != PT:
                        pe.wait_ge(q_scaled, t + 1)
                        pe.wait_ge(ld_state, 32)
                        pe.wait_ge(u_read, 6 if t == 0 else 10 + 2 * t)
                    for h in range(RH):
                        out = B(5 + h // 2)[:, (h % 2) * RV:(h % 2 + 1) * RV]
                        mm = pe.matmul(out, sm[:, h * P:(h + 1) * P], rv[:, t, h * RV:(h + 1) * RV],
                                       start=(h % 2 == 0), stop=(t == PT and h % 2 == 1), skip_group_check=True)
                        if t != PT:
                            pe.matmul(out, qf[:, h * P:(h + 1) * P], state_f[:, h * RV:(h + 1) * RV],
                                      start=False, stop=False, skip_group_check=True)
                            mm = pe.matmul(out, qb[:, h * P:(h + 1) * P], states_b[:, t, h * RV:(h + 1) * RV],
                                           start=False, stop=(h % 2 == 1), skip_group_check=True)
                    mm.then_inc(pe_o, 1)
                elif e[0] == "S":
                    s = e[1]
                    h, t = steps[s]
                    if t == 0:
                        wait_freed(pe, where[("T4", "prep", h, 2)])
                    if s:
                        pe.wait_ge(exp_done, 2 * s)
                    else:
                        pe.wait_ge(sc_masked, NT)
                        pe.wait_ge(rt_read, NT)
                        pe.wait_ge(u_read, 2 * len(UPDATES))
                    for c in range(2):
                        q = qz[h % 2][:, c, t * P:(t + 1) * P] if t < PT else qzp[h % 2][:, c, :]
                        spans = [(0, 512), (512, 768)] if c == 0 else [(0, 256), (256, 768)]
                        if t == PT:
                            spans = [(0, P)]
                        for lo, hi in spans:
                            keys = kT[h % 2][:, lo:hi] if t < PT else kT[h % 2][:, KEYS:KEYS + P]
                            mm = pe.matmul(score[c][:, lo:hi], q, keys, start=True, stop=True, skip_group_check=True)
                    mm.then_inc(pe_scores, 1)
                elif e[0] == "AT":
                    s = e[1]
                    h, t = steps[s]
                    pe.wait_ge(mixed_ready, s + 1)
                    if s:
                        pe.wait_ge(at_read, s)
                    else:
                        pe.wait_ge(o_read, NT)
                    for k in range(6 if t < PT else 1):
                        mm = pe.transpose(B(5 + k // 4)[:, (k % 4) * P:(k % 4 + 1) * P], mixed[:, k * P:(k + 1) * P], ident)
                    mm.then_inc(pe_at, 1)
                elif e[0] == "PV":
                    s = e[1]
                    h, t = steps[s]
                    c0 = P * (h % 4)
                    pe.wait_ge(at_read, s + 1)
                    if s:
                        pe.wait_ge(pv_read, s)
                    else:
                        pe.wait_ge(u_read, 2 * len(UPDATES))
                    if t == 0:
                        wait_freed(pe, where[("mm", f"dv{h // 4}", PT)])
                    if t == PT:
                        mm = pe.matmul(B(7)[:, 0:P], mixedT[s % 2][:, 0:P], dv[:, PT, c0:c0 + P], start=True, stop=True)
                    else:
                        for k in range(6):
                            v = dv[:, k, c0:c0 + P] if k < 4 else ctx_v[:, k - 4, c0:c0 + P]
                            mm = pe.matmul(B(7)[:, 0:P], mixedT[s % 2][:, k * P:(k + 1) * P], v, start=(k == 0), stop=(k == 5))
                    mm.then_inc(pe_pv, 1)

            pe.wait_ge(route_d, 3)
            pe.matmul(B(3)[:, 0:NT * NE], R("before"), e_any.rearrange("p t n -> p (t n)"), start=True, stop=True)
            pe.matmul(B(4)[:, 0:NT * NE], R("ones"), e_any.rearrange("p t n -> p (t n)"), start=True, stop=True).then_inc(pe_rank, 1)
            pe.wait_ge(route_d, 4)
            for x in range(2 * NT):
                mm = pe.matmul(B(5)[:, 0:NPAIR], hot_pos[:, x, :], val_pair[:, x, :], start=(x == 0), stop=(x == 2 * NT - 1))
            mm.then_inc(pe_table, 1)

            def gathered(slot):
                for k in range(KC):
                    mm = pe.transpose(B(k // 4)[:, (k % 4) * P:(k % 4 + 1) * P], xg[:, slot, k * P:(k + 1) * P], ident)
                return mm

            def gate_up(slot, e0, bank_at):
                for k in range(KC):
                    for i in range(2):
                        mm = pe.matmul(B(bank_at)[BLK * i:BLK * (i + 1), :], xgT[slot][:, k, BLK * i:BLK * (i + 1)],
                                       w_gu[e0 + i][:, k, :, :].rearrange("p g f -> p (g f)"), start=(k == 0), stop=(k == KC - 1))
                return mm

            def hidden(slot):
                for k in range(2):
                    mm = pe.transpose(B(4)[:, k * P:(k + 1) * P], act_a[:, slot, k * P:(k + 1) * P], ident)
                return mm

            def down(slot, e0):
                for n in range(2):
                    for k in range(2):
                        for i in range(2):
                            mm = pe.matmul(B(5 + n)[BLK * i:BLK * (i + 1), :], act_aT[slot][:, k, BLK * i:BLK * (i + 1)],
                                           w_dn[e0 + i][:, k, n * N512:(n + 1) * N512], start=(k == 0), stop=(k == 1))
                return mm

            def pair_gathered(p, par, turn):
                pe.wait_ge(ld_xg[par], 16 * turn + 16)
                pe.wait_ge(xt_read, p)
                gathered(par).then_inc(pe_xt, 1)

            def pair(p, par, slot, turn, wturn, first=False, last=False):
                for i in range(2):
                    pe.wait_ge(ld_gu[slot + i], 32 * wturn + 32)
                pe.wait_ge(xt_read, p + 1)
                gate_up(par, slot, 2 + par).then_inc(pe_gu, 1)
                if not last:
                    pair_gathered(p + 1, 1 - par, turn + par)
                pe.wait_ge(gu_act, p + 1)
                hidden(par).then_inc(pe_aT, 1)
                pe.wait_ge(aT_read, p + 1)
                for i in range(2):
                    pe.wait_ge(ld_dn[slot + i], 16 * wturn + 16)
                if not first:
                    pe.wait_ge(y_a, p)
                    pe.wait_ge(y_d, p)
                down(par, slot).then_inc(pe_dn, 1)

            pe.wait_ge(idx_ready, 1)
            pe.wait_ge(ld_xg[0], 16)
            gathered(0).then_inc(pe_xt, 1)
            pair(0, 0, 0, 0, 0, first=True)
            pair(1, 1, 2, 0, 0)
            pair(2, 0, 4, 1, 0)
            with pe.Fori(0, (PAIRS - 4) // 2) as i:
                pair(2 * i + 3, 1, 0, i + 1, i + 1)
                pair(2 * i + 4, 0, 2, i + 2, i + 1)
            pair(PAIRS - 1, 1, 0, PAIRS // 2 - 1, PAIRS // 2 - 1, last=True)
            n_over = pe.value_load(n_ov[0:1, 0:1], min_val=0, max_val=OVER)
            pe.wait_ge(y_a, PAIRS)
            pe.wait_ge(y_d, PAIRS)
            with pe.If(n_over > 0):
                with pe.Fori(0, OVER // 2) as j:
                    with pe.If(n_over > 2 * j):
                        pe.wait_ge(ov_x, 16 * j + 16)
                        gathered(0).then_inc(ov_xt, 1)
                        pe.wait_ge(ov_xr, j + 1)
                        pe.wait_ge(ov_w, 96 * j + 96)
                        gate_up(0, 0, 2).then_inc(ov_gu, 1)
                        pe.wait_ge(ov_act, j + 1)
                        hidden(0).then_inc(ov_aT, 1)
                        pe.wait_ge(ov_ar, j + 1)
                        down(0, 0).then_inc(ov_dn, 1)
                    with pe.Else():
                        pe.nop()

            with pe.Else():
                pe.nop()
        @block.scalar
        def _(act):
            chain = [0]

            def link(ins):
                chain[0] += 1
                ins.then_inc(act_chain, 1)
                act.wait_ge(act_chain, chain[0])

            act.wait_ge(ld_small, 16 * 16)
            act.activation(rows_t[0:16, :], rows[0:16, :], ACT.Tanh, scale=0.5).then_inc(act_set, 1)
            for t in range(NT):
                if t == 0:
                    act.wait_ge(ld_x, 16 * NT)
                else:
                    act.wait_ge(ssq_ready, t)
                act.activation(square_t, xn[:, t, :], ACT.Square, accum_out=ssq[:, t:t + 1]).then_inc(ssq_ready, 1)
            act.wait_ge(dve_set, 3)
            act.activation(dec_e[:], dec_n[:], ACT.Exp, scale=-1.0).then_inc(act_set, 1)
            act.wait_ge(dve_set, 4)
            act.activation(dec_e[:], dec_n[:], ACT.Ln).then_inc(act_set, 1)
            act.wait_ge(dve_set, 5)
            act.wait_ge(ld_const, 32)
            for h in range(8):
                fw = h < 4
                act.activation(decay_e[:, h, :], C("rel_f" if fw else "rel_b"), ACT.Exp, scale=lg[:, h:h + 1])
                act.activation(q_dec[:, h, :], C("pos_f" if fw else "pos_b"), ACT.Exp, scale=lg[:, h:h + 1])
            act.activation(kd[:], dec_n[:], ACT.Exp)
            act.activation(cd[:], lg[:], ACT.Exp, scale=float(P))
            act.activation(lam_s[:], lam_s[:], ACT.Exp).then_inc(act_set, 1)

            def scale_copy(dst, src, s, b=None):
                if b is None:
                    return act.activation(dst, src, ACT.Copy, scale=s)
                return act.activation(dst, src, ACT.Identity, scale=s, bias=b)

            def dense_item(n):
                item = dense[n]
                src = B(n % 2)
                if item[0] == "T4":
                    if freed[n][0] != "A":
                        return
                    _, what, t, half = item
                    act.wait_ge(pe_dense, n + 1)
                    if what == "prep":
                        h, i = t, half
                        if i == 0:
                            if h < 2:
                                act.wait_ge(dve_set, 8)
                            act.copy(qz[h % 2][0:DH, 0, :], src[0:DH, :])
                            ins = act.copy(qz[h % 2][DH:P, 1, :], src[DH:P, :])
                        elif i == 1:
                            ins = act.copy(kT[h % 2][:, 0:512], src)
                        else:
                            act.copy(kT[h % 2][:, 512:KEYS + P], src[:, 0:3 * P])
                            act.copy(qzp[h % 2][0:DH, 0, :], src[0:DH, 3 * P:4 * P])
                            ins = act.copy(qzp[h % 2][DH:P, 1, :], src[DH:P, 3 * P:4 * P])
                    else:
                        s = 1 if t == PT else 0
                        if what == "h":
                            act.wait_ge(dve_set, 7)
                            for k in range(4):
                                kk = 4 * half + k
                                ins = scale_copy(h_full[:, kk, t * P:(t + 1) * P], src[:, k * P:(k + 1) * P],
                                                 mul1[:, kk, s:s + 1], modc[:, kk, s:s + 1])
                        elif what == "o":
                            for k in range(4):
                                kk = 4 * half + k
                                ins = scale_copy(oT[:, kk, t * P:(t + 1) * P], src[:, k * P:(k + 1) * P], cols[:, 16 + kk:17 + kk])
                        elif what == "od":
                            if t == 0:
                                wait_freed(act, where[("mm", "wr1", PT)])
                            ins = scale_copy(odT[:, 4 * half:4 * half + 4, t * P:(t + 1) * P],
                                             src.rearrange("p (k n) -> p k n", k=4), cols[:, 24:25])
                        else:
                            ins = scale_copy(mT[:, 4 * half:4 * half + 4, t * P:(t + 1) * P],
                                             src.rearrange("p (k n) -> p k n", k=4), 0.5)
                    free(ins, n)
                    return
                _, s, t, hh = item
                kind = s[:2]
                if kind in ("wr", "wd", "wo"):
                    return
                act.wait_ge(pe_dense, n + 1)
                src = src[:, 0:N256]
                if kind == "rg":
                    u = gate_at[item[1:]] - 1
                    if u == 0:
                        act.wait_ge(pe_rt, NT)
                        act.wait_ge(u_keys, len(UPDATES))
                    if u >= 2:
                        act.wait_ge(gate_done, u - 1)
                    act.activation(gate_t[:, u % 2, :], src, ACT.Tanh, scale=0.5).then_inc(tanh_done, 1)
                    return
                if kind in ("gr", "gd"):
                    v = spill_at[item[1:]]
                    if v == 0:
                        act.wait_ge(gate_done, len(gate_at))
                    if v >= 4:
                        act.wait_ge(st_gate[v % 4], 16 * (v // 4))
                    free(act.activation(gate_t[:, v % 4, :], src, ACT.Tanh, scale=0.5), n)
                    return
                if kind == "dv" or kind == "dk":
                    if s[2] == "1" and t == PT:
                        act.wait_ge(st_kv[0], 16 * 2)
                if s == "dq0" and t == 0:
                    act.wait_ge(dve_set, 6)
                dst = {"rq": rq, "rk": rk, "rv": rv, "dq": dq, "dk": dk, "dv": dv}[kind]
                c0 = N256 * hh + (N512 * int(s[2]) if kind == "rv" else 0)
                free(act.copy(dst[:, t, c0:c0 + N256], src), n)

            def high_part(n):
                _, _, t, half = dense[n]
                wait_freed(act, n)
                act.copy(h_hi[:, 4 * half:4 * half + 4, t * P:(t + 1) * P],
                         h_full[:, 4 * half:4 * half + 4, t * P:(t + 1) * P]).then_inc(h_rounded, 1)

            for e in plan:
                if e[0] == "dense":
                    dense_item(e[1])
                    if dense[e[1]][:2] == ("T4", "h"):
                        high_part(e[1])
                elif e[0] == "N":
                    t = e[1]
                    act.wait_ge(x1_ready, min(2 * t + 3, 2 * NT))
                    if t:
                        act.wait_ge(st_sq2, t)
                    act.activation(square2, x1[:, t, :], ACT.Square, accum_out=ssq[:, t:t + 1]).then_inc(st_sq2, 1)
                elif e[0] == "R":
                    t = e[1]
                    act.wait_ge(pe_h2, t + 1)
                    for i in range(2):
                        ins = act.copy(h2T[:, 4 * i:4 * i + 4, t * P:(t + 1) * P], B(5 + i).rearrange("p (k n) -> p k n", k=4))
                    ins.then_inc(h2_read, 1)
                elif e[0] == "cv":
                    i = e[1]
                    act.wait_ge(ld_w[i % 2], 16 * (i // 2 + 1))
                    act.copy(w_hi[i % 2][:], w_raw[i % 2]).then_inc(w_rounded, 1)
                elif e[0] == "RT":
                    i = RET.index(e[1])
                    act.wait_ge(pe_rt, i + 1)
                    if i == 0:
                        act.wait_ge(mod_cols, 3)
                        act.wait_ge(st_mod, 16 * 8)
                    else:
                        act.wait_ge(pe_sc, i)
                        if i > 1:
                            act.wait_ge(q_scaled, i - 1)
                    act.copy(rqT, B(2))
                    act.copy(rkT, B(3)).then_inc(rt_read, 1)
                elif e[0] == "O":
                    i = RET.index(e[1])
                    act.wait_ge(pe_o, i + 1)
                    act.copy(ret[:, e[1], 0:N512], B(5))
                    act.copy(ret[:, e[1], N512:D], B(6)).then_inc(o_read, 1)
                elif e[0] == "S":
                    s = e[1]
                    h, t = steps[s]
                    n = KEYS if t < PT else P
                    act.wait_ge(max_ready, s + 1)
                    if s:
                        act.wait_ge(mixed_ready, s)
                    for c in range(2):
                        act.activation(probs[:, c, 0:n], score[c][:, 0:n], ACT.Exp, bias=neg_mx[:, s % 2, c:c + 1],
                                       scale=DH ** -0.5, accum_out=den[:, s % 2, c:c + 1]).then_inc(exp_done, 1)
                elif e[0] == "AT":
                    s = e[1]
                    act.wait_ge(pe_at, s + 1)
                    if steps[s][1] < PT:
                        act.copy(mixedT[s % 2][:, 0:N512], B(5))
                        act.copy(mixedT[s % 2][:, N512:KEYS], B(6)[:, 0:CTX]).then_inc(at_read, 1)
                    else:
                        act.copy(mixedT[s % 2][:, 0:P], B(5)[:, 0:P]).then_inc(at_read, 1)
                elif e[0] == "PV":
                    s = e[1]
                    h, t = steps[s]
                    act.wait_ge(pe_pv, s + 1)
                    if s == 0:
                        act.wait_ge(pe_o, NT)
                    scale_copy(od[:, t, h * P:(h + 1) * P], B(7)[:, 0:P], rden[:, s % 2, 0:1])
                    act.activation(B(7)[:, P:2 * P], B(7)[:, 0:P], ACT.Square, scale=rden[:, s % 2, 0:1],
                                   accum_out=od_ss[:, t, h:h + 1]).then_inc(pv_read, 1)

            act.wait_ge(route_d, 1)
            act.activation(g_diff, g_diff, ACT.Exp).then_inc(route_a, 1)
            act.wait_ge(route_d, 2)
            act.activation(e_x, e_x, ACT.Exp).then_inc(route_a, 1)

            def pair(p, par):
                act.wait_ge(pe_xt, p + 1)
                for i in range(2):
                    ins = act.copy(xgT[par][:, 4 * i:4 * i + 4, :], B(i).rearrange("p (k n) -> p k n", k=4))
                ins.then_inc(xt_read, 1)

            def pair_gate(p, par):
                act.wait_ge(pe_gu, p + 1)
                act.activation(act_t[:, par, :], B(2 + par)[:, 0:FF], ACT.Tanh, scale=0.5).then_inc(gu_tanh, 1)

            def pair_hidden(p, par):
                act.wait_ge(pe_aT, p + 1)
                act.copy(act_aT[par], B(4)[:, 0:2 * P].rearrange("p (k n) -> p k n", k=2)).then_inc(aT_read, 1)

            def pair_rows(p, par, turn, first=False):
                act.wait_ge(pe_dn, p + 1)
                if not first:
                    act.wait_ge(st_y[par], 16 * turn)
                act.copy(y_out[:, par, 0:N512], B(5)).then_inc(y_a, 1)

            def whole(p, par, turn, first=False, last=False):
                pair_gate(p, par)
                if not last:
                    pair(p + 1, 1 - par)
                pair_hidden(p, par)
                pair_rows(p, par, turn, first=first)

            pair(0, 0)
            whole(0, 0, 0, first=True)
            whole(1, 1, 0, first=True)
            with act.Fori(1, PAIRS // 2 - 1) as i:
                for par in range(2):
                    whole(2 * i + par, par, i)
            h = PAIRS // 2 - 1
            whole(2 * h, 0, h)
            whole(2 * h + 1, 1, h, last=True)
            n_over = act.value_load(n_ov[0:1, 0:1], min_val=0, max_val=OVER)
            act.wait_ge(st_y[0], 16 * PAIRS // 2)
            act.wait_ge(st_y[1], 16 * PAIRS // 2)
            with act.If(n_over > 0):
                with act.Fori(0, OVER // 2) as j:
                    with act.If(n_over > 2 * j):
                        act.wait_ge(ov_xt, j + 1)
                        for i in range(2):
                            ins = act.copy(xgT[0][:, 4 * i:4 * i + 4, :], B(i).rearrange("p (k n) -> p k n", k=4))
                        ins.then_inc(ov_xr, 1)
                        act.wait_ge(ov_gu, j + 1)
                        act.activation(act_t[:, 0, :], B(2)[:, 0:FF], ACT.Tanh, scale=0.5).then_inc(ov_tanh, 1)
                        act.wait_ge(ov_aT, j + 1)
                        act.copy(act_aT[0], B(4)[:, 0:2 * P].rearrange("p (k n) -> p k n", k=2)).then_inc(ov_ar, 1)
                        act.wait_ge(ov_dn, j + 1)
                        act.copy(y_out[:, 0, 0:N512], B(5)).then_inc(ov_ya, 1)
                    with act.Else():
                        act.nop()
            with act.Else():
                act.nop()
            def first_rows(t):
                act.wait_ge(ld_y[t], 32)
                act.activation(y1[:, t, :], y1[:, t, :], ACT.Copy, scale=w_tok[:, 0, t:t + 1]).then_inc(y_scaled, 1)

            first_rows(0)
            for t in range(NT):
                if t + 1 < NT:
                    first_rows(t + 1)
                act.wait_ge(y_used, t + 1)
                act.activation(y1[:, t, :], x1[:, t, :], ACT.Square, accum_out=ssq[:, t:t + 1]).then_inc(fin_sq, 1)

        @block.vector
        def _(dve):
            chain = [0]

            def link(ins):
                chain[0] += 1
                ins.then_inc(dve_chain, 1)
                dve.wait_ge(dve_chain, chain[0])

            n_set = [0]

            def setp(ins):
                n_set[0] += 1
                ins.then_inc(dve_set, 1)
                dve.wait_ge(dve_set, n_set[0])

            dve.memset(ccol, 0.0)
            dve.memset(neg_half[:], -0.5)
            dve.wait_ge(act_set, 1)
            setp(dve.scalar_tensor_tensor(out=rows[0:16, :], in0=rows_t[0:16, :], scalar=1.0, in1=rows[0:16, :],
                                          op0=ALU.add, op1=ALU.mult))
            dve.wait_ge(pe_set, 1)
            link(dve.tensor_copy(cols[:], B(7)[:, 16:41]))
            link(dve.tensor_scalar(cols[:, 16:24], cols[:, 16:24], 0.5, None, ALU.mult))
            link(dve.tensor_scalar(cols[:, 24:25], cols[:, 24:25], 0.8, None, ALU.mult))
            setp(dve.tensor_scalar(ccol[:, :, 0:2], B(7)[:, 0:16].rearrange("p (s k) -> p k s", s=2), 0.5, None, ALU.mult))
            setp(dve.scalar_tensor_tensor(out=dec_n[:], in0=dec[:], scalar=-1.0, in1=dec[:], op0=ALU.mult, op1=ALU.max))
            dve.wait_ge(act_set, 2)
            setp(dve.tensor_scalar(dec_n[:], dec_e[:], 1.0, None, ALU.add))
            link(dve.tensor_scalar(dec[:], dec[:], 0.0, None, ALU.min))
            dve.wait_ge(act_set, 3)
            link(dve.tensor_tensor(lg[:], dec[:], dec_e[:], ALU.subtract))
            dve.wait_ge(ld_const, 32)
            link(dve.tensor_scalar(dec_n[:, 0:4], lg[:, 0:4], C("kpos")[:, 0:1], None, ALU.mult))
            link(dve.tensor_scalar(dec_n[:, 4:8], lg[:, 4:8], C("kpos")[:, 1:2], None, ALU.mult))
            link(dve.tensor_tensor_reduce(lam_in[:, 0, :], lam_in[:, 0, :], lam_in[:, 1, :], 1.0, 0.0, ALU.mult, ALU.add, lam_s[:, 0:1]))
            setp(dve.tensor_tensor_reduce(lam_in[:, 2, :], lam_in[:, 2, :], lam_in[:, 3, :], 1.0, 0.0, ALU.mult, ALU.add, lam_s[:, 1:2]))
            dve.wait_ge(rstd_ready, 1)
            for t in range(NT):
                dve.tensor_scalar(xn[:, t, :], xn[:, t, :], rstd[:, t:t + 1], None, ALU.mult).then_inc(xn_ready, 1)
            dve.wait_ge(act_set, 4)
            link(dve.tensor_tensor(decay_e[:, 0:4, :], decay_e[:, 0:4, :], C("on_f").unsqueeze(1).to_broadcast([P, 4, P]), ALU.mult))
            link(dve.tensor_tensor(decay_e[:, 4:8, :], decay_e[:, 4:8, :], C("on_b").unsqueeze(1).to_broadcast([P, 4, P]), ALU.mult))
            link(dve.tensor_scalar(kd[:], kd[:], RK ** -0.5, None, ALU.mult))
            link(dve.tensor_tensor(neg_lam[:], lam_s[:, 1:2], lam_s[:, 0:1], ALU.subtract))
            link(dve.tensor_scalar(neg_lam[:], neg_lam[:], 0.2, None, ALU.subtract))
            setp(dve.tensor_tensor(ret_mask[:], decay_e[:, 0:4, :], decay_e[:, 4:8, :], ALU.add))

            def ada_rows_out(r):
                dve.wait_ge(pe_ada, (r + 1) * KC)
                if r == 0:
                    dve.wait_ge(ld_small, 16 * 16)
                dve.tensor_tensor(mod_rows[:, r, :], B(7), bias_rows[:, r, :], ALU.add).then_inc(ada_rows, 1)
                dve.wait_ge(pe_modT, r + 1)
                dst = modc[:, 16 * r:16 * r + 16, :].rearrange("p (j m) s -> p m j s", m=4)
                src = B(2).rearrange("p (m j x) -> p m j x", m=4, j=4)[:, :, :, 0:2]
                dve.tensor_copy(dst, src).then_inc(mod_cols, 1)

            ada_rows_out(0)
            dve.wait_ge(mod_cols, 1)
            link(dve.tensor_scalar(mul1[:], modc[:, 8:16, :], 1.0, None, ALU.add))
            setp(dve.tensor_tensor(mul1[:], mul1[:], cols[:, 0:8].unsqueeze(2).to_broadcast([P, KC, 2]), ALU.mult))

            n_rope, n_merged, n_out = [0], [0], [0]

            def dense_item(n):
                item = dense[n]
                src = B(n % 2)
                if item[0] == "T4":
                    if freed[n][0] != "D":
                        return
                    _, what, t, half = item
                    dve.wait_ge(pe_dense, n + 1)
                    s = 1 if t == PT else 0
                    if what in ("h", "o"):
                        for k in range(4):
                            kk = 4 * half + k
                            if what == "h":
                                ins = dve.tensor_scalar(h_full[:, kk, t * P:(t + 1) * P], src[:, k * P:(k + 1) * P],
                                                        mul1[:, kk, s:s + 1], modc[:, kk, s:s + 1], ALU.mult, ALU.add)
                            else:
                                ins = dve.tensor_scalar(oT[:, kk, t * P:(t + 1) * P], src[:, k * P:(k + 1) * P],
                                                        cols[:, 16 + kk:17 + kk], None, ALU.mult)
                    else:
                        dst = odT if what == "od" else mT
                        if what == "od" and t == 0:
                            wait_freed(dve, where[("mm", "wr1", PT)])
                        ins = dve.tensor_scalar(dst[:, 4 * half:4 * half + 4, t * P:(t + 1) * P],
                                                src.rearrange("p (k n) -> p k n", k=4),
                                                cols[:, 24:25] if what == "od" else 0.5, None, ALU.mult)
                    free(ins, n)
                    return
                _, s, t, hh = item
                kind = s[:2]
                c0 = N512 * int(s[2]) if len(s) > 2 else 0
                if kind in ("dq", "dk") and t < PT and hh == 1:
                    wait_freed(dve, n)
                    x = (dq if kind == "dq" else dk)[:, t, :].rearrange("p (g a i f) -> p g a i f", g=8, a=2, i=2)
                    cs = [C(k)[:, 32 * t:32 * t + 32].rearrange("p (a f) -> p a f", a=2).unsqueeze(1).to_broadcast([P, 8, 2, 16])
                          for k in ("cos", "sin")]
                    tmp = [rope_t[:, i, :].rearrange("p (g a f) -> p g a f", g=8, a=2) for i in range(4)]
                    if n_rope[0]:
                        dve.wait_ge(rope_done, n_rope[0])
                    n_rope[0] += 1
                    for i in range(4):
                        ins = dve.tensor_tensor(tmp[i], x[:, :, :, i // 2, :], cs[i % 2], ALU.mult)
                    link(ins)
                    dve.tensor_tensor(x[:, :, :, 0, :], tmp[0], tmp[3], ALU.subtract)
                    ins = dve.tensor_tensor(x[:, :, :, 1, :], tmp[1], tmp[2], ALU.add)
                    ins.then_inc(rope_done, 1)
                elif kind == "rg":
                    u = gate_at[item[1:]]
                    c0 += N256 * hh
                    dve.wait_ge(tanh_done, u)
                    if u == 1:
                        dve.wait_ge(o_normed, NT)
                    free(dve.scalar_tensor_tensor(out=gate_p[:, u % 2, :], in0=gate_t[:, (u - 1) % 2, :], scalar=1.0,
                                                  in1=src[:, 0:N256], op0=ALU.add, op1=ALU.mult), n)
                    wait_freed(dve, n)
                    dve.tensor_tensor(ret[:, t, c0:c0 + N256], ret[:, t, c0:c0 + N256], gate_p[:, u % 2, :],
                                      ALU.mult).then_inc(gate_done, 1)
                elif kind == "wr":
                    dve.wait_ge(pe_dense, n + 1)
                    dve.wait_ge(ld_gr, 16)
                    free(dve.scalar_tensor_tensor(out=merge[:, t, c0:c0 + N512], in0=gr_t[:, t, c0:c0 + N512], scalar=1.0,
                                                  in1=src, op0=ALU.add, op1=ALU.mult), n)
                elif kind == "wd":
                    dve.wait_ge(pe_dense, n + 1)
                    dve.wait_ge(ld_gd, 16)
                    m = merge_t[:, n % 2, :]
                    if n_merged[0]:
                        dve.wait_ge(merged, n_merged[0])
                    n_merged[0] += 1
                    free(dve.scalar_tensor_tensor(out=m, in0=gd_t[:, t, c0:c0 + N512], scalar=1.0, in1=src,
                                                  op0=ALU.add, op1=ALU.mult), n)
                    wait_freed(dve, n)
                    dve.tensor_tensor(merge[:, t, c0:c0 + N512], merge[:, t, c0:c0 + N512], m, ALU.add).then_inc(merged, 1)
                elif kind == "wo":
                    dve.wait_ge(pe_dense, n + 1)
                    dve.wait_ge(ld_x1, 16 * NT)
                    dve.wait_ge(ld_g1, 32)
                    m = merge_t[:, n % 2, :]
                    if n_out[0]:
                        dve.wait_ge(x1_ready, n_out[0])
                    n_out[0] += 1
                    free(dve.tensor_tensor(m, src, g1_rows[:, 1 if t == PT else 0, c0:c0 + N512], ALU.mult), n)
                    wait_freed(dve, n)
                    dve.tensor_tensor(x1[:, t, c0:c0 + N512], x1[:, t, c0:c0 + N512], m, ALU.add).then_inc(x1_ready, 1)

            def low_part(n):
                _, _, t, half = dense[n]
                dve.wait_ge(h_rounded, 2 * t + half + 1)
                at_ = (slice(None), slice(4 * half, 4 * half + 4), slice(t * P, (t + 1) * P))
                dve.tensor_tensor(h_lo[at_], h_full[at_], h_hi[at_].bitcast(F32), ALU.subtract).then_inc(h_split, 1)

            def router_input(t):
                if t == 0:
                    dve.wait_ge(ld_route, 16 * 6)
                    dve.wait_ge(ld_row2, 16 * 4)
                    for i in range(2):
                        ins = dve.scalar_tensor_tensor(out=scale2[:, i, :], in0=scale2[:, i, :], scalar=1.0, in1=n2_row,
                                                       op0=ALU.add, op1=ALU.mult)
                    link(ins)
                i = 1 if t == PT else 0
                dve.wait_ge(pool2, t + 1)
                if t >= 2:
                    dve.wait_ge(pe_h2, t - 1)
                    dve.wait_ge(st_h2[t % 2], 16 * (t // 2))
                link(dve.scalar_tensor_tensor(out=h2[:, t % 2, :], in0=x1[:, t, :], scalar=rstd[:, t:t + 1], in1=scale2[:, i, :],
                                              op0=ALU.mult, op1=ALU.mult))
                dve.tensor_tensor(h2[:, t % 2, :], h2[:, t % 2, :], shift2[:, i, :], ALU.add).then_inc(h2_ready, 1)

            n_read = 0
            for e in plan:
                if e[0] == "dense":
                    dense_item(e[1])
                    if dense[e[1]][:2] == ("T4", "h"):
                        low_part(e[1])
                elif e[0] == "N":
                    router_input(e[1])
                elif e[0] == "cv":
                    i = e[1]
                    dve.wait_ge(w_rounded, i + 1)
                    dve.tensor_tensor(w_lo[i % 2][:], w_raw[i % 2], w_hi[i % 2][:].bitcast(F32), ALU.subtract).then_inc(w_split, 1)
                elif e[0] == "ada":
                    if e[2] == KC - 1:
                        ada_rows_out(e[1])
                elif e[0] == "U":
                    _, u, half, b = e
                    dirn, t = UPDATES[u]
                    n_read += 1
                    dve.wait_ge(pe_u, n_read)
                    if n_read == 1:
                        dve.wait_ge(ld_state, 32)
                    if t == PT:
                        i = 0 if dirn == "f" else 1
                        if i == 0 and half == 0:
                            dve.wait_ge(st_mod, 16 * 8)
                        dve.tensor_copy(state_out[:, i, half * N512:(half + 1) * N512], B(b)).then_inc(u_read, 1)
                    else:
                        for i in range(2):
                            h = 2 * half + i
                            old = state_f if dirn == "f" else states_b[:, t, :]
                            new = state_f if dirn == "f" else states_b[:, t - 1, :]
                            dcol = h if dirn == "f" else 4 + h
                            ins = dve.scalar_tensor_tensor(out=new[:, h * RV:(h + 1) * RV], in0=old[:, h * RV:(h + 1) * RV],
                                                           scalar=cd[:, dcol:dcol + 1], in1=B(b)[:, i * RV:(i + 1) * RV],
                                                           op0=ALU.mult, op1=ALU.add)
                        ins.then_inc(u_read, 1)
                        dve.wait_ge(u_read, n_read)
                elif e[0] == "SC":
                    i = RET.index(e[1])
                    dve.wait_ge(pe_sc, i + 1)
                    if i:
                        dve.wait_ge(pe_o, i)
                    dve.tensor_tensor(sm.rearrange("p (h n) -> p h n", h=RH), B(4).rearrange("p (h n) -> p h n", h=RH),
                                      ret_mask[:], ALU.mult).then_inc(sc_masked, 1)
                elif e[0] == "O":
                    t = e[1]
                    i = RET.index(t)
                    dve.wait_ge(o_read, i + 1)
                    if i:
                        dve.wait_ge(o_normed, i)
                    for h in range(RH):
                        ins = dve.bn_stats(bn_s[:, h, :], ret[:, t, h * RV:(h + 1) * RV])
                    link(ins)
                    for h in range(RH):
                        ins = dve.bn_aggr(bn_a[:, h, :], bn_s[:, h, :])
                    link(ins)
                    dve.tensor_scalar(var_e[:], bn_a[:, :, 1], EPS, None, ALU.add).then_inc(o_stats, 1)
                    dve.wait_ge(o_rstd, i + 1)
                    for h in range(RH):
                        ins = dve.tensor_scalar(ret[:, t, h * RV:(h + 1) * RV], ret[:, t, h * RV:(h + 1) * RV],
                                                bn_a[:, h, 0:1], ret_rstd[:, h:h + 1], ALU.subtract, ALU.mult)
                    ins.then_inc(o_normed, 1)
                elif e[0] == "ret_end":
                    dve.wait_ge(pe_o, NT)
                    dve.wait_ge(st_ret, 32)
                    for i in range(2):
                        dve.memset(qz[i][DH:P, 0, :], 0.0)
                        dve.memset(qz[i][0:DH, 1, :], 0.0)
                        dve.memset(qzp[i][DH:P, 0, :], 0.0)
                        ins = dve.memset(qzp[i][0:DH, 1, :], 0.0)
                    setp(ins)
                elif e[0] == "S":
                    s = e[1]
                    h, t = steps[s]
                    n = KEYS if t < PT else P
                    dve.wait_ge(pe_scores, s + 1)
                    dve.tensor_reduce(mx[:, 0:1], score[0][:, 0:n], AXX, ALU.max)
                    link(dve.tensor_reduce(mx[:, 1:2], score[1][:, 0:n], AXX, ALU.max))
                    dve.tensor_scalar(neg_mx[:, s % 2, :], mx[:], -DH ** -0.5, None, ALU.mult).then_inc(max_ready, 1)
                    dve.wait_ge(exp_done, 2 * s + 2)
                    if s >= 2:
                        dve.wait_ge(pv_read, s - 1)
                    link(dve.reciprocal(rden[:, s % 2, :], den[:, s % 2, :]))
                    link(dve.scalar_tensor_tensor(out=coef[:, s % 2:s % 2 + 1], in0=rden[:, s % 2, 1:2], scalar=neg_lam[:],
                                                  in1=den[:, s % 2, 0:1], op0=ALU.mult, op1=ALU.mult))
                    if s:
                        dve.wait_ge(pe_at, s)
                    if t < PT:
                        dve.scalar_tensor_tensor(out=mixed, in0=probs[:, 1, :], scalar=coef[:, s % 2:s % 2 + 1],
                                                 in1=probs[:, 0, :], op0=ALU.mult, op1=ALU.add).then_inc(mixed_ready, 1)
                    else:
                        dve.scalar_tensor_tensor(out=mixed[:, 0:P], in0=probs[:, 1, 0:P], scalar=coef[:, s % 2:s % 2 + 1],
                                                 in1=probs[:, 0, 0:P], op0=ALU.mult, op1=ALU.add).then_inc(mixed_ready, 1)

            def ramp_row(ap, lead=NE):
                return ap.unsqueeze(1).to_broadcast([P, lead, ap.shape[1]])

            def over_last(ap, n):
                return ap.unsqueeze(2).to_broadcast([P, ap.shape[1], n])

            def ramp(name, lead):
                r = R(name)
                return r.unsqueeze(1).to_broadcast([P, lead, r.shape[1]])

            dve.wait_ge(pe_logits, NT)
            link(dve.tensor_tensor(logits, B(2)[:, 0:NT * 36].rearrange("p (t n) -> p t n", t=NT),
                                   rb.unsqueeze(1).to_broadcast([P, NT, 36]), ALU.add))
            lgrp = logits[:, :, 0:GRP]
            link(dve.tensor_reduce(g_max, lgrp, AXX, ALU.max))
            dve.tensor_tensor(g_diff, lgrp, over_last(g_max, GRP), ALU.subtract).then_inc(route_d, 1)

            def first_hit(eq, values, top, idx, onehot, ramp_n):
                n = ramp_n
                rr = R("ramp32")[:, 0:n].unsqueeze(1).to_broadcast([P, NT, n])
                link(dve.tensor_tensor(eq, values, over_last(top, n), ALU.is_equal))
                link(dve.scalar_tensor_tensor(out=eq, in0=eq, scalar=-100.0, in1=rr, op0=ALU.mult, op1=ALU.add))
                link(dve.tensor_reduce(idx, eq, AXX, ALU.min))
                link(dve.tensor_scalar(idx, idx, 100.0, None, ALU.add))
                link(dve.tensor_tensor(onehot, rr, over_last(idx, n), ALU.is_equal))

            first_hit(g_eq, lgrp, g_max, g_idx, g_hot, GRP)
            link(dve.tensor_scalar(g_hot, g_hot, BIG, BIG, ALU.mult, ALU.subtract))
            link(dve.tensor_tensor(e_m.rearrange("p t (g e) -> p t g e", g=GRP), logits[:, :, GRP:36].rearrange("p t (g e) -> p t g e", g=GRP),
                                   g_hot.unsqueeze(3).to_broadcast([P, NT, GRP, EPG]), ALU.add))
            for k in range(2):
                link(dve.tensor_reduce(e_max[:, k, :], e_m, AXX, ALU.max))
                first_hit(e_eq, e_m, e_max[:, k, :], e_idx[:, k, :], hot[:, k, :, :], NE)
                if k == 0:
                    link(dve.scalar_tensor_tensor(out=e_m, in0=hot[:, 0, :, :], scalar=-2 * BIG, in1=e_m, op0=ALU.mult, op1=ALU.add))
            dve.tensor_tensor(e_x, e_max[:, 1, :], e_max[:, 0, :], ALU.subtract).then_inc(route_d, 1)
            dve.tensor_tensor(e_any, hot[:, 0, :, :], hot[:, 1, :, :], ALU.add).then_inc(route_d, 1)
            dve.wait_ge(route_a, 2)
            link(dve.tensor_reduce(g_sum, g_diff, AXX, ALU.add))
            link(dve.tensor_scalar(e_den, e_x, 1.0, None, ALU.add))
            link(dve.tensor_tensor(e_den, e_den, g_sum, ALU.mult))
            link(dve.reciprocal(w_tok[:, 0, :], e_den))
            link(dve.tensor_tensor(w_tok[:, 1, :], w_tok[:, 0, :], e_x, ALU.mult))
            cnt, cnt_next = cnt_a, cnt_b
            dve.wait_ge(pe_rank, 1)
            link(dve.tensor_copy(rank_m.rearrange("p t n -> p (t n)"), B(3)[:, 0:NT * NE]))
            link(dve.tensor_copy(cnt, B(4)[:, 0:NE]))
            for t in range(1, NT):
                dve.tensor_tensor(rank_m[:, t, :], rank_m[:, t, :], cnt, ALU.add)
                link(dve.tensor_tensor(cnt_next, cnt, B(4)[:, t * NE:(t + 1) * NE], ALU.add))
                cnt, cnt_next = cnt_next, cnt
            link(dve.tensor_tensor(cmp9, over_last(cnt, 9), ramp("x64", NE), ALU.is_gt))
            link(dve.tensor_reduce(over, cmp9, AXX, ALU.add))
            link(dve.tensor_tensor(low_p, ramp_row(over), R("lower").rearrange("p (e f) -> p e f", e=NE), ALU.mult))
            link(dve.tensor_reduce(over_at, low_p, AXX, ALU.add))
            link(dve.tensor_tensor(over_end, over_at, over, ALU.add))

            def pick(dst, table):
                for k in range(2):
                    ins = dve.tensor_tensor(prod[:, k, :, :], hot[:, k, :, :], table, ALU.mult)
                link(ins)
                link(dve.tensor_reduce(dst.rearrange("p (k t) -> p k t", k=2), prod, AXX, ALU.add))

            pick(rk_s, rank_m)
            pick(ob_s, over_at.unsqueeze(1).to_broadcast([P, NT, NE]))
            link(dve.tensor_tensor(cmp_r, over_last(rk_s, 9), ramp("x64", 2 * NT), ALU.is_ge))
            link(dve.tensor_reduce(qq, cmp_r, AXX, ALU.add))
            link(dve.tensor_scalar(has, qq, 1.0, None, ALU.min))
            ei = e_idx.rearrange("p k t -> p (k t)")
            link(dve.tensor_tensor(ob_s, ob_s, qq, ALU.add))
            link(dve.tensor_tensor(ob_s, ob_s, ei, ALU.subtract))
            link(dve.scalar_tensor_tensor(out=ob_s, in0=ob_s, scalar=NE - 1.0, in1=has, op0=ALU.add, op1=ALU.mult))
            link(dve.tensor_tensor(ob_s, ob_s, ei, ALU.add))
            link(dve.tensor_tensor(ob_s, ob_s, qq, ALU.subtract))
            link(dve.scalar_tensor_tensor(out=slot, in0=ob_s, scalar=float(BLK), in1=rk_s, op0=ALU.mult, op1=ALU.add))
            link(dve.tensor_copy(y_idx[:], slot))
            link(dve.tensor_tensor(cmp_p, over_last(slot, NPAIR - 1), ramp("x128", 2 * NT), ALU.is_ge))
            link(dve.tensor_reduce(pair_i, cmp_p, AXX, ALU.add))
            link(dve.scalar_tensor_tensor(out=pos_i, in0=pair_i, scalar=-float(P), in1=slot, op0=ALU.mult, op1=ALU.add))
            link(dve.tensor_tensor(hot_pos, over_last(pos_i, P), ramp("ramp128", 2 * NT), ALU.is_equal))
            link(dve.tensor_tensor(val_pair, over_last(pair_i, NPAIR), ramp("ramp26", 2 * NT), ALU.is_equal))
            for k in range(2):
                ins = dve.tensor_tensor(val_pair[:, k * NT:(k + 1) * NT, :], val_pair[:, k * NT:(k + 1) * NT, :],
                                        over_last(R("token"), NPAIR), ALU.mult)
            ins.then_inc(route_d, 1)
            link(dve.tensor_tensor(ov_cmp, ramp_row(over_end, OVER), over_last(R("ramp20"), NE), ALU.is_le))
            link(dve.tensor_reduce(ov_f, ov_cmp, AXX, ALU.add))
            link(dve.tensor_scalar(ov_f, ov_f, NE - 1.0, None, ALU.min))
            link(dve.tensor_copy(ov_exp[:], ov_f))
            link(dve.tensor_copy(n_ov[:], over_end[:, NE - 1:NE]))
            dve.wait_ge(pe_table, 1)
            dve.tensor_copy(row_idx[:], B(5)[:, 0:NPAIR]).then_inc(idx_ready, 1)

            def silu_up(src, par, wait, done):
                ins = dve.scalar_tensor_tensor(out=act_s[:, par, :], in0=act_t[:, par, :], scalar=1.0, in1=src[:, 0:FF],
                                               op0=ALU.add, op1=ALU.mult)
                ins.then_inc(wait[0], 1)
                dve.wait_ge(wait[0], wait[1])
                dve.scalar_tensor_tensor(out=act_a[:, par, :], in0=act_s[:, par, :], scalar=0.5, in1=src[:, FF:2 * FF],
                                         op0=ALU.mult, op1=ALU.mult).then_inc(done, 1)

            def pair_rows(p, par, turn, first=False):
                dve.wait_ge(pe_dn, p + 1)
                if not first:
                    dve.wait_ge(st_y[par], 16 * turn)
                dve.tensor_copy(y_out[:, par, N512:D], B(6)).then_inc(y_d, 1)

            def pair(p, par, turn, first=False):
                dve.wait_ge(gu_tanh, p + 1)
                silu_up(B(2 + par), par, (gu_half, p + 1), gu_act)
                pair_rows(p, par, turn, first=first)

            pair(0, 0, 0, first=True)
            pair(1, 1, 0, first=True)
            with dve.Fori(1, PAIRS // 2) as i:
                for par in range(2):
                    pair(2 * i + par, par, i)
            n_over = dve.value_load(n_ov[0:1, 0:1], min_val=0, max_val=OVER)
            dve.wait_ge(st_y[0], 16 * PAIRS // 2)
            dve.wait_ge(st_y[1], 16 * PAIRS // 2)
            with dve.If(n_over > 0):
                with dve.Fori(0, OVER // 2) as j:
                    with dve.If(n_over > 2 * j):
                        dve.wait_ge(ov_free, j + 1)
                        dve.tensor_copy(idx_now[:], row_idx[:, bass.ds(j + PAIRS, 1)]).then_inc(ov_idx, 1)
                        dve.wait_ge(ov_tanh, j + 1)
                        silu_up(B(2), 0, (ov_half, j + 1), ov_act)
                        dve.wait_ge(ov_dn, j + 1)
                        dve.tensor_copy(y_out[:, 0, N512:D], B(6)).then_inc(ov_yd, 1)
                    with dve.Else():
                        dve.nop()
            with dve.Else():
                dve.nop()
            def last(t):
                dve.wait_ge(fin_rstd, t + 1)
                if t >= 2:
                    dve.wait_ge(st_fin[t % 2], 16 * (t // 2))
                dve.scalar_tensor_tensor(out=fin_t[:, t % 2, :], in0=x1[:, t, :], scalar=rstd[:, t:t + 1], in1=fin_row,
                                         op0=ALU.mult, op1=ALU.mult).then_inc(fin_ready, 1)

            dve.wait_ge(ld_fin, 16 * 3)
            for t in range(NT):
                i = 1 if t == PT else 0
                acc = y1[:, t, :]
                dve.wait_ge(y_scaled, t + 1)
                link(dve.scalar_tensor_tensor(out=acc, in0=y2[:, t, :], scalar=w_tok[:, 1, t:t + 1], in1=acc, op0=ALU.mult, op1=ALU.add))
                link(dve.tensor_tensor(acc, acc, g2_rows[:, i, :], ALU.mult))
                dve.tensor_tensor(x1[:, t, :], x1[:, t, :], acc, ALU.add).then_inc(y_used, 1)
                if t:
                    last(t - 1)
                if t == NT - 1:
                    last(t)

        @block.gpsimd
        def _(pool):
            chain = [0]

            def link(ins):
                chain[0] += 1
                ins.then_inc(pool_chain, 1)
                pool.wait_ge(pool_chain, chain[0])

            pool.wait_ge(ssq_ready, NT)
            link(pool.tensor_scalar(msq[:], ssq[:], 1.0 / D, EPS, ALU.mult, ALU.add))
            pool.wait_ge(dve_set, 1)
            pool.tensor_tensor(rstd[:], msq[:], neg_half[:, 0:NT], ALU.pow).then_inc(rstd_ready, 1)

            def keys(u):
                dirn, t = UPDATES[u]
                if u == 0:
                    pool.wait_ge(dve_set, 6)
                    pool.wait_ge(mod_cols, 3)
                    pool.wait_ge(st_mod, 16 * 8)
                wait_freed(pool, where[("mm", "rv1", PT)])
                if u >= 2:
                    pool.wait_ge(pe_u, 2 * (u - 1))
                k0 = 0 if dirn == "f" else 4
                pool.tensor_tensor(ks[:, u % 2, :].rearrange("p (h n) -> p h n", h=RH), rk[:, t, :].rearrange("p (h n) -> p h n", h=RH),
                                   kd[:, k0:k0 + 4].unsqueeze(2).to_broadcast([P, RH, P]), ALU.mult).then_inc(u_keys, 1)

            seen = set()
            for e in plan:
                if e[0] == "U" and e[2] == 0:
                    if e[1] == 0:
                        keys(0)
                        keys(1)
                    elif e[1] + 1 < len(UPDATES):
                        keys(e[1] + 1)
                elif e[0] == "RT":
                    t = e[1]
                    i = RET.index(t)
                    if t != PT:
                        pool.wait_ge(rt_read, i + 1)
                        if i > 1:
                            pool.wait_ge(pe_o, i)
                        pool.tensor_tensor(qf, rqT, q_dec[:, 0:4, :].rearrange("p h n -> p (h n)"), ALU.mult)
                        pool.tensor_tensor(qb, rqT, q_dec[:, 4:8, :].rearrange("p h n -> p (h n)"), ALU.mult).then_inc(q_scaled, 1)
                elif e[0] == "O":
                    i = RET.index(e[1])
                    pool.wait_ge(o_stats, i + 1)
                    pool.tensor_tensor(ret_rstd[:], var_e[:], neg_half[:, 0:RH], ALU.pow).then_inc(o_rstd, 1)
                elif e[0] == "att_end":
                    pool.wait_ge(pv_read, len(steps))
                    link(pool.tensor_scalar(od_ss[:], od_ss[:], 1.0 / P, EPS, ALU.mult, ALU.add))
                    link(pool.tensor_tensor(od_rstd[:].rearrange("p t h -> p (t h)"), od_ss[:].rearrange("p t h -> p (t h)"),
                                            neg_half[:, 0:NT * AH], ALU.pow))
                    for t in range(NT):
                        pool.tensor_tensor(od[:, t, :].rearrange("p (h n) -> p h n", h=AH), od[:, t, :].rearrange("p (h n) -> p h n", h=AH),
                                           od_rstd[:, t, :].unsqueeze(2).to_broadcast([P, AH, P]), ALU.mult).then_inc(od_scaled, 1)

            def inverse_root(t, done):
                link(pool.tensor_scalar(msq[:, t:t + 1], ssq[:, t:t + 1], 1.0 / D, EPS, ALU.mult, ALU.add))
                pool.tensor_tensor(rstd[:, t:t + 1], msq[:, t:t + 1], neg_half[:, 0:1], ALU.pow).then_inc(done, 1)

            for t in range(NT):
                pool.wait_ge(st_sq2, t + 1)
                inverse_root(t, pool2)
            pool.wait_ge(idx_ready, 1)
            pool.wait_ge(st_h2[0], 16 * 3)
            pool.wait_ge(st_h2[1], 16 * 2)
            for p in range(PAIRS):
                if p >= 2:
                    pool.wait_ge(pe_xt, p - 1)
                pool.indirect_dma_start(xg[:, p % 2, :], None, h2_dram, bass.IndirectOffsetOnAxis(ap=row_idx[:, p:p + 1], axis=0)).then_inc(ld_xg[p % 2], 16)
            pool.sem_inc(ov_free, 1)
            pool.wait_ge(pe_xt, PAIRS)
            n_over = pool.value_load(n_ov[0:1, 0:1], min_val=0, max_val=OVER)
            with pool.If(n_over > 0):
                with pool.Fori(0, OVER // 2) as j:
                    with pool.If(n_over > 2 * j):
                        pool.wait_ge(ov_idx, j + 1)
                        pool.sem_inc(ov_take, 1)
                        pool.indirect_dma_start(xg[:, 0, :], None, h2_dram, bass.IndirectOffsetOnAxis(ap=idx_now[:], axis=0)).then_inc(ov_x, 16)
                    with pool.Else():
                        pool.nop()
            with pool.Else():
                pool.nop()
            pool.wait_ge(ov_over, 1)
            for t in range(NT):
                for k, buf in enumerate((y1, y2)):
                    pool.indirect_dma_start(buf[:, t, :], None, y_dram,
                                            bass.IndirectOffsetOnAxis(ap=y_idx[:, k * NT + t:k * NT + t + 1], axis=0)).then_inc(ld_y[t], 16)
            for t in range(NT):
                pool.wait_ge(fin_sq, t + 1)
                inverse_root(t, fin_rstd)


_INS = ["x_prompt", "x_sample", "cache_diff_k", "cache_diff_v", "state_ret_fwd", "state_ret_bwd", "c", "c_ctx", "w_ada",
        "b_ada", "norm1_g", "norm2_g", "w_in", "ret_decay_fwd", "ret_decay_bwd", "ret_norm_g", "diff_lambda_q1",
        "diff_lambda_k1", "diff_lambda_q2", "diff_lambda_k2", "diff_subln_g", "w_ret_o", "w_diff_o", "w_o",
        "router_group_w", "router_group_b", "router_expert_w", "router_expert_b", "moe_w_gate", "moe_w_up",
        "moe_w_down", "final_norm_g"]
_OUTS = [("out_p", (1, 128, D)), ("out_s", (1, 512, D)), ("out_k", (1, 1, 128, AH, 2, DH)), ("out_v", (1, 1, 128, AH, 2 * DH)),
         ("out_ret_f", (1, 1, RH, RK, RV)), ("out_ret_b", (1, 1, RH, RK, RV))]


def kernel(**inputs):
    import concourse.bacc as bacc
    from concourse.bass_utils import run_bass_kernel_spmd

    nc = bacc.Bacc("TRN2", target_bir_lowering=False, num_devices=1)
    main, coff, route, roff = host_constants()
    arrays = {f"in_{n}": np.ascontiguousarray(inputs[n]) for n in _INS}
    arrays["in_const"], arrays["in_route"] = main, route
    a = {k[3:]: nc.dram_tensor(k, v.shape, F32, kind="ExternalInput").ap() for k, v in arrays.items()}
    o = {n: nc.dram_tensor(n, shape, F32, kind="ExternalOutput").ap() for n, shape in _OUTS}
    build(nc, a, o, coff, roff, main.shape[1], route.shape[1])
    r = run_bass_kernel_spmd(nc, [arrays], core_ids=[0])
    return tuple(r.results[0][n] for n, _ in _OUTS)
```

```python
from contextlib import ExitStack

import numpy as np

import concourse.bass as bass
from concourse import mybir

F32 = mybir.dt.float32
F32R = mybir.dt.float32r
I32 = mybir.dt.int32
U32 = mybir.dt.uint32
ALU = mybir.AluOpType
ACT = mybir.ActivationFunctionType
AXX = mybir.AxisListType.X

P = 128
D = 1024
KC = D // P
NT = 5
PT = NT - 1
N512 = 512
N256 = 256
RH, RK, RV = 4, 128, 256
AH, DH = 8, 64
CTX = 256
KEYS = 512 + CTX
GRP, EPG, NE, FF = 4, 8, 32, 256
BLK = 64
PAIRS = NE // 2
OVER = 20
SLOTS = (NE + OVER) * BLK
NPAIR = (NE + OVER) // 2
EPS = 1e-6
BIG = 1e30


def host_constants():
    i = np.arange(P, dtype=np.float32)
    rel = i[None, :] - i[:, None]
    s = np.float32(RK ** -0.5)
    parts = {}
    parts["ident"] = np.eye(P, dtype=np.float32)
    parts["rel_f"] = np.maximum(rel, 0)
    parts["rel_b"] = np.maximum(-rel, 0)
    parts["on_f"] = (rel >= 0) * s
    parts["on_b"] = (rel <= 0) * s
    parts["pos_f"] = np.broadcast_to(i + 1, (P, P))
    parts["pos_b"] = np.broadcast_to(P - i, (P, P))
    parts["kpos"] = np.stack([P - 1 - i, i], 1)
    tok = np.arange(512)
    inv = (np.float32(10000.0) ** (-np.arange(16, dtype=np.float32) / np.float32(16))).astype(np.float32)
    ang = np.stack([(tok // 64).astype(np.float32)[:, None] * inv, (tok % 64).astype(np.float32)[:, None] * inv], 1)
    ang = ang.reshape(4, P, 32).transpose(1, 0, 2).reshape(P, 128).astype(np.float32)
    parts["cos"] = np.cos(ang)
    parts["sin"] = np.sin(ang)
    parts = {k: parts[k] for k in ("rel_f", "rel_b", "on_f", "on_b", "pos_f", "pos_b", "ident", "kpos", "cos", "sin")}
    main = np.concatenate([np.asarray(v, np.float32) for v in parts.values()], 1)
    at, off = 0, {}
    for k, v in parts.items():
        off[k] = (at, at + v.shape[1])
        at += v.shape[1]
    r = {}
    r["before"] = (i[:, None] < i[None, :]) * 1.0
    r["ones"] = np.ones((P, P))
    r["ramp128"] = np.broadcast_to(i, (P, P))
    r["ramp32"] = np.broadcast_to(np.arange(32), (P, 32))
    r["ramp26"] = np.broadcast_to(np.arange(NPAIR), (P, NPAIR))
    r["x64"] = np.broadcast_to(64 * np.arange(1, 10), (P, 9))
    r["x128"] = np.broadcast_to(128 * np.arange(1, NPAIR), (P, NPAIR - 1))
    r["ramp20"] = np.broadcast_to(np.arange(OVER), (P, OVER))
    r["token"] = np.arange(NT)[None, :] * P + i[:, None]
    route = np.concatenate([np.asarray(v, np.float32) for v in r.values()], 1)
    at, roff = 0, {}
    for k, v in r.items():
        roff[k] = (at, at + v.shape[1])
        at += v.shape[1]
    return np.ascontiguousarray(main, np.float32), off, np.ascontiguousarray(route, np.float32), roff


def build(nc, a, o, coff, roff, nconst, nroute):
    ctx = ExitStack()
    with ctx:
        sem_names = {}

        def sem(name):
            s = ctx.enter_context(nc.semaphore(name))
            sem_names[name] = s
            return s

        def sb(name, shape, dt=F32):
            return ctx.enter_context(nc.sbuf_tensor(name, shape, dt))

        KB = 256
        arena_base = -(-nc.sbuf_base // 32) * 32
        arena = sb("arena", [P, 198 * KB])

        def at(kb, n, kb_end=None):
            v = arena[:, int(kb * KB):int(kb * KB) + n]
            return v

        def split_at(name, kb, k, n, dt=F32R):
            return nc.alloc_sbuf_tensor_at(name, [P, k, n], dt, offset=arena_base + int(kb * 1024))

        def tiles(kb, t, n):
            return at(kb, t * n).rearrange("p (t n) -> p t n", t=t)

        setup_n = coff["ident"][0]
        const, const0 = sb("const", [P, nconst - setup_n]), at(20, setup_n)

        def C(k):
            lo, hi = coff[k]
            return const0[:, lo:hi] if lo < setup_n else const[:, lo - setup_n:hi - setup_n]

        dq, dk, dv = tiles(0, NT, N512), tiles(10, NT, N512), tiles(20, NT, N512)
        rq, rk = tiles(30, NT, N512), tiles(40, NT, N512)
        ctx_k, ctx_v = tiles(30, 2, N512), tiles(34, 2, N512)
        gate_t, gate_p = tiles(38, 4, N256), tiles(42, 2, N256)
        rope_t = tiles(82, 4, 256)
        w_raw = [split_at(f"w_loaded{i}", 86 + 16 * i, KC, N256, F32)[:] for i in range(2)]
        w_lo = [split_at(f"w_low{i}", 86 + 16 * i, KC, N256) for i in range(2)]
        w_hi = [split_at(f"w_high{i}", 94 + 16 * i, KC, N256) for i in range(2)]
        left = {}
        for kind, whole_kb, high_kb in (("h", 158, 118), ("o", 138, 118), ("od", 118, 178), ("m", 178, 138)):
            left[kind] = (split_at(kind + "_whole", whole_kb, NT, D, F32), split_at(kind + "_high", high_kb, NT, D),
                          split_at(kind + "_low", whole_kb, NT, D))
        rv, gd_t = tiles(138, NT, D), tiles(138, NT, D)
        xn = tiles(0, NT, D)
        merge = tiles(158, NT, D)
        od = tiles(178, NT, D)
        states_b = tiles(178, 4, D)
        ret = tiles(178, NT, D)
        state_f, state_out = at(50, D), tiles(54, 2, D)
        rqT, rkT = at(62, N512), at(64, N512)
        qf, qb = at(66, N512), at(68, N512)
        sm, ks = at(70, N512), tiles(72, 2, N512)
        square_t = at(76, D)
        qz = [tiles(50 + 4 * i, 2, N512) for i in range(2)]
        kT = [at(58 + 3.5 * i, KEYS + P) for i in range(2)]
        qzp = [at(65 + i, 2 * P).rearrange("p (c n) -> p c n", c=2) for i in range(2)]
        probs = at(67, 2 * KEYS).rearrange("p (c n) -> p c n", c=2)
        mixed = at(73, KEYS)
        mixedT = [at(76 + 3 * i, KEYS) for i in range(2)]
        ada_place = [at(kb, 4 * N512) for kb in (178, 186, 138, 146, 118, 126, 158, 166)]
        ada_slot = lambda i: i if i < KC else i % 2
        ada_turn = lambda i: 1 if i < KC else (i - KC) // 2 + 2
        bias_rows, mod_rows = tiles(50, 3, N512), tiles(56, 3, N512)
        rows = at(62, P)
        rows_t = at(62.5, P)
        ccol = at(63, KC * 32).rearrange("p (k m) -> p k m", k=KC)
        lam_in = at(64, 4 * DH).rearrange("p (v n) -> p v n", v=4)
        decay_e = at(65, 8 * P).rearrange("p (h n) -> p h n", h=8)
        x1 = tiles(0, NT, D)
        g1_rows = tiles(20, 2, D)
        merge_t = tiles(76, 2, N256)
        h2T = at(118, KC * NT * P).rearrange("p (k t) -> p k t", k=KC)
        scale2, shift2 = tiles(162, 2, D), tiles(170, 2, D)
        h2 = [at(158, D), at(80, D)]
        n2_row = h2[1]
        assert nroute <= 2 * KB
        route = at(78, nroute)
        R = lambda k: route[:, roff[k][0]:roff[k][1]]
        rw = at(84, KC * 36).rearrange("p (k n) -> p k n", k=KC)
        rb = at(85.25, 36)
        w_gu = [at(k, KC * 2 * FF).rearrange("p (k g f) -> p k g f", k=KC, g=2) for k in (28, 52, 86, 138, 162, 118)]
        w_dn = [at(k, 2 * D).rearrange("p (k n) -> p k n", k=2) for k in (44, 68, 102, 110, 20, 154)]
        xg, xgT = tiles(178, 2, D), [at(186 + 4 * i, D).rearrange("p (k n) -> p k n", k=KC) for i in range(2)]
        y_out = tiles(76, 2, D)
        act_t, act_s = tiles(134, 2, FF), tiles(136, 2, FF)
        act_a, act_aT = tiles(194, 2, FF), [at(196 + i, 2 * P).rearrange("p (k n) -> p k n", k=2) for i in range(2)]
        g2_rows, fin_row = tiles(118, 2, D), at(126, D)
        fin_t = tiles(162, 2, D)
        y1, y2 = tiles(28, NT, D), tiles(48, NT, D)

        scr_at = [178]

        def scratch(n):
            v = at(scr_at[0], n)
            scr_at[0] += -(-n // 8) / 32
            return v

        logits = scratch(NT * 36).rearrange("p (t n) -> p t n", t=NT)
        g_max, g_idx, g_sum, p_top = [scratch(NT) for _ in range(4)]
        g_eq, g_hot, g_diff = [scratch(NT * GRP).rearrange("p (t n) -> p t n", t=NT) for _ in range(3)]
        e_m, e_eq = [scratch(NT * NE).rearrange("p (t n) -> p t n", t=NT) for _ in range(2)]
        hot = scratch(2 * NT * NE).rearrange("p (k t n) -> p k t n", k=2, t=NT)
        e_max, e_idx = scratch(2 * NT).rearrange("p (k t) -> p k t", k=2), scratch(2 * NT).rearrange("p (k t) -> p k t", k=2)
        e_x, e_den = scratch(NT), scratch(NT)
        e_any = scratch(NT * NE).rearrange("p (t n) -> p t n", t=NT)
        rank_m = scratch(NT * NE).rearrange("p (t n) -> p t n", t=NT)
        prod = scratch(2 * NT * NE).rearrange("p (k t n) -> p k t n", k=2, t=NT)
        cnt_a, cnt_b, over_at = [scratch(NE) for _ in range(3)]
        pads = [scratch(NE + 16) for _ in range(3)]
        over, over_end = pads[0][:, 16:16 + NE], pads[1][:, 16:16 + NE]
        cmp9 = scratch(NE * 9).rearrange("p (e m) -> p e m", m=9)
        cmp_r = scratch(2 * NT * 9).rearrange("p (x m) -> p x m", m=9)
        rk_s, ob_s, qq, slot, pair_i, pos_i, has = [scratch(2 * NT) for _ in range(7)]
        cmp_p = scratch(2 * NT * (NPAIR - 1)).rearrange("p (x m) -> p x m", m=NPAIR - 1)
        hot_kb = scr_at[0]
        scratch(2 * NT * P)
        hot_pos = split_at("hot_places", hot_kb, 2 * NT, P)
        val_kb = scr_at[0]
        scratch(2 * NT * NPAIR)
        val_pair = split_at("tokens_by_pair", val_kb, 2 * NT, NPAIR)
        own_pair = scratch(2 * NT * NPAIR).rearrange("p (x n) -> p x n", n=NPAIR)
        ov_cmp = scratch(OVER * NE).rearrange("p (j e) -> p j e", j=OVER)
        ov_f, n_ov_f = scratch(OVER), scratch(1)
        assert scr_at[0] <= 198, scr_at[0]
        row_idx = sb("row_idx", [P, NPAIR], U32)
        idx_now = sb("idx_now", [P, 1], U32)
        y_idx = sb("y_idx", [P, 2 * NT], U32)
        w_tok = sb("w_tok", [P, 2, NT])
        ov_exp, n_ov = sb("ov_exp", [P, OVER], I32), sb("n_ov", [P, 1], I32)

        ssq, msq, rstd = sb("ssq", [P, NT]), sb("msq", [P, NT]), sb("rstd", [P, NT])
        neg_half = sb("neg_half", [P, 48])
        cols = sb("cols", [P, 25])
        modc = sb("modc", [P, 48, 2])
        mul1 = sb("mul1", [P, KC, 2])
        dec, dec_e, dec_n = sb("dec", [P, 8]), sb("dec_e", [P, 8]), sb("dec_n", [P, 8])
        lg = sb("lg", [P, 8])
        kd, cd = sb("kd", [P, 8]), sb("cd", [P, 8])
        lam_s, neg_lam = sb("lam_s", [P, 2]), sb("neg_lam", [P, 1])
        ret_mask = sb("ret_mask", [P, RH, P])
        q_dec = sb("q_dec", [P, 8, P])
        bn_s, bn_a = sb("bn_s", [P, RH, 6]), sb("bn_a", [P, RH, 2])
        var_e, ret_rstd = sb("var_e", [P, RH]), sb("ret_rstd", [P, RH])
        mx, neg_mx = sb("mx", [P, 2]), sb("neg_mx", [P, 2, 2])
        den, rden, coef = sb("den", [P, 2, 2]), sb("rden", [P, 2, 2]), sb("coef", [P, 2])
        od_ss, od_rstd = sb("od_ss", [P, NT, AH]), sb("od_rstd", [P, NT, AH])

        ps = ctx.enter_context(nc.psum_tensor("ps", [P, 8, N512], F32))
        B = lambda i: ps[:, i, :]
        psf = ps[:].rearrange("p b n -> p (b n)")
        score = [psf[:, 2 * N512:2 * N512 + KEYS], psf[:, 2 * N512 + KEYS:2 * N512 + 2 * KEYS]]

        h2_dram = nc.dram_tensor("h2_rows", [NT * P, D], F32).ap()
        gates_dram = nc.dram_tensor("gates", [2, P, NT, D], F32).ap()
        y_dram = nc.dram_tensor("y_rows", [SLOTS, D], F32).ap()
        mod_dram = nc.dram_tensor("mod_rows_dram", [2, 6 * D], F32).ap()

        w_in = a["w_in"][0]
        off = dict(rq=0, rk=512, rv0=1024, rv1=1536, rg0=2048, rg1=2560, dq0=3072, dq1=3584, dk0=4096,
                   dk1=4608, dv0=5120, dv1=5632, gr0=6144, gr1=6656, gd0=7168, gd1=7680)
        SECTIONS = ["rq", "rk", "rv0", "rv1", "dq0", "dk0", "dv0", "rg0", "rg1", "gr0", "gr1", "gd0", "gd1", "dq1", "dk1", "dv1",
                    "wr0", "wr1", "wd0", "wd1", "wo0", "wo1"]
        UNITS = [(s, hh) for s in SECTIONS for hh in range(2)]
        unit_at = {u: i for i, u in enumerate(UNITS)}
        LEFT = lambda s: {"wr": "o", "wd": "od", "wo": "m"}.get(s[:2], "h")

        def section_source(s, hh):
            if s in off:
                m, c = w_in, off[s]
            else:
                m = {"wr": a["w_ret_o"], "wd": a["w_diff_o"], "wo": a["w_o"]}[s[:2]][0]
                c = 512 * int(s[2])
            return m[:, c + N256 * hh:c + N256 * (hh + 1)].rearrange("(k p) n -> p k n", p=P)

        plan = []
        dense = []

        def put_dense(*item):
            plan.append(("dense", len(dense)))
            dense.append(item)

        def emit(item):
            if item[0] in ("cv", "split"):
                plan.append(item)
            else:
                put_dense(*item)

        def unit(s, hh):
            out = []
            i = unit_at[(s, hh)]
            for t in range(NT):
                out.append(("mm", s, t, hh))
                if t == 2 and i + 1 < len(UNITS):
                    out.append(("cv", i + 1))
            return out

        def section(s):
            return unit(s, 0) + unit(s, 1)

        def transposed(what, t):
            return [x for half in range(2) for x in (("T4", what, t, half), ("split", what, t, half))]

        def with_left(what, items):
            out = transposed(what, 0) + transposed(what, 1)
            for item in items:
                out.append(item)
                if item[0] == "mm" and item[2] + 2 < NT:
                    out += transposed(what, item[2] + 2)
            return out

        plan.append(("cv", 0))
        ada_k = [(r, k) for r in (1, 2) for k in range(KC)]
        n = 0
        for item in with_left("h", unit("rq", 0)) + unit("rq", 1) + [x for s in ("rk", "rv0", "rv1") for x in section(s)]:
            emit(item)
            n += item[0] == "mm"
            if item[0] == "mm" and n % 2 == 0 and ada_k:
                plan.append(("ada",) + ada_k.pop(0))
        UPDATES = [("b", 3), ("b", 2), ("b", 1), ("f", PT), ("b", PT), ("f", 0), ("f", 1), ("f", 2)]
        gaps = {0: [("U", 0, 0, 7), ("U", 0, 1, 4)],
                1: [("U", 1, 0, 7), ("U", 1, 1, 4), ("RT", PT)],
                2: [("U", 2, 0, 7), ("U", 2, 1, 4)],
                3: [("SC", PT), ("U", 3, 0, 7)],
                4: [("O", PT), ("RT", 0), ("U", 3, 1, 7), ("U", 4, 0, 4)],
                5: [("SC", 0), ("U", 4, 1, 7)],
                6: [("O", 0), ("RT", 1), ("U", 5, 0, 7), ("U", 5, 1, 4)],
                7: [("SC", 1)],
                8: [("O", 1), ("RT", 2), ("U", 6, 0, 7), ("U", 6, 1, 4)],
                9: [("SC", 2)],
                10: [("O", 2), ("RT", 3), ("U", 7, 0, 7), ("U", 7, 1, 4)],
                11: [("SC", 3)],
                12: [("O", 3)]}
        n = 0
        for item in [x for s in ("dq0", "dk0", "dv0") for x in section(s)]:
            emit(item)
            if item[0] != "cv":
                if n % 2:
                    plan.extend(gaps.get(n // 2, []))
                n += 1
        plan.append(("ret_end",))
        for s, hh, half in (("rg0", 0, None), ("rg0", 1, None), ("rg1", 0, 0), ("rg1", 1, 1)):
            for item in unit(s, hh):
                emit(item)
                if half is not None and item[0] == "mm" and item[2]:
                    put_dense("T4", "o", item[2] - 1, half)
            if half is not None:
                put_dense("T4", "o", PT, half)

        def prep(h, i):
            put_dense("T4", "prep", h, i)

        steps = [(h, t) for h in range(AH) for t in range(NT)]

        def attention(half, work):
            for i in range(3):
                prep(4 * half, i)
            mine = [s for s in range(len(steps)) if steps[s][0] // 4 == half]
            extra = {4 * half + h: [(4 * half + h + 1, i) for i in range(3)] for h in range(3)}
            products = sum(item[0] == "mm" for item in work)
            share, k = [[] for _ in mine], 0
            for item in work:
                k += item[0] == "mm"
                share[max(k - 1, 0) * len(mine) // products].append(item)
            for j, s in enumerate(mine):
                h, t = steps[s]
                plan.append(("S", s))
                if j:
                    plan.append(("AT", s - 1))
                for item in share[j]:
                    emit(item)
                if t in (1, 2, 3) and h in extra:
                    prep(*extra[h][t - 1])
                if j:
                    plan.append(("PV", s - 1))
                    if t == 0:
                        plan.append(("H", h - 1))
            plan.append(("AT", mine[-1]))
            plan.append(("PV", mine[-1]))
            plan.append(("H", 4 * half + 3))

        attention(0, [x for s in ("gr0", "gr1", "gd0", "gd1") for x in section(s)])
        for s in ["dq1", "dk1", "dv1"]:
            for item in section(s):
                emit(item)
        split_o = lambda t: [("split", "o", t, half) for half in range(2)]
        for item in split_o(0):
            emit(item)
        first = []
        for item in unit("wr0", 0):
            first += [item] + (split_o(item[2] + 1) if item[0] == "mm" and item[2] + 1 < NT else [])
        attention(1, first + unit("wr0", 1) + section("wr1"))
        plan.append(("att_end",))
        for item in with_left("od", unit("wd0", 0)) + unit("wd0", 1) + section("wd1"):
            emit(item)
        for item in with_left("m", unit("wo0", 0)) + unit("wo0", 1):
            emit(item)
        for item in (("mm", "wo1", 0, 0), ("mm", "wo1", 1, 0), ("cv", len(UNITS) - 1)):
            emit(item)
        for t in range(NT):
            if t + 2 < NT:
                put_dense("mm", "wo1", t + 2, 0)
            if t > 1:
                plan.append(("L", t - 2))
            if t:
                plan.append(("N", t - 1))
            put_dense("mm", "wo1", t, 1)
            if t:
                plan.append(("R", t - 1))
            plan.append(("Q", t))
        plan.extend([("N", NT - 1), ("L", NT - 2), ("R", NT - 1), ("L", NT - 1)])
        where = {(item[:3] if item[0] == "mm" else item): n for n, item in enumerate(dense)}

        def final_engine(n):
            kind, what = dense[n][0], dense[n][1]
            if kind == "T4":
                return "A" if what == "prep" or n % 2 == 0 else "D"
            return "D" if what[:2] in ("rg", "wr", "wd", "wo") else "A"

        count = {"A": 0, "D": 0}
        freed = []
        for n in range(len(dense)):
            e = final_engine(n)
            count[e] += 1
            freed.append((e, count[e]))
        rope_at = {}
        for item in dense:
            if item[0] == "mm" and item[1][:2] in ("dq", "dk") and item[2] < PT and item[3] == 1:
                rope_at[item[1:3]] = len(rope_at) + 1
        gate_at = {}
        for item in dense:
            if item[0] == "mm" and item[1][:2] == "rg":
                gate_at[item[1:]] = len(gate_at) + 1
        splits = [e[1:] for e in plan if e[0] == "split"]
        split_n = {x: n + 1 for n, x in enumerate(splits)}
        x1_done, k = {}, 0
        for item in dense:
            if item[0] == "mm" and item[1][:2] == "wo":
                k += 1
                x1_done[item[2]] = k
        wr_items = [n for n, item in enumerate(dense) if item[0] == "mm" and item[1][:2] == "wr"]
        spill_at = {}
        for item in dense:
            if item[0] == "mm" and item[1][:2] in ("gr", "gd"):
                spill_at[item[1:]] = len(spill_at)
        last_of = {s: where[("mm", s, PT)] for s in SECTIONS}
        unit_end = {n: unit_at[(item[1], item[3])] for n, item in enumerate(dense) if item[0] == "mm" and item[2] == PT}
        end_of = {i: n for n, i in unit_end.items()}
        n_u = {}
        u_before = 0
        sc_before = 0
        order = {}
        in_bank = {}
        for e in plan:
            if e[0] == "U":
                order[e] = (in_bank.get(e[3], 0), sc_before)
                u_before += 1
                in_bank[e[3]] = u_before
            if e[0] == "SC":
                order[e] = (u_before, sc_before)
                sc_before += 1
        RET = [PT, 0, 1, 2, 3]

        ld_const, ld_small, ld_x = sem("ld_const"), sem("ld_small"), sem("ld_x")
        ld_w = [sem("ld_w0"), sem("ld_w1")]
        ld_ada = [sem(f"ld_ada{i}") for i in range(KC)]
        ld_state, ld_ctx = sem("ld_state"), [sem("ld_ctx0"), sem("ld_ctx1")]
        act_set, dve_set, pool_set, pe_set = sem("act_set"), sem("dve_set"), sem("pool_set"), sem("pe_set")
        dve_chain, act_chain, pool_chain = sem("dve_chain"), sem("act_chain"), sem("pool_chain")
        ssq_ready, rstd_ready, xn_ready = sem("ssq_ready"), sem("rstd_ready"), sem("xn_ready")
        pe_ada, ada_rows, pe_modT, mod_cols = sem("pe_ada"), sem("ada_rows"), sem("pe_modT"), sem("mod_cols")
        pe_dense, freed_a, freed_d = sem("pe_dense"), sem("freed_a"), sem("freed_d")
        rope_done, gate_done, merged = sem("rope_done"), sem("gate_done"), sem("merged")
        pe_u, u_read, u_keys = sem("pe_u"), sem("u_read"), sem("u_keys")
        pe_rt, rt_read, q_scaled = sem("pe_rt"), sem("rt_read"), sem("q_scaled")
        pe_sc, sc_masked, pe_o, o_read = sem("pe_sc"), sem("sc_masked"), sem("pe_o"), sem("o_read")
        o_stats, o_rstd, o_normed = sem("o_stats"), sem("o_rstd"), sem("o_normed")
        pe_scores, max_ready, exp_done, mixed_ready = sem("pe_scores"), sem("max_ready"), sem("exp_done"), sem("mixed_ready")
        tanh_done = sem("tanh_done")
        w_rounded, w_split, x_rounded, x_split = sem("w_rounded"), sem("w_split"), sem("x_rounded"), sem("x_split")
        st_gate, ld_gr, ld_gd = [sem(f"st_gate{i}") for i in range(4)], [sem(f"ld_gr{i}") for i in range(4)], sem("ld_gd")
        pe_at, at_read, pe_pv, pv_read = sem("pe_at"), sem("at_read"), sem("pe_pv"), sem("pv_read")
        od_scaled, x1_ready = sem("od_scaled"), sem("x1_ready")
        st_mod, st_ret, st_kv = sem("st_mod"), sem("st_ret"), [sem("st_kv0"), sem("st_kv1")]
        st_fill = sem("st_fill")
        st_h2 = [sem("st_h2_0"), sem("st_h2_1")]
        ld_x1, ld_g1, ld_route, ld_row2 = sem("ld_x1"), sem("ld_g1"), sem("ld_route"), sem("ld_row2")
        st_sq2, pool2, h2_ready, pe_h2, h2_read, pe_logits = (sem(x) for x in
            ("st_sq2", "pool2", "h2_ready", "pe_h2", "h2_read", "pe_logits"))
        route_d, route_a, pe_rank, pe_table, idx_ready = (sem(x) for x in
            ("route_d", "route_a", "pe_rank", "pe_table", "idx_ready"))
        ld_gu, ld_dn = [sem(f"ld_gu{i}") for i in range(6)], [sem(f"ld_dn{i}") for i in range(6)]
        ld_xg = [sem("ld_xg0"), sem("ld_xg1")]
        ov_take = sem("ov_take")
        pe_xt, xt_read, pe_gu, gu_tanh, gu_act, pe_aT, aT_read, pe_dn, y_a, y_d = (sem(x) for x in
            ("pe_xt", "xt_read", "pe_gu", "gu_tanh", "gu_act", "pe_aT", "aT_read", "pe_dn", "y_a", "y_d"))
        gu_half = sem("gu_half")
        st_y = [sem("st_y0"), sem("st_y1")]
        (ov_free, ov_idx, ov_x, ov_w, ov_xt, ov_xr, ov_gu, ov_tanh, ov_half, ov_act, ov_aT, ov_ar, ov_dn, ov_ya,
         ov_yd, ov_st, ov_over) = (sem("ov_" + x) for x in ("free", "idx", "x", "w", "xt", "xr", "gu", "tanh", "half",
                                   "act", "aT", "ar", "dn", "ya", "yd", "st", "over"))
        ld_y = [sem(f"ld_y{t}") for t in range(NT)]
        y_used, fin_sq, fin_rstd, fin_ready, ld_fin = (sem(x) for x in ("y_used", "fin_sq", "fin_rstd", "fin_ready", "ld_fin"))
        y_scaled, y_sum, y_gated = sem("y_scaled"), sem("y_sum"), sem("y_gated")
        st_fin = [sem("st_fin0"), sem("st_fin1")]
        n_freed = {"A": count["A"], "D": count["D"]}

        block = ctx.enter_context(nc.Block())

        def wait_freed(eng, n):
            e, v = freed[n]
            eng.wait_ge(freed_a if e == "A" else freed_d, v)

        def free(ins, n):
            ins.then_inc(freed_a if freed[n][0] == "A" else freed_d, 1)

        @block.sync
        def _(sp):
            sp.dma_start(const[:], a["const"][:, setup_n:]).then_inc(ld_const, 16)
            sp.dma_start(const0, a["const"][:, 0:setup_n]).then_inc(ld_const, 16)
            vec = lambda v: v.rearrange("(k p) -> k p", p=P)
            for r0, v in ((0, a["c"][0]), (8, a["c_ctx"]), (16, a["norm1_g"][0]), (24, a["norm2_g"][0]),
                          (32, a["ret_norm_g"][0])):
                sp.dma_start(rows[r0:r0 + 8, :], vec(v)).then_inc(ld_small, 16)
            sp.dma_start(rows[40:41, :], vec(a["diff_subln_g"][0])).then_inc(ld_small, 16)
            sp.dma_start(dec[:, 0:4], a["ret_decay_fwd"][0].partition_broadcast(P)).then_inc(ld_small, 16)
            sp.dma_start(dec[:, 4:8], a["ret_decay_bwd"][0].partition_broadcast(P)).then_inc(ld_small, 16)
            def load_ada(i):
                if i >= KC:
                    sp.wait_ge(pe_ada, i - 1 if i >= KC + 2 else i - KC + 1)
                r, k = divmod(i, KC)
                sp.dma_start(ada_place[ada_slot(i)], a["w_ada"][0][k * P:(k + 1) * P, 2048 * r:2048 * r + 2048]).then_inc(ld_ada[ada_slot(i)], 16)

            def load_w(i):
                if i >= 2:
                    sp.wait_ge(pe_dense, end_of[i - 2] + 1)
                sp.dma_start(w_raw[i % 2], section_source(*UNITS[i])).then_inc(ld_w[i % 2], 16)

            for i in range(2):
                load_ada(i)
            for i, v in enumerate(("diff_lambda_q1", "diff_lambda_k1", "diff_lambda_q2", "diff_lambda_k2")):
                sp.dma_start(lam_in[:, i, :], a[v][0].partition_broadcast(P)).then_inc(ld_small, 16)
            for j in range(4):
                src = a["b_ada"][0].rearrange("(r j n) -> j r n", r=3, j=4)[j]
                sp.dma_start(bias_rows[32 * j:32 * j + 32, :, :], src.partition_broadcast(32)).then_inc(ld_small, 16)
            for t in range(NT):
                src = a["x_prompt"][0] if t == PT else a["x_sample"][0][t * P:(t + 1) * P, :]
                sp.dma_start(xn[:, t, :], src).then_inc(ld_x, 16)
            for i in range(2, KC):
                load_ada(i)
            load_w(0)
            load_w(1)
            load_ada(KC)
            load_ada(KC + 1)

            def mod_out():
                for r in (1, 2):
                    sp.wait_ge(ada_rows, r + 1)
                    for j in range(4):
                        c0 = (4 * r + j) * N512
                        sp.dma_start(mod_dram[:, c0:c0 + N512], mod_rows[32 * j:32 * j + 2, r, :]).then_inc(st_mod, 16)
                sp.wait_ge(pe_ada, 3 * KC)
                sp.dma_start(states_b[:, 3, :].rearrange("p (h e) -> p h e", h=RH),
                             a["state_ret_bwd"][0, 0].rearrange("h d e -> d h e")).then_inc(ld_state, 16)
                sp.wait_ge(st_mod, 16 * 8)
                sp.wait_ge(ada_rows, 3)
                sp.dma_start(state_f.rearrange("p (h e) -> p h e", h=RH),
                             a["state_ret_fwd"][0, 0].rearrange("h d e -> d h e")).then_inc(ld_state, 16)

            def fill_out():
                for i in range(OVER * BLK // (NT * P)):
                    r0 = NE * BLK + i * NT * P
                    sp.dma_start(y_dram[r0:r0 + NT * P, :].rearrange("(p k) n -> p (k n)", k=NT),
                                 left["h"][1][:].bitcast(F32).rearrange("p t n -> p (t n)")).then_inc(st_fill, 16)

            def state_out_dma(i):
                sp.wait_ge(u_read, 2 * (3 + i) + 2)
                sp.dma_start(o[("out_ret_f", "out_ret_b")[i]][0, 0].rearrange("h d e -> d h e"),
                             state_out[:, i, :].rearrange("p (h e) -> p h e", h=RH)).then_inc(st_ret, 16)

            def keys_out(half):
                c0 = N512 * half
                wait_freed(sp, where[("mm", f"dk{half}", PT)])
                sp.dma_start(o["out_k"][0, 0].rearrange("t h c d -> t (h c d)")[:, c0:c0 + N512], dk[:, PT, :]).then_inc(st_kv[half], 16)

            def values_out(half):
                c0 = N512 * half
                wait_freed(sp, where[("mm", f"dv{half}", PT)])
                sp.dma_start(o["out_v"][0, 0].rearrange("t h d -> t (h d)")[:, c0:c0 + N512], dv[:, PT, :]).then_inc(st_kv[half], 16)

            def gate_out(n):
                _, s, t, hh = dense[n]
                v = spill_at[dense[n][1:]]
                c0 = N512 * int(s[2]) + N256 * hh
                wait_freed(sp, n)
                sp.dma_start(gates_dram[0 if s[:2] == "gr" else 1, :, t, c0:c0 + N256], gate_t[:, v % 4, :]).then_inc(st_gate[v % 4], 16)

            def load_gate(v):
                _, s, t, hh = dense[wr_items[v]]
                c0 = N512 * int(s[2]) + N256 * hh
                if v >= 4:
                    wait_freed(sp, wr_items[v - 4])
                sp.dma_start(gate_t[:, v % 4, :], gates_dram[0, :, t, c0:c0 + N256]).then_inc(ld_gr[v % 4], 16)

            def load_ctx(half):
                c0 = N512 * half
                sp.dma_start(ctx_k, a["cache_diff_k"][0, 0].rearrange("(t p) h c d -> p t (h c d)", p=P)[:, :, c0:c0 + N512]).then_inc(ld_ctx[half], 16)
                sp.dma_start(ctx_v, a["cache_diff_v"][0, 0].rearrange("(t p) h d -> p t (h d)", p=P)[:, :, c0:c0 + N512]).then_inc(ld_ctx[half], 16)

            def residual():
                sp.wait_ge(pe_pv, 40)
                wait_freed(sp, wr_items[-1])
                sp.wait_ge(st_ret, 16 * 2)
                sp.wait_ge(st_kv[0], 16 * 2)
                sp.wait_ge(st_kv[1], 16 * 2)
                for t in range(NT):
                    src = a["x_prompt"][0] if t == PT else a["x_sample"][0][t * P:(t + 1) * P, :]
                    sp.dma_start(x1[:, t, :], src).then_inc(ld_x1, 16)
                for s in range(2):
                    sp.dma_start(g1_rows[:, s, :], mod_dram[s, 2 * D:3 * D].partition_broadcast(P)).then_inc(ld_g1, 16)

            def load_gate_up(e, slot):
                for g, w in enumerate((a["moe_w_gate"], a["moe_w_up"])):
                    sp.dma_start(w_gu[slot][:, :, g, :], w[0, e].rearrange("(k p) f -> p k f", p=P)).then_inc(ld_gu[slot], 16)

            def load_down(e, slot):
                sp.dma_start(w_dn[slot], a["moe_w_down"][0, e].rearrange("(k p) n -> p k n", p=P)).then_inc(ld_dn[slot], 16)

            def load_expert(e, slot):
                load_gate_up(e, slot)
                load_down(e, slot)

            for e in plan:
                if e[0] == "ada":
                    i = e[1] * KC + e[2]
                    if i + 2 < 3 * KC:
                        load_ada(i + 2)
                    if i == 3 * KC - 1:
                        mod_out()
                elif e[0] == "U" and e[1] in (3, 4) and e[2] == 1:
                    state_out_dma(e[1] - 3)
                elif e[0] == "ret_end":
                    sp.wait_ge(pe_rt, NT)
                    sp.wait_ge(u_keys, len(UPDATES))
                    load_ctx(0)
                    fill_out()
                elif e[0] == "N":
                    t = e[1]
                    sp.wait_ge(h2_ready, t + 1)
                    sp.dma_start(h2_dram[t * P:(t + 1) * P, :], h2[t % 2]).then_inc(st_h2[t % 2], 16)
                elif e == ("PV", 19):
                    sp.wait_ge(pe_pv, 20)
                    load_ctx(1)
                elif e[0] == "att_end":
                    residual()
                    load_expert(0, 0)
                    load_expert(1, 1)
                elif e[0] == "dense":
                    n = e[1]
                    item = dense[n]
                    if item[1][:2] in ("gr", "gd"):
                        gate_out(n)
                    if n in unit_end:
                        i = unit_end[n]
                        if i + 2 < len(UNITS):
                            load_w(i + 2)
                        if item[1][:2] == "dk" and item[3] == 1:
                            keys_out(int(item[1][2]))
                        elif item[1][:2] == "dv" and item[3] == 1:
                            values_out(int(item[1][2]))
                    if item[0] == "mm" and item[1][:2] == "wr" and wr_items.index(n) + 4 < len(wr_items):
                        load_gate(wr_items.index(n) + 4)
                    if n == last_of["dv1"]:
                        for x in st_gate:
                            sp.wait_ge(x, 16 * len(spill_at) // 4)
                        for v in range(4):
                            load_gate(v)
                    elif n == last_of["wr1"]:
                        sp.wait_ge(pe_dense, n + 1)
                        sp.dma_start(gd_t, gates_dram[1]).then_inc(ld_gd, 16)
                    elif n == last_of["wo1"]:
                        sp.wait_ge(pe_dense, n + 1)
                        load_expert(2, 2)
                        load_expert(3, 3)
                    elif n == last_of["wd1"]:
                        sp.wait_ge(pe_dense, n + 1)
                        sp.dma_start(route, a["route"]).then_inc(ld_route, 16)
                        sp.dma_start(rw[:, :, 0:GRP], a["router_group_w"][0].rearrange("(k p) n -> p k n", p=P)).then_inc(ld_route, 16)
                        sp.dma_start(rw[:, :, GRP:36], a["router_expert_w"][0].rearrange("(k p) n -> p k n", p=P)).then_inc(ld_route, 16)
                        sp.dma_start(rb[:, 0:GRP], a["router_group_b"][0].partition_broadcast(P)).then_inc(ld_route, 16)
                        sp.dma_start(rb[:, GRP:36], a["router_expert_b"][0].partition_broadcast(P)).then_inc(ld_route, 16)
                        sp.dma_start(n2_row, a["norm2_g"][0].partition_broadcast(P)).then_inc(ld_route, 16)
                    elif item == ("T4", "m", PT, 1):
                        sp.wait_ge(pe_dense, n + 1)
                        for i in range(2):
                            sp.dma_start(scale2[:, i, :], mod_dram[i, 4 * D:5 * D].partition_broadcast(P)).then_inc(ld_row2, 16)
                            sp.dma_start(shift2[:, i, :], mod_dram[i, 3 * D:4 * D].partition_broadcast(P)).then_inc(ld_row2, 16)
            sp.wait_ge(h2_ready, NT)
            load_expert(4, 4)
            sp.wait_ge(pe_logits, NT)
            load_gate_up(5, 5)
            sp.wait_ge(st_h2[0], 16 * 3)
            sp.wait_ge(st_h2[1], 16 * 2)
            load_down(5, 5)

            def pair_io(p, par, into=None):
                if into:
                    sp.wait_ge(pe_gu, p + 1)
                    for i in range(2):
                        load_gate_up(into[0] + i, into[1] + i)
                    sp.wait_ge(pe_dn, p + 1)
                    for i in range(2):
                        load_down(into[0] + i, into[1] + i)
                sp.wait_ge(y_a, p + 1)
                sp.wait_ge(y_d, p + 1)
                sp.dma_start(y_dram[bass.ds(p * P, P), :], y_out[:, par, :]).then_inc(st_y[par], 16)

            pair_io(0, 0, (6, 0))
            pair_io(1, 1, (8, 2))
            pair_io(2, 0)
            for i in range(2):
                sp.dma_start(g2_rows[:, i, :], mod_dram[i, 5 * D:6 * D].partition_broadcast(P)).then_inc(ld_fin, 16)
            sp.dma_start(fin_row, a["final_norm_g"].partition_broadcast(P)).then_inc(ld_fin, 16)
            with sp.Fori(0, (PAIRS - 6) // 2) as i:
                pair_io(2 * i + 3, 1, (4 * i + 10, 0))
                pair_io(2 * i + 4, 0, (4 * i + 12, 2))
            pair_io(PAIRS - 3, 1, (NE - 2, 0))
            pair_io(PAIRS - 2, 0)
            pair_io(PAIRS - 1, 1)
            for par in range(2):
                sp.wait_ge(st_y[par], 16 * PAIRS // 2)
            n_over = sp.value_load(n_ov[0:1, 0:1], min_val=0, max_val=OVER)
            with sp.If(n_over > 0):
                with sp.Fori(0, OVER // 2) as j:
                    with sp.If(n_over > 2 * j):
                        sp.wait_ge(ov_free, j + 1)
                        for i in range(2):
                            e = sp.value_load(ov_exp[0:1, bass.ds(2 * j + i, 1)], min_val=0, max_val=NE - 1)
                            for g, w in enumerate((a["moe_w_gate"], a["moe_w_up"])):
                                sp.dma_start(w_gu[i][:, :, g, :], w[0, bass.ds(e, 1)].rearrange("o (k p) f -> p (o k) f", p=P)).then_inc(ov_w, 16)
                            sp.dma_start(w_dn[i], a["moe_w_down"][0, bass.ds(e, 1)].rearrange("o (k p) n -> p (o k) n", p=P)).then_inc(ov_w, 16)
                        sp.wait_ge(ov_ya, j + 1)
                        sp.wait_ge(ov_yd, j + 1)
                        sp.dma_start(y_dram[bass.ds((j + PAIRS) * P, P), :], y_out[:, 0, :]).then_inc(ov_st, 16)
                        sp.wait_ge(ov_st, 16 * j + 16)
                        sp.sem_inc(ov_free, 1)
                    with sp.Else():
                        sp.nop()
            with sp.Else():
                sp.nop()
            sp.sem_inc(ov_over, 1)
            for t in range(NT):
                sp.wait_ge(fin_ready, t + 1)
                dst = o["out_p"][0] if t == PT else o["out_s"][0][t * P:(t + 1) * P, :]
                sp.dma_start(dst, fin_t[:, t % 2, :]).then_inc(st_fin[t % 2], 16)
            sp.wait_ge(st_fin[0], 16 * 3)
            sp.wait_ge(st_fin[1], 16 * 2)
            sp.wait_ge(st_ret, 16 * 2)
            sp.wait_ge(st_kv[0], 16 * 2)
            sp.wait_ge(st_kv[1], 16 * 2)

        @block.tensor
        def _(pe):
            ident = C("ident")
            pe.wait_ge(ld_const, 32)
            pe.wait_ge(dve_set, 1)
            pe.transpose(B(7)[:, 0:41], rows[0:41, :], ident[0:41, 0:41]).then_inc(pe_set, 1)

            def ada(r, k):
                i = r * KC + k
                pe.wait_ge(ld_ada[ada_slot(i)], 16 * ada_turn(i))
                if k == 0:
                    pe.wait_ge(dve_set, 2)
                    if r:
                        pe.wait_ge(ada_rows, r)
                for j in range(4):
                    mm = pe.matmul(B(7)[32 * j:32 * j + 32, :], ccol[:, k, :], ada_place[ada_slot(i)][:, j * N512:(j + 1) * N512],
                                   start=(k == 0), stop=(k == KC - 1))
                mm.then_inc(pe_ada, 1)

            def mod_columns(r):
                pe.wait_ge(ada_rows, r + 1)
                if r:
                    pe.wait_ge(mod_cols, r)
                for m in range(4):
                    mm = pe.transpose(B(2)[:, m * P:(m + 1) * P], mod_rows[:, r, m * P:(m + 1) * P], ident)
                mm.then_inc(pe_modT, 1)

            for k in range(KC):
                ada(0, k)
            mod_columns(0)

            def dense_item(n):
                item = dense[n]
                if n >= 2:
                    wait_freed(pe, n - 2)
                out = B(n % 2)
                if item[0] == "mm":
                    _, s, t, hh = item
                    i = unit_at[(s, hh)]
                    if t == 0:
                        pe.wait_ge(w_split, i + 1)
                    kind = LEFT(s)
                    if s in ("rq", "wr0", "wd0", "wo0") and hh == 0:
                        pe.wait_ge(x_split, split_n[(kind, t, 1)])
                    _, x_hi, x_lo = left[kind]
                    for k in range(KC):
                        for j, (x, w) in enumerate(((x_hi, w_hi), (x_hi, w_lo), (x_lo, w_hi))):
                            mm = pe.matmul(out[:, 0:N256], x[:, t, k * P:(k + 1) * P], w[i % 2][:, k, :],
                                           start=(k == 0 and j == 0), stop=(k == KC - 1 and j == 2))
                else:
                    _, what, t, half = item
                    if what == "prep":
                        h, i = t, half
                        c0 = P * (h % 4)
                        hf = h // 4
                        if i == 0:
                            pe.wait_ge(rope_done, rope_at[(f"dq{hf}", PT - 1)])
                            src = [dq[:, q, c0:c0 + P] for q in range(4)]
                        elif i == 1:
                            pe.wait_ge(rope_done, rope_at[(f"dk{hf}", PT - 1)])
                            src = [dk[:, q, c0:c0 + P] for q in range(4)]
                        else:
                            pe.wait_ge(ld_ctx[hf], 32)
                            wait_freed(pe, where[("mm", f"dk{hf}", PT)])
                            src = [ctx_k[:, 0, c0:c0 + P], ctx_k[:, 1, c0:c0 + P], dk[:, PT, c0:c0 + P], dq[:, PT, c0:c0 + P]]
                    else:
                        if what == "h":
                            pe.wait_ge(xn_ready, t + 1)
                            buf = xn
                        elif what == "o":
                            pe.wait_ge(gate_done, gate_at[(f"rg{half}", t, 1)])
                            buf = ret
                        elif what == "od":
                            pe.wait_ge(od_scaled, 4 * (half + 1))
                            buf = od
                        else:
                            pe.wait_ge(merged, 3 * NT + t + 1)
                            buf = merge
                        src = [buf[:, t, (4 * half + k) * P:(4 * half + k + 1) * P] for k in range(4)]
                    for k in range(4):
                        mm = pe.transpose(out[:, k * P:(k + 1) * P], src[k], ident)
                mm.then_inc(pe_dense, 1)

            def update(e):
                _, u, half, b = e
                dirn, t = UPDATES[u]
                ub, sc = order[e]
                pe.wait_ge(u_keys, u + 1)
                if ub:
                    pe.wait_ge(u_read, ub)
                if b == 4 and sc:
                    pe.wait_ge(sc_masked, sc)
                for i in range(2):
                    h = 2 * half + i
                    mm = pe.matmul(B(b)[:, i * RV:(i + 1) * RV], ks[:, u % 2, h * P:(h + 1) * P],
                                   rv[:, t, h * RV:(h + 1) * RV], start=(i == 0), stop=(i == 1), skip_group_check=True)
                mm.then_inc(pe_u, 1)

            def router_transposes(t):
                pe.wait_ge(h2_ready, t + 1)
                if t:
                    pe.wait_ge(h2_read, t)
                else:
                    pe.wait_ge(at_read, len(steps))
                for k in range(KC):
                    mm = pe.transpose(B(5 + k // 4)[:, (k % 4) * P:(k % 4 + 1) * P], h2[t % 2][:, k * P:(k + 1) * P], ident)
                mm.then_inc(pe_h2, 1)

            def logits_of(t):
                if t == 0:
                    pe.wait_ge(ld_route, 16 * 6)
                    pe.wait_ge(mixed_ready, len(steps))
                pe.wait_ge(h2_read, t + 1)
                for k in range(KC):
                    mm = pe.matmul(B(2)[:, t * 36:(t + 1) * 36], h2T[:, k, t * P:(t + 1) * P], rw[:, k, :],
                                   start=(k == 0), stop=(k == KC - 1), skip_group_check=True)
                mm.then_inc(pe_logits, 1)

            n_rt = n_sc = n_o = 0
            for e in plan:
                if e[0] == "dense":
                    dense_item(e[1])
                elif e[0] == "R":
                    router_transposes(e[1])
                elif e[0] == "L":
                    logits_of(e[1])
                elif e[0] == "ada":
                    ada(e[1], e[2])
                    if e[2] == KC - 1:
                        mod_columns(e[1])
                elif e[0] == "U":
                    update(e)
                elif e[0] == "RT":
                    t = e[1]
                    if n_rt:
                        pe.wait_ge(rt_read, n_rt)
                    if n_rt == 0:
                        pe.wait_ge(mod_cols, 3)
                    for h in range(RH):
                        pe.transpose(B(2)[:, h * P:(h + 1) * P], rq[:, t, h * P:(h + 1) * P], ident)
                    for h in range(RH):
                        mm = pe.transpose(B(3)[:, h * P:(h + 1) * P], rk[:, t, h * P:(h + 1) * P], ident)
                    mm.then_inc(pe_rt, 1)
                    n_rt += 1
                elif e[0] == "SC":
                    n_sc += 1
                    pe.wait_ge(rt_read, n_sc)
                    pe.wait_ge(u_read, order[e][0])
                    if n_sc > 1:
                        pe.wait_ge(sc_masked, n_sc - 1)
                    for h in range(RH):
                        mm = pe.matmul(B(4)[:, h * P:(h + 1) * P], rkT[:, h * P:(h + 1) * P], rqT[:, h * P:(h + 1) * P],
                                       start=(h == 0), stop=(h == RH - 1), skip_group_check=True)
                    mm.then_inc(pe_sc, 1)
                elif e[0] == "O":
                    t = e[1]
                    n_o += 1
                    pe.wait_ge(sc_masked, n_o)
                    if n_o > 1:
                        pe.wait_ge(o_read, n_o - 1)
                    if t != PT:
                        pe.wait_ge(q_scaled, t + 1)
                        pe.wait_ge(ld_state, 32)
                        pe.wait_ge(u_read, 6 if t == 0 else 10 + 2 * t)
                    for h in range(RH):
                        out = B(5 + h // 2)[:, (h % 2) * RV:(h % 2 + 1) * RV]
                        mm = pe.matmul(out, sm[:, h * P:(h + 1) * P], rv[:, t, h * RV:(h + 1) * RV],
                                       start=(h % 2 == 0), stop=(t == PT and h % 2 == 1), skip_group_check=True)
                        if t != PT:
                            pe.matmul(out, qf[:, h * P:(h + 1) * P], state_f[:, h * RV:(h + 1) * RV],
                                      start=False, stop=False, skip_group_check=True)
                            mm = pe.matmul(out, qb[:, h * P:(h + 1) * P], states_b[:, t, h * RV:(h + 1) * RV],
                                           start=False, stop=(h % 2 == 1), skip_group_check=True)
                    mm.then_inc(pe_o, 1)
                elif e[0] == "S":
                    s = e[1]
                    h, t = steps[s]
                    if t == 0:
                        wait_freed(pe, where[("T4", "prep", h, 2)])
                    if s:
                        pe.wait_ge(exp_done, 2 * s)
                    else:
                        pe.wait_ge(sc_masked, NT)
                        pe.wait_ge(rt_read, NT)
                        pe.wait_ge(u_read, 2 * len(UPDATES))
                    for c in range(2):
                        q = qz[h % 2][:, c, t * P:(t + 1) * P] if t < PT else qzp[h % 2][:, c, :]
                        spans = [(0, 512), (512, 768)] if c == 0 else [(0, 256), (256, 768)]
                        if t == PT:
                            spans = [(0, P)]
                        for lo, hi in spans:
                            keys = kT[h % 2][:, lo:hi] if t < PT else kT[h % 2][:, KEYS:KEYS + P]
                            mm = pe.matmul(score[c][:, lo:hi], q, keys, start=True, stop=True, skip_group_check=True)
                    mm.then_inc(pe_scores, 1)
                elif e[0] == "AT":
                    s = e[1]
                    h, t = steps[s]
                    pe.wait_ge(mixed_ready, s + 1)
                    if s:
                        pe.wait_ge(at_read, s)
                    else:
                        pe.wait_ge(o_read, NT)
                    for k in range(6 if t < PT else 1):
                        mm = pe.transpose(B(5 + k // 4)[:, (k % 4) * P:(k % 4 + 1) * P], mixed[:, k * P:(k + 1) * P], ident)
                    mm.then_inc(pe_at, 1)
                elif e[0] == "PV":
                    s = e[1]
                    h, t = steps[s]
                    c0 = P * (h % 4)
                    pe.wait_ge(at_read, s + 1)
                    if s:
                        pe.wait_ge(pv_read, s)
                    else:
                        pe.wait_ge(u_read, 2 * len(UPDATES))
                    if t == 0:
                        wait_freed(pe, where[("mm", f"dv{h // 4}", PT)])
                    if t == PT:
                        mm = pe.matmul(B(7)[:, 0:P], mixedT[s % 2][:, 0:P], dv[:, PT, c0:c0 + P], start=True, stop=True)
                    else:
                        for k in range(6):
                            v = dv[:, k, c0:c0 + P] if k < 4 else ctx_v[:, k - 4, c0:c0 + P]
                            mm = pe.matmul(B(7)[:, 0:P], mixedT[s % 2][:, k * P:(k + 1) * P], v, start=(k == 0), stop=(k == 5))
                    mm.then_inc(pe_pv, 1)

            pe.wait_ge(route_d, 3)
            pe.matmul(B(3)[:, 0:NT * NE], R("before"), e_any.rearrange("p t n -> p (t n)"), start=True, stop=True)
            pe.matmul(B(4)[:, 0:NT * NE], R("ones"), e_any.rearrange("p t n -> p (t n)"), start=True, stop=True).then_inc(pe_rank, 1)
            pe.wait_ge(route_d, 4)
            for x in range(2 * NT):
                mm = pe.matmul(B(5)[:, 0:NPAIR], hot_pos[:, x, :], val_pair[:, x, :], start=(x == 0), stop=(x == 2 * NT - 1))
            mm.then_inc(pe_table, 1)

            def gathered(slot):
                for k in range(KC):
                    mm = pe.transpose(B(k // 4)[:, (k % 4) * P:(k % 4 + 1) * P], xg[:, slot, k * P:(k + 1) * P], ident)
                return mm

            def gate_up(slot, e0, bank_at):
                for k in range(KC):
                    for i in range(2):
                        mm = pe.matmul(B(bank_at)[BLK * i:BLK * (i + 1), :], xgT[slot][:, k, BLK * i:BLK * (i + 1)],
                                       w_gu[e0 + i][:, k, :, :].rearrange("p g f -> p (g f)"), start=(k == 0), stop=(k == KC - 1))
                return mm

            def hidden(slot):
                for k in range(2):
                    mm = pe.transpose(B(4)[:, k * P:(k + 1) * P], act_a[:, slot, k * P:(k + 1) * P], ident)
                return mm

            def down(slot, e0):
                for n in range(2):
                    for k in range(2):
                        for i in range(2):
                            mm = pe.matmul(B(5 + n)[BLK * i:BLK * (i + 1), :], act_aT[slot][:, k, BLK * i:BLK * (i + 1)],
                                           w_dn[e0 + i][:, k, n * N512:(n + 1) * N512], start=(k == 0), stop=(k == 1))
                return mm

            def pair_gathered(p, par, turn):
                pe.wait_ge(ld_xg[par], 16 * turn + 16)
                pe.wait_ge(xt_read, p)
                gathered(par).then_inc(pe_xt, 1)

            def pair(p, par, slot, turn, wturn, first=False, last=False):
                for i in range(2):
                    pe.wait_ge(ld_gu[slot + i], 32 * wturn + 32)
                pe.wait_ge(xt_read, p + 1)
                gate_up(par, slot, 2 + par).then_inc(pe_gu, 1)
                if not last:
                    pair_gathered(p + 1, 1 - par, turn + par)
                pe.wait_ge(gu_act, p + 1)
                hidden(par).then_inc(pe_aT, 1)
                pe.wait_ge(aT_read, p + 1)
                for i in range(2):
                    pe.wait_ge(ld_dn[slot + i], 16 * wturn + 16)
                if not first:
                    pe.wait_ge(y_a, p)
                    pe.wait_ge(y_d, p)
                down(par, slot).then_inc(pe_dn, 1)

            pe.wait_ge(idx_ready, 1)
            pe.wait_ge(ld_xg[0], 16)
            gathered(0).then_inc(pe_xt, 1)
            pair(0, 0, 0, 0, 0, first=True)
            pair(1, 1, 2, 0, 0)
            pair(2, 0, 4, 1, 0)
            with pe.Fori(0, (PAIRS - 4) // 2) as i:
                pair(2 * i + 3, 1, 0, i + 1, i + 1)
                pair(2 * i + 4, 0, 2, i + 2, i + 1)
            pair(PAIRS - 1, 1, 0, PAIRS // 2 - 1, PAIRS // 2 - 1, last=True)
            n_over = pe.value_load(n_ov[0:1, 0:1], min_val=0, max_val=OVER)
            pe.wait_ge(y_a, PAIRS)
            pe.wait_ge(y_d, PAIRS)
            with pe.If(n_over > 0):
                with pe.Fori(0, OVER // 2) as j:
                    with pe.If(n_over > 2 * j):
                        pe.wait_ge(ov_x, 16 * j + 16)
                        gathered(0).then_inc(ov_xt, 1)
                        pe.wait_ge(ov_xr, j + 1)
                        pe.wait_ge(ov_w, 96 * j + 96)
                        gate_up(0, 0, 2).then_inc(ov_gu, 1)
                        pe.wait_ge(ov_act, j + 1)
                        hidden(0).then_inc(ov_aT, 1)
                        pe.wait_ge(ov_ar, j + 1)
                        down(0, 0).then_inc(ov_dn, 1)
                    with pe.Else():
                        pe.nop()

            with pe.Else():
                pe.nop()
        @block.scalar
        def _(act):
            chain = [0]

            def link(ins):
                chain[0] += 1
                ins.then_inc(act_chain, 1)
                act.wait_ge(act_chain, chain[0])

            act.wait_ge(ld_small, 16 * 16)
            act.activation(rows_t[0:16, :], rows[0:16, :], ACT.Tanh, scale=0.5).then_inc(act_set, 1)
            for t in range(NT):
                if t == 0:
                    act.wait_ge(ld_x, 16 * NT)
                else:
                    act.wait_ge(ssq_ready, t)
                act.activation(square_t, xn[:, t, :], ACT.Square, accum_out=ssq[:, t:t + 1]).then_inc(ssq_ready, 1)
            act.wait_ge(dve_set, 3)
            act.activation(dec_e[:], dec_n[:], ACT.Exp, scale=-1.0).then_inc(act_set, 1)
            act.wait_ge(dve_set, 4)
            act.activation(dec_e[:], dec_n[:], ACT.Ln).then_inc(act_set, 1)
            act.wait_ge(dve_set, 5)
            act.wait_ge(ld_const, 32)
            for h in range(8):
                fw = h < 4
                act.activation(decay_e[:, h, :], C("rel_f" if fw else "rel_b"), ACT.Exp, scale=lg[:, h:h + 1])
                act.activation(q_dec[:, h, :], C("pos_f" if fw else "pos_b"), ACT.Exp, scale=lg[:, h:h + 1])
            act.activation(kd[:], dec_n[:], ACT.Exp)
            act.activation(cd[:], lg[:], ACT.Exp, scale=float(P))
            act.activation(lam_s[:], lam_s[:], ACT.Exp).then_inc(act_set, 1)

            def scale_copy(dst, src, s, b=None):
                if b is None:
                    return act.activation(dst, src, ACT.Copy, scale=s)
                return act.activation(dst, src, ACT.Identity, scale=s, bias=b)

            def dense_item(n):
                item = dense[n]
                src = B(n % 2)
                if item[0] == "T4":
                    if freed[n][0] != "A":
                        return
                    _, what, t, half = item
                    act.wait_ge(pe_dense, n + 1)
                    if what == "prep":
                        h, i = t, half
                        if i == 0:
                            if h < 2:
                                act.wait_ge(dve_set, 8)
                            act.copy(qz[h % 2][0:DH, 0, :], src[0:DH, :])
                            ins = act.copy(qz[h % 2][DH:P, 1, :], src[DH:P, :])
                        elif i == 1:
                            ins = act.copy(kT[h % 2][:, 0:512], src)
                        else:
                            act.copy(kT[h % 2][:, 512:KEYS + P], src[:, 0:3 * P])
                            act.copy(qzp[h % 2][0:DH, 0, :], src[0:DH, 3 * P:4 * P])
                            ins = act.copy(qzp[h % 2][DH:P, 1, :], src[DH:P, 3 * P:4 * P])
                    else:
                        s = 1 if t == PT else 0
                        if what == "h":
                            act.wait_ge(dve_set, 7)
                            for k in range(4):
                                kk = 4 * half + k
                                ins = scale_copy(left["h"][0][:, t, kk * P:(kk + 1) * P], src[:, k * P:(k + 1) * P],
                                                 mul1[:, kk, s:s + 1], modc[:, kk, s:s + 1])
                        elif what == "o":
                            for k in range(4):
                                kk = 4 * half + k
                                ins = scale_copy(left["o"][0][:, t, kk * P:(kk + 1) * P], src[:, k * P:(k + 1) * P], cols[:, 16 + kk:17 + kk])
                        elif what == "od":
                            if t == 0:
                                wait_freed(act, where[("mm", "wr1", PT)])
                            ins = scale_copy(left["od"][0][:, t, N512 * half:N512 * (half + 1)], src, cols[:, 24:25])
                        else:
                            ins = scale_copy(left["m"][0][:, t, N512 * half:N512 * (half + 1)], src, 0.5)
                    free(ins, n)
                    return
                _, s, t, hh = item
                kind = s[:2]
                if kind in ("wr", "wd", "wo"):
                    return
                act.wait_ge(pe_dense, n + 1)
                src = src[:, 0:N256]
                if kind == "rg":
                    u = gate_at[item[1:]] - 1
                    if u == 0:
                        act.wait_ge(pe_rt, NT)
                        act.wait_ge(u_keys, len(UPDATES))
                    if u >= 2:
                        act.wait_ge(gate_done, u - 1)
                    act.activation(gate_t[:, u % 2, :], src, ACT.Tanh, scale=0.5).then_inc(tanh_done, 1)
                    return
                if kind in ("gr", "gd"):
                    v = spill_at[item[1:]]
                    if v == 0:
                        act.wait_ge(gate_done, len(gate_at))
                    if v >= 4:
                        act.wait_ge(st_gate[v % 4], 16 * (v // 4))
                    free(act.activation(gate_t[:, v % 4, :], src, ACT.Tanh, scale=0.5), n)
                    return
                if kind == "dv" or kind == "dk":
                    if s[2] == "1" and t == PT:
                        act.wait_ge(st_kv[0], 16 * 2)
                if s == "dq0" and t == 0:
                    act.wait_ge(dve_set, 6)
                dst = {"rq": rq, "rk": rk, "rv": rv, "dq": dq, "dk": dk, "dv": dv}[kind]
                c0 = N256 * hh + (N512 * int(s[2]) if kind == "rv" else 0)
                free(act.copy(dst[:, t, c0:c0 + N256], src), n)

            def high_part(what, t, half):
                wait_freed(act, where[("T4", what, t, half)])
                if what == "o" and t == 0 and half == 0:
                    act.wait_ge(st_fill, 16 * 2)
                c = slice(N512 * half, N512 * (half + 1))
                act.copy(left[what][1][:, t, c], left[what][0][:, t, c]).then_inc(x_rounded, 1)

            for e in plan:
                if e[0] == "dense":
                    dense_item(e[1])
                elif e[0] == "split":
                    high_part(*e[1:])
                elif e[0] == "Q":
                    t = e[1]
                    act.wait_ge(x1_ready, x1_done[t])
                    if t:
                        act.wait_ge(st_sq2, t)
                    act.activation(psf[:, 3 * N512:5 * N512], x1[:, t, :], ACT.Square, accum_out=ssq[:, t:t + 1]).then_inc(st_sq2, 1)
                elif e[0] == "R":
                    t = e[1]
                    act.wait_ge(pe_h2, t + 1)
                    for i in range(2):
                        ins = act.copy(h2T[:, 4 * i:4 * i + 4, t * P:(t + 1) * P], B(5 + i).rearrange("p (k n) -> p k n", k=4))
                    ins.then_inc(h2_read, 1)
                elif e[0] == "cv":
                    i = e[1]
                    act.wait_ge(ld_w[i % 2], 16 * (i // 2 + 1))
                    act.copy(w_hi[i % 2][:], w_raw[i % 2]).then_inc(w_rounded, 1)
                elif e[0] == "RT":
                    i = RET.index(e[1])
                    act.wait_ge(pe_rt, i + 1)
                    if i == 0:
                        act.wait_ge(mod_cols, 3)
                        act.wait_ge(st_mod, 16 * 8)
                    else:
                        act.wait_ge(pe_sc, i)
                        if i > 1:
                            act.wait_ge(q_scaled, i - 1)
                    act.copy(rqT, B(2))
                    act.copy(rkT, B(3)).then_inc(rt_read, 1)
                elif e[0] == "O":
                    i = RET.index(e[1])
                    act.wait_ge(pe_o, i + 1)
                    act.copy(ret[:, e[1], 0:N512], B(5))
                    act.copy(ret[:, e[1], N512:D], B(6)).then_inc(o_read, 1)
                elif e[0] == "S":
                    s = e[1]
                    h, t = steps[s]
                    n = KEYS if t < PT else P
                    act.wait_ge(max_ready, s + 1)
                    if s:
                        act.wait_ge(mixed_ready, s)
                    for c in range(2):
                        act.activation(probs[:, c, 0:n], score[c][:, 0:n], ACT.Exp, bias=neg_mx[:, s % 2, c:c + 1],
                                       scale=DH ** -0.5, accum_out=den[:, s % 2, c:c + 1]).then_inc(exp_done, 1)
                elif e[0] == "AT":
                    s = e[1]
                    act.wait_ge(pe_at, s + 1)
                    if steps[s][1] < PT:
                        act.copy(mixedT[s % 2][:, 0:N512], B(5))
                        act.copy(mixedT[s % 2][:, N512:KEYS], B(6)[:, 0:CTX]).then_inc(at_read, 1)
                    else:
                        act.copy(mixedT[s % 2][:, 0:P], B(5)[:, 0:P]).then_inc(at_read, 1)
                elif e[0] == "PV":
                    s = e[1]
                    h, t = steps[s]
                    act.wait_ge(pe_pv, s + 1)
                    if s == 0:
                        act.wait_ge(pe_o, NT)
                    scale_copy(od[:, t, h * P:(h + 1) * P], B(7)[:, 0:P], rden[:, s % 2, 0:1])
                    act.activation(B(7)[:, P:2 * P], B(7)[:, 0:P], ACT.Square, scale=rden[:, s % 2, 0:1],
                                   accum_out=od_ss[:, t, h:h + 1]).then_inc(pv_read, 1)

            act.wait_ge(route_d, 1)
            act.activation(g_diff, g_diff, ACT.Exp).then_inc(route_a, 1)
            act.wait_ge(route_d, 2)
            act.activation(e_x, e_x, ACT.Exp).then_inc(route_a, 1)

            def pair(p, par):
                act.wait_ge(pe_xt, p + 1)
                for i in range(2):
                    ins = act.copy(xgT[par][:, 4 * i:4 * i + 4, :], B(i).rearrange("p (k n) -> p k n", k=4))
                ins.then_inc(xt_read, 1)

            def pair_gate(p, par):
                act.wait_ge(pe_gu, p + 1)
                act.activation(act_t[:, par, :], B(2 + par)[:, 0:FF], ACT.Tanh, scale=0.5).then_inc(gu_tanh, 1)

            def pair_hidden(p, par):
                act.wait_ge(pe_aT, p + 1)
                act.copy(act_aT[par], B(4)[:, 0:2 * P].rearrange("p (k n) -> p k n", k=2)).then_inc(aT_read, 1)

            def pair_rows(p, par, turn, first=False):
                act.wait_ge(pe_dn, p + 1)
                if not first:
                    act.wait_ge(st_y[par], 16 * turn)
                act.copy(y_out[:, par, 0:N512], B(5)).then_inc(y_a, 1)

            def whole(p, par, turn, first=False, last=False):
                pair_gate(p, par)
                if not last:
                    pair(p + 1, 1 - par)
                pair_hidden(p, par)
                pair_rows(p, par, turn, first=first)

            pair(0, 0)
            whole(0, 0, 0, first=True)
            whole(1, 1, 0, first=True)
            with act.Fori(1, PAIRS // 2 - 1) as i:
                for par in range(2):
                    whole(2 * i + par, par, i)
            h = PAIRS // 2 - 1
            whole(2 * h, 0, h)
            whole(2 * h + 1, 1, h, last=True)
            n_over = act.value_load(n_ov[0:1, 0:1], min_val=0, max_val=OVER)
            act.wait_ge(st_y[0], 16 * PAIRS // 2)
            act.wait_ge(st_y[1], 16 * PAIRS // 2)
            with act.If(n_over > 0):
                with act.Fori(0, OVER // 2) as j:
                    with act.If(n_over > 2 * j):
                        act.wait_ge(ov_xt, j + 1)
                        for i in range(2):
                            ins = act.copy(xgT[0][:, 4 * i:4 * i + 4, :], B(i).rearrange("p (k n) -> p k n", k=4))
                        ins.then_inc(ov_xr, 1)
                        act.wait_ge(ov_gu, j + 1)
                        act.activation(act_t[:, 0, :], B(2)[:, 0:FF], ACT.Tanh, scale=0.5).then_inc(ov_tanh, 1)
                        act.wait_ge(ov_aT, j + 1)
                        act.copy(act_aT[0], B(4)[:, 0:2 * P].rearrange("p (k n) -> p k n", k=2)).then_inc(ov_ar, 1)
                        act.wait_ge(ov_dn, j + 1)
                        act.copy(y_out[:, 0, 0:N512], B(5)).then_inc(ov_ya, 1)
                    with act.Else():
                        act.nop()
            with act.Else():
                act.nop()
            def first_rows(t):
                act.wait_ge(ld_y[t], 32)
                act.activation(y1[:, t, :], y1[:, t, :], ACT.Copy, scale=w_tok[:, 0, t:t + 1]).then_inc(y_scaled, 1)

            first_rows(0)
            for t in range(NT):
                if t + 1 < NT:
                    first_rows(t + 1)
                act.wait_ge(y_used, t + 1)
                act.activation(y1[:, t, :], x1[:, t, :], ACT.Square, accum_out=ssq[:, t:t + 1]).then_inc(fin_sq, 1)

        @block.vector
        def _(dve):
            chain = [0]

            def link(ins):
                chain[0] += 1
                ins.then_inc(dve_chain, 1)
                dve.wait_ge(dve_chain, chain[0])

            n_set = [0]

            def setp(ins):
                n_set[0] += 1
                ins.then_inc(dve_set, 1)
                dve.wait_ge(dve_set, n_set[0])

            dve.memset(ccol, 0.0)
            dve.memset(neg_half[:], -0.5)
            dve.wait_ge(act_set, 1)
            setp(dve.scalar_tensor_tensor(out=rows[0:16, :], in0=rows_t[0:16, :], scalar=1.0, in1=rows[0:16, :],
                                          op0=ALU.add, op1=ALU.mult))
            dve.wait_ge(pe_set, 1)
            link(dve.tensor_copy(cols[:], B(7)[:, 16:41]))
            link(dve.tensor_scalar(cols[:, 16:24], cols[:, 16:24], 0.5, None, ALU.mult))
            link(dve.tensor_scalar(cols[:, 24:25], cols[:, 24:25], 0.8, None, ALU.mult))
            setp(dve.tensor_scalar(ccol[:, :, 0:2], B(7)[:, 0:16].rearrange("p (s k) -> p k s", s=2), 0.5, None, ALU.mult))
            setp(dve.scalar_tensor_tensor(out=dec_n[:], in0=dec[:], scalar=-1.0, in1=dec[:], op0=ALU.mult, op1=ALU.max))
            dve.wait_ge(act_set, 2)
            setp(dve.tensor_scalar(dec_n[:], dec_e[:], 1.0, None, ALU.add))
            link(dve.tensor_scalar(dec[:], dec[:], 0.0, None, ALU.min))
            dve.wait_ge(act_set, 3)
            link(dve.tensor_tensor(lg[:], dec[:], dec_e[:], ALU.subtract))
            dve.wait_ge(ld_const, 32)
            link(dve.tensor_scalar(dec_n[:, 0:4], lg[:, 0:4], C("kpos")[:, 0:1], None, ALU.mult))
            link(dve.tensor_scalar(dec_n[:, 4:8], lg[:, 4:8], C("kpos")[:, 1:2], None, ALU.mult))
            link(dve.tensor_tensor_reduce(lam_in[:, 0, :], lam_in[:, 0, :], lam_in[:, 1, :], 1.0, 0.0, ALU.mult, ALU.add, lam_s[:, 0:1]))
            setp(dve.tensor_tensor_reduce(lam_in[:, 2, :], lam_in[:, 2, :], lam_in[:, 3, :], 1.0, 0.0, ALU.mult, ALU.add, lam_s[:, 1:2]))
            dve.wait_ge(rstd_ready, 1)
            for t in range(NT):
                dve.tensor_scalar(xn[:, t, :], xn[:, t, :], rstd[:, t:t + 1], None, ALU.mult).then_inc(xn_ready, 1)
            dve.wait_ge(act_set, 4)
            link(dve.tensor_tensor(decay_e[:, 0:4, :], decay_e[:, 0:4, :], C("on_f").unsqueeze(1).to_broadcast([P, 4, P]), ALU.mult))
            link(dve.tensor_tensor(decay_e[:, 4:8, :], decay_e[:, 4:8, :], C("on_b").unsqueeze(1).to_broadcast([P, 4, P]), ALU.mult))
            link(dve.tensor_scalar(kd[:], kd[:], RK ** -0.5, None, ALU.mult))
            link(dve.tensor_tensor(neg_lam[:], lam_s[:, 1:2], lam_s[:, 0:1], ALU.subtract))
            link(dve.tensor_scalar(neg_lam[:], neg_lam[:], 0.2, None, ALU.subtract))
            setp(dve.tensor_tensor(ret_mask[:], decay_e[:, 0:4, :], decay_e[:, 4:8, :], ALU.add))

            def ada_rows_out(r):
                dve.wait_ge(pe_ada, (r + 1) * KC)
                if r == 0:
                    dve.wait_ge(ld_small, 16 * 16)
                dve.tensor_tensor(mod_rows[:, r, :], B(7), bias_rows[:, r, :], ALU.add).then_inc(ada_rows, 1)
                dve.wait_ge(pe_modT, r + 1)
                dst = modc[:, 16 * r:16 * r + 16, :].rearrange("p (j m) s -> p m j s", m=4)
                src = B(2).rearrange("p (m j x) -> p m j x", m=4, j=4)[:, :, :, 0:2]
                dve.tensor_copy(dst, src).then_inc(mod_cols, 1)

            ada_rows_out(0)
            dve.wait_ge(mod_cols, 1)
            link(dve.tensor_scalar(mul1[:], modc[:, 8:16, :], 1.0, None, ALU.add))
            setp(dve.tensor_tensor(mul1[:], mul1[:], cols[:, 0:8].unsqueeze(2).to_broadcast([P, KC, 2]), ALU.mult))

            n_rope, n_merged, n_out = [0], [0], [0]

            def dense_item(n):
                item = dense[n]
                src = B(n % 2)
                if item[0] == "T4":
                    if freed[n][0] != "D":
                        return
                    _, what, t, half = item
                    dve.wait_ge(pe_dense, n + 1)
                    s = 1 if t == PT else 0
                    if what in ("h", "o"):
                        for k in range(4):
                            kk = 4 * half + k
                            if what == "h":
                                ins = dve.tensor_scalar(left["h"][0][:, t, kk * P:(kk + 1) * P], src[:, k * P:(k + 1) * P],
                                                        mul1[:, kk, s:s + 1], modc[:, kk, s:s + 1], ALU.mult, ALU.add)
                            else:
                                ins = dve.tensor_scalar(left["o"][0][:, t, kk * P:(kk + 1) * P], src[:, k * P:(k + 1) * P],
                                                        cols[:, 16 + kk:17 + kk], None, ALU.mult)
                    else:
                        if what == "od" and t == 0:
                            wait_freed(dve, where[("mm", "wr1", PT)])
                        ins = dve.tensor_scalar(left[what][0][:, t, N512 * half:N512 * (half + 1)], src,
                                                cols[:, 24:25] if what == "od" else 0.5, None, ALU.mult)
                    free(ins, n)
                    return
                _, s, t, hh = item
                kind = s[:2]
                c0 = N512 * int(s[2]) if len(s) > 2 else 0
                if kind in ("dq", "dk") and t < PT and hh == 1:
                    wait_freed(dve, n)
                    x = (dq if kind == "dq" else dk)[:, t, :].rearrange("p (g a i f) -> p g a i f", g=8, a=2, i=2)
                    cs = [C(k)[:, 32 * t:32 * t + 32].rearrange("p (a f) -> p a f", a=2).unsqueeze(1).to_broadcast([P, 8, 2, 16])
                          for k in ("cos", "sin")]
                    tmp = [rope_t[:, i, :].rearrange("p (g a f) -> p g a f", g=8, a=2) for i in range(4)]
                    if n_rope[0]:
                        dve.wait_ge(rope_done, n_rope[0])
                    n_rope[0] += 1
                    for i in range(4):
                        ins = dve.tensor_tensor(tmp[i], x[:, :, :, i // 2, :], cs[i % 2], ALU.mult)
                    link(ins)
                    dve.tensor_tensor(x[:, :, :, 0, :], tmp[0], tmp[3], ALU.subtract)
                    ins = dve.tensor_tensor(x[:, :, :, 1, :], tmp[1], tmp[2], ALU.add)
                    ins.then_inc(rope_done, 1)
                elif kind == "rg":
                    u = gate_at[item[1:]]
                    c0 += N256 * hh
                    dve.wait_ge(tanh_done, u)
                    if u == 1:
                        dve.wait_ge(o_normed, NT)
                    free(dve.scalar_tensor_tensor(out=gate_p[:, u % 2, :], in0=gate_t[:, (u - 1) % 2, :], scalar=1.0,
                                                  in1=src[:, 0:N256], op0=ALU.add, op1=ALU.mult), n)
                    wait_freed(dve, n)
                    dve.tensor_tensor(ret[:, t, c0:c0 + N256], ret[:, t, c0:c0 + N256], gate_p[:, u % 2, :],
                                      ALU.mult).then_inc(gate_done, 1)
                elif kind == "wr":
                    dve.wait_ge(pe_dense, n + 1)
                    v = wr_items.index(n)
                    c0 += N256 * hh
                    dve.wait_ge(ld_gr[v % 4], 16 * (v // 4 + 1))
                    free(dve.scalar_tensor_tensor(out=merge[:, t, c0:c0 + N256], in0=gate_t[:, v % 4, :], scalar=1.0,
                                                  in1=src[:, 0:N256], op0=ALU.add, op1=ALU.mult), n)
                elif kind == "wd":
                    c0 += N256 * hh
                    dve.wait_ge(pe_dense, n + 1)
                    dve.wait_ge(ld_gd, 16)
                    m = merge_t[:, n % 2, :]
                    if n_merged[0]:
                        dve.wait_ge(merged, n_merged[0])
                    n_merged[0] += 1
                    free(dve.scalar_tensor_tensor(out=m, in0=gd_t[:, t, c0:c0 + N256], scalar=1.0, in1=src[:, 0:N256],
                                                  op0=ALU.add, op1=ALU.mult), n)
                    wait_freed(dve, n)
                    dve.tensor_tensor(merge[:, t, c0:c0 + N256], merge[:, t, c0:c0 + N256], m, ALU.add).then_inc(merged, 1)
                elif kind == "wo":
                    c0 += N256 * hh
                    dve.wait_ge(pe_dense, n + 1)
                    dve.wait_ge(ld_x1, 16 * NT)
                    dve.wait_ge(ld_g1, 32)
                    m = merge_t[:, n % 2, :]
                    if n_out[0]:
                        dve.wait_ge(x1_ready, n_out[0])
                    n_out[0] += 1
                    free(dve.tensor_tensor(m, src[:, 0:N256], g1_rows[:, 1 if t == PT else 0, c0:c0 + N256], ALU.mult), n)
                    wait_freed(dve, n)
                    dve.tensor_tensor(x1[:, t, c0:c0 + N256], x1[:, t, c0:c0 + N256], m, ALU.add).then_inc(x1_ready, 1)

            def low_part(what, t, half):
                dve.wait_ge(x_rounded, split_n[(what, t, half)])
                c = slice(N512 * half, N512 * (half + 1))
                whole, high, low = left[what]
                dve.tensor_tensor(low[:, t, c], whole[:, t, c], high[:, t, c].bitcast(F32), ALU.subtract).then_inc(x_split, 1)

            def router_input(t):
                if t == 0:
                    dve.wait_ge(ld_route, 16 * 6)
                    dve.wait_ge(ld_row2, 16 * 4)
                    for i in range(2):
                        ins = dve.scalar_tensor_tensor(out=scale2[:, i, :], in0=scale2[:, i, :], scalar=1.0, in1=n2_row,
                                                       op0=ALU.add, op1=ALU.mult)
                    link(ins)
                i = 1 if t == PT else 0
                dve.wait_ge(pool2, t + 1)
                if t >= 2:
                    dve.wait_ge(pe_h2, t - 1)
                    dve.wait_ge(st_h2[t % 2], 16 * (t // 2))
                link(dve.scalar_tensor_tensor(out=h2[t % 2], in0=x1[:, t, :], scalar=rstd[:, t:t + 1], in1=scale2[:, i, :],
                                              op0=ALU.mult, op1=ALU.mult))
                dve.tensor_tensor(h2[t % 2], h2[t % 2], shift2[:, i, :], ALU.add).then_inc(h2_ready, 1)

            n_read = 0
            for e in plan:
                if e[0] == "dense":
                    dense_item(e[1])
                elif e[0] == "split":
                    low_part(*e[1:])
                elif e[0] == "N":
                    router_input(e[1])
                elif e[0] == "cv":
                    i = e[1]
                    dve.wait_ge(w_rounded, i + 1)
                    dve.tensor_tensor(w_lo[i % 2][:], w_raw[i % 2], w_hi[i % 2][:].bitcast(F32), ALU.subtract).then_inc(w_split, 1)
                elif e[0] == "ada":
                    if e[2] == KC - 1:
                        ada_rows_out(e[1])
                elif e[0] == "U":
                    _, u, half, b = e
                    dirn, t = UPDATES[u]
                    n_read += 1
                    dve.wait_ge(pe_u, n_read)
                    if n_read == 1:
                        dve.wait_ge(ld_state, 32)
                    if t == PT:
                        i = 0 if dirn == "f" else 1
                        if i == 0 and half == 0:
                            dve.wait_ge(st_mod, 16 * 8)
                        dve.tensor_copy(state_out[:, i, half * N512:(half + 1) * N512], B(b)).then_inc(u_read, 1)
                    else:
                        for i in range(2):
                            h = 2 * half + i
                            old = state_f if dirn == "f" else states_b[:, t, :]
                            new = state_f if dirn == "f" else states_b[:, t - 1, :]
                            dcol = h if dirn == "f" else 4 + h
                            ins = dve.scalar_tensor_tensor(out=new[:, h * RV:(h + 1) * RV], in0=old[:, h * RV:(h + 1) * RV],
                                                           scalar=cd[:, dcol:dcol + 1], in1=B(b)[:, i * RV:(i + 1) * RV],
                                                           op0=ALU.mult, op1=ALU.add)
                        ins.then_inc(u_read, 1)
                        dve.wait_ge(u_read, n_read)
                elif e[0] == "SC":
                    i = RET.index(e[1])
                    dve.wait_ge(pe_sc, i + 1)
                    if i:
                        dve.wait_ge(pe_o, i)
                    dve.tensor_tensor(sm.rearrange("p (h n) -> p h n", h=RH), B(4).rearrange("p (h n) -> p h n", h=RH),
                                      ret_mask[:], ALU.mult).then_inc(sc_masked, 1)
                elif e[0] == "O":
                    t = e[1]
                    i = RET.index(t)
                    dve.wait_ge(o_read, i + 1)
                    if i:
                        dve.wait_ge(o_normed, i)
                    for h in range(RH):
                        ins = dve.bn_stats(bn_s[:, h, :], ret[:, t, h * RV:(h + 1) * RV])
                    link(ins)
                    for h in range(RH):
                        ins = dve.bn_aggr(bn_a[:, h, :], bn_s[:, h, :])
                    link(ins)
                    dve.tensor_scalar(var_e[:], bn_a[:, :, 1], EPS, None, ALU.add).then_inc(o_stats, 1)
                    dve.wait_ge(o_rstd, i + 1)
                    for h in range(RH):
                        ins = dve.tensor_scalar(ret[:, t, h * RV:(h + 1) * RV], ret[:, t, h * RV:(h + 1) * RV],
                                                bn_a[:, h, 0:1], ret_rstd[:, h:h + 1], ALU.subtract, ALU.mult)
                    ins.then_inc(o_normed, 1)
                elif e[0] == "ret_end":
                    dve.wait_ge(pe_o, NT)
                    dve.wait_ge(st_ret, 32)
                    for i in range(2):
                        dve.memset(qz[i][DH:P, 0, :], 0.0)
                        dve.memset(qz[i][0:DH, 1, :], 0.0)
                        dve.memset(qzp[i][DH:P, 0, :], 0.0)
                        ins = dve.memset(qzp[i][0:DH, 1, :], 0.0)
                    setp(ins)
                elif e[0] == "S":
                    s = e[1]
                    h, t = steps[s]
                    n = KEYS if t < PT else P
                    dve.wait_ge(pe_scores, s + 1)
                    dve.tensor_reduce(mx[:, 0:1], score[0][:, 0:n], AXX, ALU.max)
                    link(dve.tensor_reduce(mx[:, 1:2], score[1][:, 0:n], AXX, ALU.max))
                    dve.tensor_scalar(neg_mx[:, s % 2, :], mx[:], -DH ** -0.5, None, ALU.mult).then_inc(max_ready, 1)
                    dve.wait_ge(exp_done, 2 * s + 2)
                    if s >= 2:
                        dve.wait_ge(pv_read, s - 1)
                    link(dve.reciprocal(rden[:, s % 2, :], den[:, s % 2, :]))
                    link(dve.scalar_tensor_tensor(out=coef[:, s % 2:s % 2 + 1], in0=rden[:, s % 2, 1:2], scalar=neg_lam[:],
                                                  in1=den[:, s % 2, 0:1], op0=ALU.mult, op1=ALU.mult))
                    if s:
                        dve.wait_ge(pe_at, s)
                    if t < PT:
                        dve.scalar_tensor_tensor(out=mixed, in0=probs[:, 1, :], scalar=coef[:, s % 2:s % 2 + 1],
                                                 in1=probs[:, 0, :], op0=ALU.mult, op1=ALU.add).then_inc(mixed_ready, 1)
                    else:
                        dve.scalar_tensor_tensor(out=mixed[:, 0:P], in0=probs[:, 1, 0:P], scalar=coef[:, s % 2:s % 2 + 1],
                                                 in1=probs[:, 0, 0:P], op0=ALU.mult, op1=ALU.add).then_inc(mixed_ready, 1)

            def ramp_row(ap, lead=NE):
                return ap.unsqueeze(1).to_broadcast([P, lead, ap.shape[1]])

            def over_last(ap, n):
                return ap.unsqueeze(2).to_broadcast([P, ap.shape[1], n])

            def ramp(name, lead):
                r = R(name)
                return r.unsqueeze(1).to_broadcast([P, lead, r.shape[1]])

            dve.wait_ge(pe_logits, NT)
            link(dve.tensor_tensor(logits, B(2)[:, 0:NT * 36].rearrange("p (t n) -> p t n", t=NT),
                                   rb.unsqueeze(1).to_broadcast([P, NT, 36]), ALU.add))
            lgrp = logits[:, :, 0:GRP]
            for x in pads:
                dve.memset(x[:, 0:16], 0.0)
            link(dve.tensor_reduce(g_max, lgrp, AXX, ALU.max))
            dve.tensor_tensor(g_diff, lgrp, over_last(g_max, GRP), ALU.subtract).then_inc(route_d, 1)

            def first_hit(eq, values, top, idx, onehot, ramp_n):
                n = ramp_n
                rr = R("ramp32")[:, 0:n].unsqueeze(1).to_broadcast([P, NT, n])
                link(dve.tensor_tensor(eq, values, over_last(top, n), ALU.is_equal))
                link(dve.scalar_tensor_tensor(out=eq, in0=eq, scalar=-100.0, in1=rr, op0=ALU.mult, op1=ALU.add))
                link(dve.tensor_reduce(idx, eq, AXX, ALU.min))
                link(dve.tensor_scalar(idx, idx, 100.0, None, ALU.add))
                link(dve.tensor_tensor(onehot, rr, over_last(idx, n), ALU.is_equal))

            first_hit(g_eq, lgrp, g_max, g_idx, g_hot, GRP)
            link(dve.tensor_scalar(g_hot, g_hot, BIG, BIG, ALU.mult, ALU.subtract))
            link(dve.tensor_tensor(e_m.rearrange("p t (g e) -> p t g e", g=GRP), logits[:, :, GRP:36].rearrange("p t (g e) -> p t g e", g=GRP),
                                   g_hot.unsqueeze(3).to_broadcast([P, NT, GRP, EPG]), ALU.add))
            for k in range(2):
                link(dve.tensor_reduce(e_max[:, k, :], e_m, AXX, ALU.max))
                first_hit(e_eq, e_m, e_max[:, k, :], e_idx[:, k, :], hot[:, k, :, :], NE)
                if k == 0:
                    link(dve.scalar_tensor_tensor(out=e_m, in0=hot[:, 0, :, :], scalar=-2 * BIG, in1=e_m, op0=ALU.mult, op1=ALU.add))
            dve.tensor_tensor(e_x, e_max[:, 1, :], e_max[:, 0, :], ALU.subtract).then_inc(route_d, 1)
            dve.tensor_tensor(e_any, hot[:, 0, :, :], hot[:, 1, :, :], ALU.add).then_inc(route_d, 1)
            dve.wait_ge(route_a, 2)
            link(dve.tensor_reduce(g_sum, g_diff, AXX, ALU.add))
            link(dve.tensor_scalar(e_den, e_x, 1.0, None, ALU.add))
            link(dve.tensor_tensor(e_den, e_den, g_sum, ALU.mult))
            link(dve.reciprocal(w_tok[:, 0, :], e_den))
            link(dve.tensor_tensor(w_tok[:, 1, :], w_tok[:, 0, :], e_x, ALU.mult))
            cnt, cnt_next = cnt_a, cnt_b
            dve.wait_ge(pe_rank, 1)
            link(dve.tensor_copy(rank_m.rearrange("p t n -> p (t n)"), B(3)[:, 0:NT * NE]))
            link(dve.tensor_copy(cnt, B(4)[:, 0:NE]))
            for t in range(1, NT):
                dve.tensor_tensor(rank_m[:, t, :], rank_m[:, t, :], cnt, ALU.add)
                link(dve.tensor_tensor(cnt_next, cnt, B(4)[:, t * NE:(t + 1) * NE], ALU.add))
                cnt, cnt_next = cnt_next, cnt
            link(dve.tensor_tensor(cmp9, over_last(cnt, 9), ramp("x64", NE), ALU.is_gt))
            link(dve.tensor_reduce(over, cmp9, AXX, ALU.add))
            for n, (src, dst) in enumerate(((0, 1), (1, 2), (2, 1), (1, 2), (2, 1))):
                link(dve.tensor_tensor(pads[dst][:, 16:16 + NE], pads[src][:, 16:16 + NE],
                                       pads[src][:, 16 - 2 ** n:16 - 2 ** n + NE], ALU.add))
            link(dve.tensor_tensor(over_at, over_end, over, ALU.subtract))

            def pick(dst, table):
                for k in range(2):
                    ins = dve.tensor_tensor(prod[:, k, :, :], hot[:, k, :, :], table, ALU.mult)
                link(ins)
                link(dve.tensor_reduce(dst.rearrange("p (k t) -> p k t", k=2), prod, AXX, ALU.add))

            pick(rk_s, rank_m)
            pick(ob_s, over_at.unsqueeze(1).to_broadcast([P, NT, NE]))
            link(dve.tensor_tensor(cmp_r, over_last(rk_s, 9), ramp("x64", 2 * NT), ALU.is_ge))
            link(dve.tensor_reduce(qq, cmp_r, AXX, ALU.add))
            link(dve.tensor_scalar(has, qq, 1.0, None, ALU.min))
            ei = e_idx.rearrange("p k t -> p (k t)")
            link(dve.tensor_tensor(ob_s, ob_s, qq, ALU.add))
            link(dve.tensor_tensor(ob_s, ob_s, ei, ALU.subtract))
            link(dve.scalar_tensor_tensor(out=ob_s, in0=ob_s, scalar=NE - 1.0, in1=has, op0=ALU.add, op1=ALU.mult))
            link(dve.tensor_tensor(ob_s, ob_s, ei, ALU.add))
            link(dve.tensor_tensor(ob_s, ob_s, qq, ALU.subtract))
            link(dve.scalar_tensor_tensor(out=slot, in0=ob_s, scalar=float(BLK), in1=rk_s, op0=ALU.mult, op1=ALU.add))
            link(dve.tensor_copy(y_idx[:], slot))
            link(dve.tensor_tensor(cmp_p, over_last(slot, NPAIR - 1), ramp("x128", 2 * NT), ALU.is_ge))
            link(dve.tensor_reduce(pair_i, cmp_p, AXX, ALU.add))
            link(dve.scalar_tensor_tensor(out=pos_i, in0=pair_i, scalar=-float(P), in1=slot, op0=ALU.mult, op1=ALU.add))
            link(dve.tensor_tensor(hot_pos[:], over_last(pos_i, P), ramp("ramp128", 2 * NT), ALU.is_equal))
            link(dve.tensor_tensor(own_pair, over_last(pair_i, NPAIR), ramp("ramp26", 2 * NT), ALU.is_equal))
            for k in range(2):
                ins = dve.tensor_tensor(val_pair[:, k * NT:(k + 1) * NT, :], own_pair[:, k * NT:(k + 1) * NT, :],
                                        over_last(R("token"), NPAIR), ALU.mult)
            ins.then_inc(route_d, 1)
            link(dve.tensor_tensor(ov_cmp, ramp_row(over_end, OVER), over_last(R("ramp20"), NE), ALU.is_le))
            link(dve.tensor_reduce(ov_f, ov_cmp, AXX, ALU.add))
            link(dve.tensor_scalar(ov_f, ov_f, NE - 1.0, None, ALU.min))
            link(dve.tensor_copy(ov_exp[:], ov_f))
            link(dve.tensor_copy(n_ov[:], over_end[:, NE - 1:NE]))
            dve.wait_ge(pe_table, 1)
            dve.tensor_copy(row_idx[:], B(5)[:, 0:NPAIR]).then_inc(idx_ready, 1)

            def silu_up(src, par, wait, done):
                ins = dve.scalar_tensor_tensor(out=act_s[:, par, :], in0=act_t[:, par, :], scalar=1.0, in1=src[:, 0:FF],
                                               op0=ALU.add, op1=ALU.mult)
                ins.then_inc(wait[0], 1)
                dve.wait_ge(wait[0], wait[1])
                dve.scalar_tensor_tensor(out=act_a[:, par, :], in0=act_s[:, par, :], scalar=0.5, in1=src[:, FF:2 * FF],
                                         op0=ALU.mult, op1=ALU.mult).then_inc(done, 1)

            def pair_rows(p, par, turn, first=False):
                dve.wait_ge(pe_dn, p + 1)
                if not first:
                    dve.wait_ge(st_y[par], 16 * turn)
                dve.tensor_copy(y_out[:, par, N512:D], B(6)).then_inc(y_d, 1)

            def pair(p, par, turn, first=False):
                dve.wait_ge(gu_tanh, p + 1)
                silu_up(B(2 + par), par, (gu_half, p + 1), gu_act)
                pair_rows(p, par, turn, first=first)

            pair(0, 0, 0, first=True)
            pair(1, 1, 0, first=True)
            with dve.Fori(1, PAIRS // 2) as i:
                for par in range(2):
                    pair(2 * i + par, par, i)
            n_over = dve.value_load(n_ov[0:1, 0:1], min_val=0, max_val=OVER)
            dve.wait_ge(st_y[0], 16 * PAIRS // 2)
            dve.wait_ge(st_y[1], 16 * PAIRS // 2)
            with dve.If(n_over > 0):
                with dve.Fori(0, OVER // 2) as j:
                    with dve.If(n_over > 2 * j):
                        dve.wait_ge(ov_free, j + 1)
                        dve.tensor_copy(idx_now[:], row_idx[:, bass.ds(j + PAIRS, 1)]).then_inc(ov_idx, 1)
                        dve.wait_ge(ov_tanh, j + 1)
                        silu_up(B(2), 0, (ov_half, j + 1), ov_act)
                        dve.wait_ge(ov_dn, j + 1)
                        dve.tensor_copy(y_out[:, 0, N512:D], B(6)).then_inc(ov_yd, 1)
                    with dve.Else():
                        dve.nop()
            with dve.Else():
                dve.nop()
            def last(t):
                dve.wait_ge(fin_rstd, t + 1)
                if t >= 2:
                    dve.wait_ge(st_fin[t % 2], 16 * (t // 2))
                dve.scalar_tensor_tensor(out=fin_t[:, t % 2, :], in0=x1[:, t, :], scalar=rstd[:, t:t + 1], in1=fin_row,
                                         op0=ALU.mult, op1=ALU.mult).then_inc(fin_ready, 1)

            dve.wait_ge(ld_fin, 16 * 3)
            def add(t):
                dve.wait_ge(y_gated, t + 1)
                dve.tensor_tensor(x1[:, t, :], x1[:, t, :], y1[:, t, :], ALU.add).then_inc(y_used, 1)

            for t in range(NT):
                dve.wait_ge(y_scaled, t + 1)
                dve.scalar_tensor_tensor(out=y1[:, t, :], in0=y2[:, t, :], scalar=w_tok[:, 1, t:t + 1], in1=y1[:, t, :],
                                         op0=ALU.mult, op1=ALU.add).then_inc(y_sum, 1)
                if t:
                    add(t - 1)
                if t > 1:
                    last(t - 2)
            add(NT - 1)
            last(NT - 2)
            last(NT - 1)

        @block.gpsimd
        def _(pool):
            chain = [0]

            def link(ins):
                chain[0] += 1
                ins.then_inc(pool_chain, 1)
                pool.wait_ge(pool_chain, chain[0])

            pool.wait_ge(ssq_ready, NT)
            link(pool.tensor_scalar(msq[:], ssq[:], 1.0 / D, EPS, ALU.mult, ALU.add))
            pool.wait_ge(dve_set, 1)
            pool.tensor_tensor(rstd[:], msq[:], neg_half[:, 0:NT], ALU.pow).then_inc(rstd_ready, 1)

            def keys(u):
                dirn, t = UPDATES[u]
                if u == 0:
                    pool.wait_ge(dve_set, 6)
                    pool.wait_ge(mod_cols, 3)
                    pool.wait_ge(st_mod, 16 * 8)
                wait_freed(pool, where[("mm", "rv1", PT)])
                if u >= 2:
                    pool.wait_ge(pe_u, 2 * (u - 1))
                k0 = 0 if dirn == "f" else 4
                pool.tensor_tensor(ks[:, u % 2, :].rearrange("p (h n) -> p h n", h=RH), rk[:, t, :].rearrange("p (h n) -> p h n", h=RH),
                                   kd[:, k0:k0 + 4].unsqueeze(2).to_broadcast([P, RH, P]), ALU.mult).then_inc(u_keys, 1)

            seen = set()
            for e in plan:
                if e[0] == "U" and e[2] == 0:
                    if e[1] == 0:
                        keys(0)
                        keys(1)
                    elif e[1] + 1 < len(UPDATES):
                        keys(e[1] + 1)
                elif e[0] == "RT":
                    t = e[1]
                    i = RET.index(t)
                    if t != PT:
                        pool.wait_ge(rt_read, i + 1)
                        if i > 1:
                            pool.wait_ge(pe_o, i)
                        pool.tensor_tensor(qf, rqT, q_dec[:, 0:4, :].rearrange("p h n -> p (h n)"), ALU.mult)
                        pool.tensor_tensor(qb, rqT, q_dec[:, 4:8, :].rearrange("p h n -> p (h n)"), ALU.mult).then_inc(q_scaled, 1)
                elif e[0] == "O":
                    i = RET.index(e[1])
                    pool.wait_ge(o_stats, i + 1)
                    pool.tensor_tensor(ret_rstd[:], var_e[:], neg_half[:, 0:RH], ALU.pow).then_inc(o_rstd, 1)
                elif e[0] == "H":
                    h = e[1]
                    c = slice(h * P, (h + 1) * P)
                    pool.wait_ge(pv_read, NT * (h + 1))
                    link(pool.tensor_scalar(od_ss[:, :, h], od_ss[:, :, h], 1.0 / P, EPS, ALU.mult, ALU.add))
                    link(pool.tensor_tensor(od_rstd[:, :, h], od_ss[:, :, h], neg_half[:, 0:NT], ALU.pow))
                    pool.tensor_tensor(od[:, :, c], od[:, :, c], od_rstd[:, :, h].unsqueeze(2).to_broadcast([P, NT, P]),
                                       ALU.mult).then_inc(od_scaled, 1)

            def inverse_root(t, done):
                link(pool.tensor_scalar(msq[:, t:t + 1], ssq[:, t:t + 1], 1.0 / D, EPS, ALU.mult, ALU.add))
                pool.tensor_tensor(rstd[:, t:t + 1], msq[:, t:t + 1], neg_half[:, 0:1], ALU.pow).then_inc(done, 1)

            for t in range(NT):
                pool.wait_ge(st_sq2, t + 1)
                inverse_root(t, pool2)
            pool.wait_ge(idx_ready, 1)
            pool.wait_ge(st_h2[0], 16 * 3)
            pool.wait_ge(st_h2[1], 16 * 2)
            for p in range(PAIRS):
                if p >= 2:
                    pool.wait_ge(pe_xt, p - 1)
                pool.indirect_dma_start(xg[:, p % 2, :], None, h2_dram, bass.IndirectOffsetOnAxis(ap=row_idx[:, p:p + 1], axis=0)).then_inc(ld_xg[p % 2], 16)
            pool.sem_inc(ov_free, 1)
            pool.wait_ge(pe_xt, PAIRS)
            n_over = pool.value_load(n_ov[0:1, 0:1], min_val=0, max_val=OVER)
            with pool.If(n_over > 0):
                with pool.Fori(0, OVER // 2) as j:
                    with pool.If(n_over > 2 * j):
                        pool.wait_ge(ov_idx, j + 1)
                        pool.sem_inc(ov_take, 1)
                        pool.indirect_dma_start(xg[:, 0, :], None, h2_dram, bass.IndirectOffsetOnAxis(ap=idx_now[:], axis=0)).then_inc(ov_x, 16)
                    with pool.Else():
                        pool.nop()
            with pool.Else():
                pool.nop()
            pool.wait_ge(ov_over, 1)
            for t in range(NT):
                for k, buf in enumerate((y1, y2)):
                    pool.indirect_dma_start(buf[:, t, :], None, y_dram,
                                            bass.IndirectOffsetOnAxis(ap=y_idx[:, k * NT + t:k * NT + t + 1], axis=0)).then_inc(ld_y[t], 16)
            pool.wait_ge(ld_fin, 16 * 3)
            for t in range(NT):
                pool.wait_ge(y_sum, t + 1)
                pool.tensor_tensor(y1[:, t, :], y1[:, t, :], g2_rows[:, 1 if t == PT else 0, :], ALU.mult).then_inc(y_gated, 1)
                if t:
                    pool.wait_ge(fin_sq, t)
                    inverse_root(t - 1, fin_rstd)
            pool.wait_ge(fin_sq, NT)
            inverse_root(NT - 1, fin_rstd)


_INS = ["x_prompt", "x_sample", "cache_diff_k", "cache_diff_v", "state_ret_fwd", "state_ret_bwd", "c", "c_ctx", "w_ada",
        "b_ada", "norm1_g", "norm2_g", "w_in", "ret_decay_fwd", "ret_decay_bwd", "ret_norm_g", "diff_lambda_q1",
        "diff_lambda_k1", "diff_lambda_q2", "diff_lambda_k2", "diff_subln_g", "w_ret_o", "w_diff_o", "w_o",
        "router_group_w", "router_group_b", "router_expert_w", "router_expert_b", "moe_w_gate", "moe_w_up",
        "moe_w_down", "final_norm_g"]
_OUTS = [("out_p", (1, 128, D)), ("out_s", (1, 512, D)), ("out_k", (1, 1, 128, AH, 2, DH)), ("out_v", (1, 1, 128, AH, 2 * DH)),
         ("out_ret_f", (1, 1, RH, RK, RV)), ("out_ret_b", (1, 1, RH, RK, RV))]


def kernel(**inputs):
    import concourse.bacc as bacc
    from concourse.bass_utils import run_bass_kernel_spmd

    nc = bacc.Bacc("TRN2", target_bir_lowering=False, num_devices=1)
    main, coff, route, roff = host_constants()
    arrays = {f"in_{n}": np.ascontiguousarray(inputs[n]) for n in _INS}
    arrays["in_const"], arrays["in_route"] = main, route
    a = {k[3:]: nc.dram_tensor(k, v.shape, F32, kind="ExternalInput").ap() for k, v in arrays.items()}
    o = {n: nc.dram_tensor(n, shape, F32, kind="ExternalOutput").ap() for n, shape in _OUTS}
    build(nc, a, o, coff, roff, main.shape[1], route.shape[1])
    r = run_bass_kernel_spmd(nc, [arrays], core_ids=[0])
    return tuple(r.results[0][n] for n, _ in _OUTS)
```
